# Optimizing a Trainium2 kernel written in Bass

```python
import math
import jax
import jax.numpy as jnp
from jax import lax
import numpy as np

D_MODEL = 2048
BATCH = 1
SEQ = 128
DEPTH = 1
DEC_BATCH = 1
DEC_SEQ = 256
PAST_LEN = 128

GRID_W = 64
N_HEADS = 16
N_KV_HEADS = 4
HEAD_DIM = D_MODEL // N_HEADS
Q_WIDTH = N_HEADS * HEAD_DIM
KV_WIDTH = N_KV_HEADS * HEAD_DIM
HY_WIDTH = D_MODEL // 2
HY_SHORT_K = 3
HY_EMB_DIM = 33
HY_FILTER_HIDDEN = 64
HY_FAST_DECAY = 0.3
HY_SLOW_DECAY = 1.5
HY_DECAY_TARGET = 1e-2
N_BRANCH = 2
IN_WIDTH = Q_WIDTH + 2 * KV_WIDTH + 3 * HY_WIDTH + N_BRANCH * D_MODEL
N_EXPERTS = 16
EXPERT_FF = D_MODEL // 2
CAPACITY_FACTOR = 2
Q_BLOCK = 128
ROPE_THETA = 10000.0
NORM_EPS = 1e-6

kernel_name = 'hybrid_diffusion_attn_hyena_ec_step'

def rms_norm(x, g):
    xf = x.astype(jnp.float32)
    y = xf * lax.rsqrt(jnp.mean(xf * xf, axis=-1, keepdims=True) + NORM_EPS)
    return (y * g.astype(jnp.float32)).astype(x.dtype)

def modulate(x, shift, scale):
    return x * (1.0 + scale) + shift

def ada_modulation(cond, w_ada, b_ada):
    mod = jax.nn.silu(cond) @ w_ada + b_ada
    return jnp.split(mod[:, None, :], 6, axis=-1)

def axial_rope(x):
    L = x.shape[1]
    n_rows = L // GRID_W
    rows = jnp.repeat(jnp.arange(n_rows, dtype=jnp.float32), GRID_W)
    cols = jnp.tile(jnp.arange(GRID_W, dtype=jnp.float32), n_rows)
    half = HEAD_DIM // 2
    inv_freq = ROPE_THETA ** (-jnp.arange(0, half, 2, dtype=jnp.float32) / half)
    xf = x.astype(jnp.float32)

    def rot(xa, pos):
        ang = pos[:, None] * inv_freq[None, :]
        cos = jnp.cos(ang)[None, :, None, :]
        sin = jnp.sin(ang)[None, :, None, :]
        x1, x2 = jnp.split(xa, 2, axis=-1)
        return jnp.concatenate([x1 * cos - x2 * sin, x2 * cos + x1 * sin], axis=-1)

    out = jnp.concatenate([rot(xf[..., :half], rows), rot(xf[..., half:], cols)], axis=-1)
    return out.astype(x.dtype)

def blocked_attention(q, k, v):
    B, L, H, d = q.shape
    kv = k.shape[2]
    g = H // kv
    nb = L // Q_BLOCK
    qb = q.reshape(B, nb, Q_BLOCK, kv, g, d).transpose(1, 0, 2, 3, 4, 5)
    scale = d ** -0.5

    def one_block(qblk):
        s = jnp.einsum('bqkgd,bskd->bkgqs', qblk, k, preferred_element_type=jnp.float32) * scale
        p = jax.nn.softmax(s, axis=-1).astype(v.dtype)
        return jnp.einsum('bkgqs,bskd->bqkgd', p, v)

    o = lax.map(one_block, qb)
    return o.transpose(1, 0, 2, 3, 4, 5).reshape(B, L, H * d)

def centred_short_conv(u, w, b):
    L = u.shape[1]
    pad = HY_SHORT_K // 2
    up = jnp.pad(u, ((0, 0), (pad, pad), (0, 0)))
    y = b
    for i in range(HY_SHORT_K):
        y = y + up[:, i:i + L] * w[i]
    return y

def hyena_filter(L, f1_w, f1_b, sin_freq, f2_w, f2_b, f3_w):
    f32 = jnp.float32
    t = jnp.linspace(0.0, 1.0, L, dtype=f32)
    bands = (HY_EMB_DIM - 1) // 2
    w = 2.0 * math.pi * jnp.arange(L, dtype=f32) / L
    f = jnp.linspace(1e-4, bands - 1, bands, dtype=f32)
    ang = w[:, None] * f[None, :]
    z = jnp.concatenate([t[:, None], jnp.cos(ang), -jnp.sin(ang)], axis=-1)
    freq = sin_freq.astype(f32)
    h = jnp.sin(freq * (z @ f1_w.astype(f32) + f1_b.astype(f32)))
    h = jnp.sin(freq * (h @ f2_w.astype(f32) + f2_b.astype(f32)))
    h = h @ f3_w.astype(f32)
    max_decay = math.log(HY_DECAY_TARGET) / HY_FAST_DECAY
    min_decay = math.log(HY_DECAY_TARGET) / HY_SLOW_DECAY
    deltas = jnp.abs(jnp.linspace(min_decay, max_decay, HY_WIDTH, dtype=f32))
    decay = jnp.exp(-t[:, None] * deltas[None, :])
    h_fwd = h[:, :HY_WIDTH] * decay
    h_bwd = h[:, HY_WIDTH:] * decay
    return jnp.concatenate([h_fwd, jnp.zeros((1, HY_WIDTH), f32), h_bwd[1:][::-1]], axis=0)

def long_conv(u, h2, skip):
    L = u.shape[1]
    uf = jnp.fft.rfft(u.astype(jnp.float32), n=2 * L, axis=1)
    hf = jnp.fft.rfft(h2, n=2 * L, axis=0)
    y = jnp.fft.irfft(uf * hf[None], n=2 * L, axis=1)[:, :L]
    return (y + u.astype(jnp.float32) * skip.astype(jnp.float32)).astype(u.dtype)

def parallel_mixer(h, p, ctx_k, ctx_v):
    B, L, _ = h.shape
    proj = h @ p['w_in']
    o1 = Q_WIDTH
    o2 = o1 + KV_WIDTH
    o3 = o2 + KV_WIDTH
    o4 = o3 + 3 * HY_WIDTH
    q = rms_norm(proj[..., :o1].reshape(B, L, N_HEADS, HEAD_DIM), p['q_norm_g'])
    k = rms_norm(proj[..., o1:o2].reshape(B, L, N_KV_HEADS, HEAD_DIM), p['k_norm_g'])
    v = proj[..., o2:o3].reshape(B, L, N_KV_HEADS, HEAD_DIM)
    hy = proj[..., o3:o4]
    gate_attn, gate_hy = jnp.split(proj[..., o4:], N_BRANCH, axis=-1)
    if ctx_k is None:
        k_all, v_all = k, v
    else:
        q = axial_rope(q)
        k_all = jnp.concatenate([axial_rope(k), ctx_k.astype(k.dtype)], axis=1)
        v_all = jnp.concatenate([v, ctx_v.astype(v.dtype)], axis=1)
    y_attn = blocked_attention(q, k_all, v_all) @ p['w_attn_o']
    hy = centred_short_conv(hy, p['hy_conv_w'], p['hy_conv_b'])
    x0, x1, vh = jnp.split(hy, 3, axis=-1)
    filt = hyena_filter(L, p['hy_f1_w'], p['hy_f1_b'], p['hy_sin_freq'],
                        p['hy_f2_w'], p['hy_f2_b'], p['hy_f3_w'])
    z = long_conv(vh * x1, filt, p['hy_skip'])
    y_hy = (x0 * z) @ p['w_hy_o']
    merged = jax.nn.sigmoid(gate_attn) * y_attn + jax.nn.sigmoid(gate_hy) * y_hy
    return merged @ p['w_out'], k, v

def expert_choice_ffn(h, p):
    B, L, D = h.shape
    n = B * L
    cap = CAPACITY_FACTOR * n // N_EXPERTS
    xs = h.reshape(n, D)
    aff = jax.nn.softmax((xs @ p['w_router']).astype(jnp.float32), axis=-1)
    g, idx = lax.top_k(aff.T, cap)
    xe = xs[idx]
    a = jnp.einsum('ecd,edf->ecf', xe, p['w_exp_gate'])
    u = jnp.einsum('ecd,edf->ecf', xe, p['w_exp_up'])
    ye = jnp.einsum('ecf,efd->ecd', jax.nn.silu(a) * u, p['w_exp_down']) * g[..., None].astype(h.dtype)
    out = jnp.zeros((n, D), h.dtype).at[idx.reshape(-1)].add(ye.reshape(-1, D))
    return out.reshape(B, L, D)

def trunk_layer(x, mods, p, ctx_k, ctx_v):
    shift1, scale1, gate1, shift2, scale2, gate2 = mods
    h = modulate(rms_norm(x, p['g_pre_mix']), shift1, scale1)
    m, k, v = parallel_mixer(h, p, ctx_k, ctx_v)
    x = x + gate1 * rms_norm(m, p['g_post_mix'])
    h = modulate(rms_norm(x, p['g_pre_ffn']), shift2, scale2)
    f = expert_choice_ffn(h, p)
    x = x + gate2 * rms_norm(f, p['g_post_ffn'])
    return x, k, v

def setup_inputs(seed: int = 0) -> dict:
    key = jax.random.key(seed)
    ks = jax.random.split(key, 32)
    f32 = jnp.float32

    def nrm(k, shape, scale):
        return jax.random.normal(k, shape, f32) * scale

    def gain(k, shape):
        return 1.0 + 0.05 * jax.random.normal(k, shape, f32)

    D = D_MODEL
    H = HY_FILTER_HIDDEN
    return {
        'x_prompt': nrm(ks[0], (BATCH, SEQ, D), 1.0),
        'x_sample': nrm(ks[1], (DEC_BATCH, DEC_SEQ, D), 1.0),
        'cache_k_ctx': nrm(ks[2], (DEC_BATCH, DEPTH, PAST_LEN, N_KV_HEADS, HEAD_DIM), 1.0),
        'cache_v_ctx': nrm(ks[3], (DEC_BATCH, DEPTH, PAST_LEN, N_KV_HEADS, HEAD_DIM), 1.0),
        'c': nrm(ks[4], (DEC_BATCH, D), 1.0),
        'c_ctx': nrm(ks[5], (D,), 1.0),
        'w_ada': nrm(ks[6], (DEPTH, D, 6 * D), 0.2 * D ** -0.5),
        'b_ada': nrm(ks[7], (DEPTH, 6 * D), 0.02),
        'g_pre_mix': gain(ks[8], (DEPTH, D)),
        'g_post_mix': gain(ks[9], (DEPTH, D)),
        'g_pre_ffn': gain(ks[10], (DEPTH, D)),
        'g_post_ffn': gain(ks[11], (DEPTH, D)),
        'w_in': nrm(ks[12], (DEPTH, D, IN_WIDTH), D ** -0.5),
        'q_norm_g': gain(ks[13], (DEPTH, HEAD_DIM)),
        'k_norm_g': gain(ks[14], (DEPTH, HEAD_DIM)),
        'w_attn_o': nrm(ks[15], (DEPTH, Q_WIDTH, D), Q_WIDTH ** -0.5),
        'hy_conv_w': nrm(ks[16], (DEPTH, HY_SHORT_K, 3 * HY_WIDTH), HY_SHORT_K ** -0.5),
        'hy_conv_b': nrm(ks[17], (DEPTH, 3 * HY_WIDTH), 0.02),
        'hy_f1_w': nrm(ks[18], (DEPTH, HY_EMB_DIM, H), HY_EMB_DIM ** -0.5),
        'hy_f1_b': nrm(ks[19], (DEPTH, H), 0.02),
        'hy_sin_freq': gain(ks[20], (DEPTH, H)),
        'hy_f2_w': nrm(ks[21], (DEPTH, H, H), H ** -0.5),
        'hy_f2_b': nrm(ks[22], (DEPTH, H), 0.02),
        'hy_f3_w': nrm(ks[23], (DEPTH, H, 2 * HY_WIDTH), 0.02 * H ** -0.5),
        'hy_skip': nrm(ks[24], (DEPTH, HY_WIDTH), 0.5),
        'w_hy_o': nrm(ks[25], (DEPTH, HY_WIDTH, D), HY_WIDTH ** -0.5),
        'w_out': nrm(ks[26], (DEPTH, D, D), D ** -0.5),
        'w_router': nrm(ks[27], (DEPTH, D, N_EXPERTS), D ** -0.5),
        'w_exp_gate': nrm(ks[28], (DEPTH, N_EXPERTS, D, EXPERT_FF), D ** -0.5),
        'w_exp_up': nrm(ks[29], (DEPTH, N_EXPERTS, D, EXPERT_FF), D ** -0.5),
        'w_exp_down': nrm(ks[30], (DEPTH, N_EXPERTS, EXPERT_FF, D), EXPERT_FF ** -0.5),
    }

def reference(x_prompt, x_sample, cache_k_ctx, cache_v_ctx, c, c_ctx, w_ada, b_ada,
              g_pre_mix, g_post_mix, g_pre_ffn, g_post_ffn, w_in, q_norm_g, k_norm_g,
              w_attn_o, hy_conv_w, hy_conv_b, hy_f1_w, hy_f1_b, hy_sin_freq, hy_f2_w,
              hy_f2_b, hy_f3_w, hy_skip, w_hy_o, w_out, w_router, w_exp_gate, w_exp_up,
              w_exp_down):
    x = x_prompt
    y = x_sample
    new_k = []
    new_v = []
    for l in range(DEPTH):
        p = {
            'g_pre_mix': g_pre_mix[l], 'g_post_mix': g_post_mix[l],
            'g_pre_ffn': g_pre_ffn[l], 'g_post_ffn': g_post_ffn[l],
            'w_in': w_in[l], 'q_norm_g': q_norm_g[l], 'k_norm_g': k_norm_g[l],
            'w_attn_o': w_attn_o[l], 'hy_conv_w': hy_conv_w[l], 'hy_conv_b': hy_conv_b[l],
            'hy_f1_w': hy_f1_w[l], 'hy_f1_b': hy_f1_b[l], 'hy_sin_freq': hy_sin_freq[l],
            'hy_f2_w': hy_f2_w[l], 'hy_f2_b': hy_f2_b[l], 'hy_f3_w': hy_f3_w[l],
            'hy_skip': hy_skip[l], 'w_hy_o': w_hy_o[l], 'w_out': w_out[l],
            'w_router': w_router[l], 'w_exp_gate': w_exp_gate[l],
            'w_exp_up': w_exp_up[l], 'w_exp_down': w_exp_down[l],
        }
        mods_ctx = ada_modulation(c_ctx[None, :], w_ada[l], b_ada[l])
        x, k_ctx, v_ctx = trunk_layer(x, mods_ctx, p, None, None)
        new_k.append(k_ctx)
        new_v.append(v_ctx)
        mods_lat = ada_modulation(c, w_ada[l], b_ada[l])
        y, _, _ = trunk_layer(y, mods_lat, p, cache_k_ctx[:, l], cache_v_ctx[:, l])
    state_k_ctx = jnp.stack(new_k, axis=1)
    state_v_ctx = jnp.stack(new_v, axis=1)
    return (x, y, state_k_ctx, state_v_ctx)


_drawn_inputs = setup_inputs


def setup_inputs(seed=0):
    import zlib

    import numpy as np

    out = dict(_drawn_inputs(seed))
    spreads = {}
    factors = {'cache_k_ctx': 4.871,
     'cache_v_ctx': 3.754,
     'g_post_mix': 6.65,
     'g_post_ffn': 8.0,
     'q_norm_g': 8.0,
     'hy_conv_b': 8.0,
     'hy_f1_w': 3.262,
     'hy_f1_b': 8.0,
     'hy_sin_freq': 8.0,
     'hy_f2_w': 2.798,
     'hy_f2_b': 8.0,
     'hy_f3_w': 3.013}
    for name, (base, spread) in spreads.items():
        noise = np.random.default_rng([zlib.crc32(name.encode()), seed]).standard_normal(out[name].shape)
        drawn = base * np.exp(spread * noise) if base else spread * noise
        out[name] = jnp.asarray(drawn.astype(out[name].dtype))
    for name, factor in factors.items():
        out[name] = (out[name] * factor).astype(out[name].dtype)
    return out
```

```python
from contextlib import ExitStack
import math

import numpy as np

import concourse.bass as bass
from concourse import mybir

F32 = mybir.dt.float32
ALU = mybir.AluOpType
ACT = mybir.ActivationFunctionType
AX_X = mybir.AxisListType.X
ds = bass.ds

P = 128
D = 2048
KT = D // P
NC_ = 512
HK = 8
TC, TL = 128, 256
T = TC + TL
MT = T // P
SEG = ((0, TC), (TC, T))
NH, NKV, HD = 16, 4, 128
GRP = NH // NKV
KVW = NKV * HD
HYW = D // 2
HYT = HYW // P
PAST = 128
NE = 16
FF = D // 2
CAPC, CAPL = 2 * TC // NE, 2 * TL // NE
SLOTS = CAPC + CAPL
EPS = 1e-6
SCALE = HD ** -0.5
HF = 64
HE = 33
MAGIC = 1.5 * 2.0 ** 23
TWO_PI = 2.0 * math.pi
PI_A = 6.28125
PI_B = float(np.float32(np.round((TWO_PI - PI_A) * 2 ** 20) / 2 ** 20))
PI_C = float(np.float32(TWO_PI - PI_A - PI_B))
PI_IN = 3.1415925

ADA_A = 8
SHIFT1, SCALE1, GATE1, SHIFT2, SCALE2, GATE2 = range(6)

C_COND, C_BADA, C_GPRE1, C_GPOST1, C_GPRE2, C_GPOST2, C_CW, C_CB, C_SKIP = 0, 32, 128, 144, 160, 176, 192, 264, 288
N_COLS = 296
T_ID, T_SEL2, T_SEL16, T_SLOT = 0, 128, 130, 146
N_TABS = 178


def build(nc, x_prompt, x_sample, cache_k, cache_v, cols, w_ada, w_in, qk_g, w_attn_o, f1_w, f_vec, f2_w,
          f3_w, w_hy_o, w_out, w_router, w_gate, w_up, w_down, tabs, dft, zfeat, decay, rope,
          y_prompt, y_sample, state_k, state_v):
    ctx = ExitStack()
    with ctx:
        def sb(name, n):
            return ctx.enter_context(nc.sbuf_tensor(name, [P, n], F32))

        def sem(name):
            return ctx.enter_context(nc.semaphore(name))

        def view(t, off, *dims):
            n = int(np.prod(dims))
            v = t[:, off:off + n]
            if len(dims) == 1:
                return v
            names = "abcd"[:len(dims)]
            return v.rearrange(f"p ({' '.join(names)}) -> p {' '.join(names)}",
                               **{k: d for k, d in zip(names[1:], dims[1:])})

        ring_t = sb("ring", 4 * HK * NC_)
        RA, RB, RC = sb("RA", MT * D), sb("RB", MT * D), sb("RC", MT * D)
        RE, RF, RG = sb("RE", 2 * MT * D), sb("RF", 3072), sb("RG", 2048)
        KC = sb("KC", N_COLS + N_TABS)
        MODS = sb("MODS", 192 + 64 + 64)
        SM = sb("SM", 136)

        ring = view(ring_t, 0, 4, HK, NC_)
        col = KC[:, 0:N_COLS]
        ident = KC[:, N_COLS + T_ID:N_COLS + T_ID + P]
        sel2 = KC[:, N_COLS + T_SEL2:N_COLS + T_SEL2 + 2]
        sel16 = KC[:, N_COLS + T_SEL16:N_COLS + T_SEL16 + 16]
        slot_no = KC[:, N_COLS + T_SLOT:N_COLS + T_SLOT + 32]
        mod = view(MODS, 0, 96, 2)
        amp = view(MODS, 192, 2, KT, 2)
        gout = view(MODS, 256, 2, KT, 2)

        spec = view(RA, 0, 3, 2, HYW)
        rope_t = view(RA, 0, 2, 2, HD)
        rot = view(RA, 512, 2, 2, 2, HD)
        gain_b = view(RA, 1536, 2, HD)
        t_a, t_b = view(RA, 1792, NC_), view(RA, 2304, NC_)
        q_st = view(RA, 0, MT, GRP, HD)
        k_st = view(RA, 1536, 4, HD)
        v_st = view(RA, 2048, 4, HD)
        qT = view(RA, 2560, GRP, T)
        kT = view(RA, 4096, NC_)
        res = view(RA, 0, MT, D)
        hT = view(RB, 0, KT, T)
        scat = view(RB, 0, NE, T)
        xn = view(RC, 0, MT, D)
        Z = view(RC, 0, 3, 2, NC_)
        dft_t = view(RC, 3072, 2560)
        fwd_l, fwd_c = view(RC, 3072, 2, 2, TL), view(RC, 4096, 2, TC)
        inv_l, inv_c = view(RC, 4352, 2, 2, TL), view(RC, 5376, 2, TC)
        oT = view(RC, 0, NH, T)
        mix = view(RC, 0, MT, D)
        facc = view(RC, 0, MT, D)
        hN = view(RE, 0, MT, D)
        dec = view(RE, 6144, MT, HYW)
        f3 = view(RE, 9216, D)
        zf = view(RE, 11264, T)
        f1 = view(RE, 11648, HF)
        f2 = view(RE, 11712, HF)
        fv = view(RE, 11776, 3)
        hyT = view(RE, 0, 3 * HYT, T)
        uN = view(RE, 9216, MT, HYW)
        qkN = view(RE, 0, MT, D + KVW)
        vN = view(RE, 7680, 4, KVW)
        kcN = view(RE, 9728, KVW)
        prob = view(RE, 10240, 2, 2 * 384 + TC)
        sg = view(RE, 0, 2 * KT, T)
        xeT = view(RE, 0, KT, NE, SLOTS)
        sq_scr = view(RF, 0, D)
        yhT = view(RF, 0, HYT, T)
        selG = view(RF, 0, NE, P)
        selL = view(RF, 2048, 2, NE, CAPL)
        x_cur = view(RF, 0, KT, SLOTS)
        s_cur = view(RF, 768, T)
        hTe = view(RF, 1152, HK, SLOTS)
        rowbuf = view(RG, 0, NC_)
        condS = view(RG, 512, KT, 32)
        arg, rnd = view(RE, 11792, T), view(RF, 2048, T)
        tmp = view(RG, 1024, NC_)
        probT = view(RG, 1024, 896)
        wr = view(RG, 0, KT, 32)
        ones = view(RG, 512, P)
        diag = view(RG, 1024, 2, NC_)
        lgr = view(RG, 512, T)
        selC = view(RG, 512, NE, CAPC)
        aT, wk, cum = view(RG, 896, T), view(RG, 1280, T), view(RG, 1664, T)
        act_s, h_s = view(RG, 0, NC_), view(RG, 512, NC_)
        ye = view(RG, 1024, 2, NC_)

        ss = view(SM, 0, 12)
        neghalf = view(SM, 124, 12)
        rstd = view(SM, 24, 12)
        rstd3 = view(SM, 24, MT, 4)
        mx = view(SM, 36, 2, 3)
        nb = view(SM, 42, 2, 3)
        rs = view(SM, 48, 2, 3)
        ri = view(SM, 54, 2, 3)
        aff = view(SM, 60, MT, NE)
        vsel = view(SM, 0, MT, NE)
        smx = view(SM, 108, MT)
        m8 = view(SM, 112, 8)

        PS = ctx.enter_context(nc.psum_tensor("PS", [P, 8, 512], F32))

        def bank(b, n=512, off=0, p0=0, p1=P):
            return PS[p0:p1, b, off:off + n]

        landed = [sem(f"landed{j}") for j in range(4)]
        blocks_used = sem("blocks_used")
        small_in, x_in, filt_in, dft_in, qk_in, cache_in, xres_in, wr_in = (
            sem(n) for n in ("small_in", "x_in", "filt_in", "dft_in", "qk_in", "cache_in", "xres_in", "wr_in"))
        out_done = sem("out_done")
        cond_ready, rows_copied, cols_done = sem("cond_ready"), sem("rows_copied"), sem("cols_done")
        sumsq1, ms1, rstd1, xn1 = sem("sumsq1"), sem("ms1"), sem("rstd1"), sem("xn1")
        tr1, tr1_copied = sem("tr1"), sem("tr1_copied")
        f_mm, f_arg, f_sin, f_taps, f_tapmm = (sem(n) for n in ("f_mm", "f_arg", "f_sin", "f_taps", "f_tapmm"))
        f_sumdiff, f_dft, f_spec_a, f_spec_v = (sem(n) for n in ("f_sumdiff", "f_dft", "f_spec_a", "f_spec_v"))
        mod1_read, conv_free, conv_mid = sem("mod1_read"), sem("conv_free"), sem("conv_mid")
        u_ready, u_tr, u_cp, u_dft, z_ready, z_inv, yh_done = (
            sem(n) for n in ("u_ready", "u_tr", "u_cp", "u_dft", "z_ready", "z_inv", "yh_done"))
        qkv_raw, q_ms, q_rstd, qk_done, v_done, rope_done = (
            sem(n) for n in ("qkv_raw", "q_ms", "q_rstd", "qk_done", "v_done", "rope_done"))
        staged, at_trq, at_qT, at_kT, at_s, at_max, at_exp, at_norm, at_trp, at_pa, at_pb, at_o, at_oc = (
            sem(n) for n in ("staged", "at_trq", "at_qT", "at_kT", "at_s", "at_max", "at_exp", "at_norm",
                             "at_trp", "at_pa", "at_pb", "at_o", "at_oc"))
        mod2_read, gate_sig, ao_done, ho_done, mod3_read = (
            sem(n) for n in ("mod2_read", "gate_sig", "ao_done", "ho_done", "mod3_read"))
        wo_cp, ms2, rstd2, diag_ready, g_bc, g_used = (
            sem(n) for n in ("wo_cp", "ms2", "rstd2", "diag_ready", "g_bc", "g_used"))
        res_ready, sumsq3, ms3, rstd3s, xn2, tr2, tr2_v, tr2_a = (
            sem(n) for n in ("res_ready", "sumsq3", "ms3", "rstd3s", "xn2", "tr2", "tr2_v", "tr2_a"))
        wr_zero, lg_mm, lg_cp, lg_nat, lg_sub, lg_exp, aff_ready, aff_tr, v_ready, v_tr, sel_ready = (
            sem(n) for n in ("wr_zero", "lg_mm", "lg_cp", "lg_nat", "lg_sub", "lg_exp", "aff_ready", "aff_tr",
                             "v_ready", "v_tr", "sel_ready"))
        gat_l, gat_c, gat_lv, gat_ca = (sem(n) for n in ("gat_l", "gat_c", "gat_lv", "gat_ca"))
        sg_ready, sg_tr, sg_cp = sem("sg_ready"), sem("sg_tr"), sem("sg_cp")
        facc_zero, xe_st, sc_st, e_silu, e_h, e_htr, e_hT, e_yc, e_sc, e_acc = (
            sem(n) for n in ("facc_zero", "xe_st", "sc_st", "e_silu", "e_h", "e_htr", "e_hT", "e_yc", "e_sc",
                             "e_acc"))
        sumsq4, ms4, rstd4, diag2_ready, g2_bc, g2_used, y_ready = (
            sem(n) for n in ("sumsq4", "ms4", "rstd4", "diag2_ready", "g2_bc", "g2_used", "y_ready"))

        B_HY = ADA_A // 2
        B_QKV = B_HY + 6
        B_GA = B_QKV + 6
        B_GB = B_GA + 4
        B_AO = B_GB + 2
        B_HO = B_AO + 2
        B_WO = B_HO + 1
        B_EX = B_WO + 2

        def block(w, h, c):
            return w[h * HK * P:(h + 1) * HK * P, ds(c * NC_, NC_)].rearrange("(k p) n -> p k n", p=P)

        blk = ctx.enter_context(nc.Block())

        @blk.sync
        def _(sp):
            def turn(b, parts):
                for j, (w, h, c) in enumerate(parts):
                    if b is not None:
                        sp.wait_ge(blocks_used, b * 4 + (j - 3))
                    sp.dma_start(ring[:, j], block(w, h, c)).then_inc(landed[j], 16)

            turn(None, [(w_ada, 0, 0), (w_ada, 1, 0), (w_ada, 0, 1), (w_ada, 1, 1)])
            with sp.Fori(1, ADA_A // 2) as i:
                turn(i, [(w_ada, 0, 2 * i), (w_ada, 1, 2 * i), (w_ada, 0, 2 * i + 1), (w_ada, 1, 2 * i + 1)])
            for base, ada0, in0, n in ((B_HY, 8, 6, 6), (B_QKV, 14, 0, 6), (B_GA, 20, 12, 4)):
                with sp.Fori(0, n) as i:
                    turn(i + base, [(w_ada, 0, i + ada0), (w_ada, 1, i + ada0),
                                    (w_in, 0, i + in0), (w_in, 1, i + in0)])
            for base, w, c0 in ((B_GB, w_in, 16), (B_AO, w_attn_o, 0)):
                with sp.Fori(0, 2) as i:
                    turn(i + base, [(w, 0, 2 * i + c0), (w, 1, 2 * i + c0),
                                    (w, 0, 2 * i + (c0 + 1)), (w, 1, 2 * i + (c0 + 1))])
            turn(B_HO, [(w_hy_o, 0, c) for c in range(4)])
            with sp.Fori(0, 2) as i:
                turn(i + B_WO, [(w_out, 0, 2 * i), (w_out, 1, 2 * i),
                                (w_out, 0, 2 * i + 1), (w_out, 1, 2 * i + 1)])
            with sp.Fori(0, NE) as e:
                def rows(w, n_rows, h, c):
                    return w[ds(e * n_rows + h * HK * P, HK * P), c * NC_:(c + 1) * NC_] \
                        .rearrange("(k p) n -> p k n", p=P)
                for n in range(2):
                    for j, (w, h) in enumerate(((w_gate, 0), (w_up, 0), (w_gate, 1), (w_up, 1))):
                        sp.wait_ge(blocks_used, e * 12 + (4 * (B_EX + n) + j - 3))
                        sp.dma_start(ring[:, j], rows(w, D, h, n)).then_inc(landed[j], 16)
                for j in range(4):
                    sp.wait_ge(blocks_used, e * 12 + (4 * (B_EX + 2) + j - 3))
                    sp.dma_start(ring[:, j], rows(w_down, FF, 0, j)).then_inc(landed[j], 16)
            for m in range(MT):
                sp.wait_ge(y_ready, m + 1)
                dst = y_prompt if m == 0 else y_sample[(m - 1) * P:m * P, :]
                sp.dma_start(dst, res[:, m, :]).then_inc(out_done, 16)
            sp.wait_ge(out_done, 16 * (MT + 2))

        @blk.tensor
        def _(pe):
            mm, trp = nc.tensor.matmul, nc.tensor.transpose

            def ada(b, j0, rows_bank):
                for h in range(2):
                    pe.wait_ge(landed[j0 + h], b * 16 + 16)
                    for k in range(HK):
                        kk, g = h * HK + k, k % 4
                        last = mm(bank(rows_bank, p0=32 * g, p1=32 * g + 32), condS[:, kk, :],
                                  ring[:, j0 + h, k, :], start=kk < 4, stop=kk >= KT - 4)
                    last.then_inc(blocks_used, 1)

            def ada_cols(c, which):
                pe.wait_ge(rows_copied, c + 1)
                src = rowbuf if which == 0 else tmp
                for j in range(4):
                    last = mm(PS[:, 6, ds(c * 8 + 2 * j, 2)], src[:, j * P:(j + 1) * P], sel2,
                              start=True, stop=True)
                last.then_inc(cols_done, 1)

            def channels(b, j0, b0, rhs):
                for h in range(2):
                    pe.wait_ge(landed[j0 + h], b * 16 + 16)
                    for k in range(HK):
                        for c in range(4):
                            last = mm(bank(b0 + c, T), ring[:, j0 + h, k, c * P:(c + 1) * P],
                                      rhs[:, h * HK + k, :], start=(h == 0 and k == 0),
                                      stop=(h == 1 and k == HK - 1))
                    last.then_inc(blocks_used, 1)

            def tokens(b, j0, b0, lhs):
                for h in range(2):
                    pe.wait_ge(landed[j0 + h], b * 16 + 16)
                    for k in range(HK):
                        for m in range(MT):
                            last = mm(bank(b0 + m), lhs[:, h * HK + k, m * P:(m + 1) * P],
                                      ring[:, j0 + h, k, :], start=(h == 0 and k == 0),
                                      stop=(h == 1 and k == HK - 1))
                    last.then_inc(blocks_used, 1)

            pe.wait_ge(small_in, 32)

            pe.wait_ge(filt_in, 112)
            mm(bank(0, T, p1=HF), f1[0:HE, :], zf[0:HE, :], start=True, stop=True).then_inc(f_mm, 1)
            pe.wait_ge(xn1, MT)
            for k in range(KT):
                if k >= 3:
                    pe.wait_ge(tr1_copied, k - 2)
                for m in range(MT):
                    last = trp(bank(1 + k % 3, P, m * P), xn[:, m, k * P:(k + 1) * P], ident)
                last.then_inc(tr1, 1)
            pe.wait_ge(f_sin, 1)
            mm(bank(4, T, p1=HF), f2[0:HF, :], arg[0:HF, :], start=True, stop=True).then_inc(f_mm, 1)

            pe.wait_ge(cond_ready, 1)
            with pe.Fori(0, ADA_A // 2) as i:
                ada(i, 0, 7)
                ada(i, 2, 5)
                ada_cols(i * 2, 0)
                ada_cols(i * 2 + 1, 1)

            pe.wait_ge(f_sin, 2)
            for m in range(MT):
                for c in range(4):
                    n = 4 * m + c
                    if n >= 4:
                        pe.wait_ge(f_taps, n - 3)
                    elif n > 0:
                        pe.wait_ge(tr1_copied, KT)
                    mm(bank(n % 4), arg[0:HF, m * P:(m + 1) * P], f3[0:HF, c * NC_:(c + 1) * NC_],
                       start=True, stop=True).then_inc(f_tapmm, 1)
            pe.wait_ge(dft_in, 16)
            pe.wait_ge(f_taps, 12)
            pe.wait_ge(f_sumdiff, 1)
            n = 0
            for j in range(3):
                for cs in range(2):
                    taps = dec if cs == 0 else hN
                    for half in range(2):
                        if n >= 4:
                            pe.wait_ge(f_spec_a if n % 2 == 0 else f_spec_v, (n - 4) // 2 + 1)
                        hs = slice(half * NC_, (half + 1) * NC_)
                        if j == 0:
                            last = mm(bank(n % 4), fwd_c[:, cs, :], taps[:, 0, hs], start=True, stop=True)
                        else:
                            for t in range(2):
                                last = mm(bank(n % 4), fwd_l[:, t, cs, (j - 1) * P:j * P], taps[:, 1 + t, hs],
                                          start=t == 0, stop=t == 1)
                        last.then_inc(f_dft, 1)
                        n += 1

            with pe.Fori(0, 6) as i:
                ada(i + B_HY, 0, 7)
                pe.wait_ge(conv_free, i * 4 + 4)
                channels(i + B_HY, 2, 0, hT)
                ada_cols(i + 8, 0)

            pe.wait_ge(conv_free, 28)
            pe.wait_ge(u_ready, 1)
            for n, (m, half) in enumerate((m, half) for half in range(2) for m in range(MT)):
                for c in range(4):
                    last = trp(bank(n, P, c * P), hyT[:, 2 * HYT + half * 4 + c, m * P:(m + 1) * P], ident)
                last.then_inc(u_tr, 1)
            for half in range(2):
                hs = slice(half * NC_, (half + 1) * NC_)
                pe.wait_ge(u_cp, 6)
                if half:
                    pe.wait_ge(z_ready, 3)
                for j in range(3):
                    for cs in range(2):
                        b = 2 * j + cs
                        if j == 0:
                            last = mm(bank(b), fwd_c[:, cs, :], uN[:, 0, hs], start=True, stop=True)
                        else:
                            for t in range(2):
                                last = mm(bank(b), fwd_l[:, t, cs, (j - 1) * P:j * P], uN[:, 1 + t, hs],
                                          start=t == 0, stop=t == 1)
                    last.then_inc(u_dft, 1)
                pe.wait_ge(z_ready, 3 * half + 3)
                for c in range(4):
                    n = 4 * half + c
                    cc = slice(c * P, (c + 1) * P)
                    b = 7 if n % 2 == 0 else 5
                    if n >= 2:
                        pe.wait_ge(yh_done, n - 1)
                    for cs in range(2):
                        mm(bank(b, TC), Z[:, 0, cs, cc], inv_c[:, cs, :], start=cs == 0, stop=cs == 1)
                    for q in range(4):
                        last = mm(bank(b, TL, TC), Z[:, 1 + q // 2, q % 2, cc], inv_l[:, q // 2, q % 2, :],
                                  start=q == 0, stop=q == 3)
                    last.then_inc(z_inv, 1)
                if half == 0:
                    pe.wait_ge(yh_done, 4)

            pe.wait_ge(yh_done, 8)
            with pe.Fori(0, 6) as i:
                ada(i + B_QKV, 0, 7)
                pe.wait_ge(qkv_raw, i * 3 + 3)
                tokens(i + B_QKV, 2, 0, hT)
                ada_cols(i + 14, 0)

            pe.wait_ge(mod2_read, 1)

            def scores(g, j):
                b0 = 2 * (j % 2)
                mm(bank(b0, 384), qT[:, j, TC:TC + P], kT[:, TC:], start=True, stop=True)
                mm(bank(b0, TC, 384), qT[:, j, 0:TC], kT[:, 0:TC], start=True, stop=True)
                mm(bank(b0 + 1, 384), qT[:, j, TC + P:T], kT[:, TC:], start=True, stop=True).then_inc(at_s, 1)

            with pe.Fori(0, NKV) as g:
                pe.wait_ge(staged, g + 1)
                for j in range(GRP):
                    for m in range(MT):
                        last = trp(bank(j, P, m * P), q_st[:, m, j, :], ident)
                    last.then_inc(at_trq, 1)
                for m in range(4):
                    last = trp(bank(4, P, m * P), k_st[:, m, :], ident)
                last.then_inc(at_trq, 1)
                pe.wait_ge(at_qT, g * 4 + 4)
                pe.wait_ge(at_kT, g + 1)
                scores(g, 0)
                for j in range(GRP):
                    if j + 1 < GRP:
                        if j >= 1:
                            pe.wait_ge(at_exp, g * 4 + j)
                        scores(g, j + 1)
                    pe.wait_ge(at_norm, g * 4 + (j + 1))
                    for kt in range(3):
                        for qt in range(2):
                            o = kt * 256 + qt * P
                            last = trp(bank(4 + o // 512, P, o % 512),
                                       prob[:, j % 2, qt * 384 + kt * P:qt * 384 + (kt + 1) * P], ident)
                    last = trp(bank(5, P, 256), prob[:, j % 2, 768:896], ident)
                    last.then_inc(at_trp, 1)
                    pe.wait_ge(at_pa, g * 4 + (j + 1))
                    pe.wait_ge(at_pb, g * 4 + (j + 1))
                    b = 6 + j % 2
                    if j >= 2:
                        pe.wait_ge(at_oc, g * 4 + (j - 1))
                    mm(bank(b, TC), v_st[:, 0, :], probT[:, 768:896], start=True, stop=True)
                    for kt in range(3):
                        last = mm(bank(b, TL, TC), v_st[:, 1 + kt, :], probT[:, kt * 256:(kt + 1) * 256],
                                  start=kt == 0, stop=kt == 2)
                    last.then_inc(at_o, 1)
                pe.wait_ge(at_oc, g * 4 + 4)

            with pe.Fori(0, 4) as i:
                ada(i + B_GA, 0, 7)
                pe.wait_ge(gate_sig, i * 4 + 1)
                channels(i + B_GA, 2, 0, hT)
                ada_cols(i + 20, 0)
            pe.wait_ge(mod3_read, 1)
            with pe.Fori(0, 2) as i:
                for a in range(2):
                    pe.wait_ge(gate_sig, i * 8 + (17 if a == 0 else 13))
                    channels(i + B_GB, 2 * a, 4 * a, hT)
            pe.wait_ge(gate_sig, 33)
            with pe.Fori(0, 2) as i:
                for a in range(2):
                    pe.wait_ge(ao_done, i * 8 + (4 * a + 1))
                    channels(i + B_AO, 2 * a, 4 * a, oT)
            for c in range(4):
                pe.wait_ge(ao_done, 17)
                if c >= 2:
                    pe.wait_ge(ho_done, 4 * (c - 1))
                pe.wait_ge(landed[c], 16 * (B_HO + 1))
                for k in range(HYT):
                    for j in range(4):
                        last = mm(bank(4 * (c % 2) + j, T), ring[:, c, k, j * P:(j + 1) * P], yhT[:, k, :],
                                  start=k == 0, stop=k == HYT - 1)
                last.then_inc(blocks_used, 1)
            pe.wait_ge(ho_done, 16)
            with pe.Fori(0, 2) as i:
                for a in range(2):
                    pe.wait_ge(wo_cp, i * 6 + (3 * a + 1))
                    tokens(i + B_WO, 2 * a, 3 * a, sg)

            def broadcast_gates(ready, done, used):
                for n in range(8):
                    pe.wait_ge(ready, n + 1)
                    if n >= 2:
                        pe.wait_ge(used, n - 1)
                    mm(bank(6 + n % 2), ones, diag[:, n % 2, :], start=True, stop=True).then_inc(done, 1)

            broadcast_gates(diag_ready, g_bc, g_used)

            pe.wait_ge(xn2, MT)
            for k in range(KT):
                if k >= 4:
                    pe.wait_ge(tr2_v if k % 2 == 0 else tr2_a, k // 2 - 1)
                for m in range(MT):
                    last = trp(bank(k % 4, P, m * P), xn[:, m, k * P:(k + 1) * P], ident)
                last.then_inc(tr2, 1)
            pe.wait_ge(wr_in, 16)
            pe.wait_ge(tr2_v, KT // 2)
            pe.wait_ge(tr2_a, KT // 2)
            for k in range(KT):
                g = k % 4
                last = mm(bank(4, T, p0=32 * g, p1=32 * g + 32), wr[:, k, :], hT[:, k, :],
                          start=k < 4, stop=k >= KT - 4)
            last.then_inc(lg_mm, 1)
            pe.wait_ge(lg_cp, 1)
            for m in range(MT):
                last = mm(bank(5, NE, m * NE), lgr[:, m * P:(m + 1) * P], sel16, start=True, stop=True)
            last.then_inc(lg_nat, 1)
            pe.wait_ge(aff_ready, 1)
            for m in range(MT):
                last = trp(bank(4, P, m * P, p1=NE), aff[:, m, :], ident)
            last.then_inc(aff_tr, 1)
            pe.wait_ge(v_ready, 1)
            for m in range(MT):
                last = trp(bank(5, NE, m * NE), cum[0:NE, m * P:(m + 1) * P], ident[0:NE, 0:NE])
            last.then_inc(v_tr, 1)
            pe.wait_ge(sel_ready, 1)
            for k in range(KT):
                if k >= 2:
                    pe.wait_ge(gat_lv, k - 1)
                    pe.wait_ge(gat_ca, k - 1)
                kk = slice(k * P, (k + 1) * P)
                mm(bank(2 + k % 2, NE * CAPC), xn[:, 0, kk], selC[:, :, :], start=True,
                   stop=True).then_inc(gat_c, 1)
                for t in range(2):
                    last = mm(bank(k % 2), xn[:, 1 + t, kk], selL[:, t, :, :], start=t == 0, stop=t == 1)
                last.then_inc(gat_l, 1)
            for m in range(MT):
                pe.wait_ge(sg_ready, m + 1)
                for q in range(4):
                    n = 4 * m + q
                    if n >= 4:
                        pe.wait_ge(sg_cp, n - 3)
                    for j in range(4):
                        last = trp(bank(4 + n % 4, P, j * P), selG[:, 4 * q + j, :], ident)
                    last.then_inc(sg_tr, 1)
            pe.wait_ge(sg_cp, 12)

            pe.wait_ge(gat_lv, KT)
            pe.wait_ge(gat_ca, KT)
            pe.wait_ge(facc_zero, 1)
            with pe.Fori(0, NE) as e:
                pe.wait_ge(xe_st, e + 1)
                for n in range(2):
                    for h in range(2):
                        pe.wait_ge(landed[2 * h], e * 48 + 16 * (B_EX + n + 1))
                        pe.wait_ge(landed[2 * h + 1], e * 48 + 16 * (B_EX + n + 1))
                        for k in range(HK):
                            for u in range(2):
                                last = mm(bank(n, p0=64 * u, p1=64 * u + SLOTS), x_cur[:, h * HK + k, :],
                                          ring[:, 2 * h + u, k, :], start=(h == 0 and k == 0),
                                          stop=(h == 1 and k == HK - 1))
                                if k == HK - 1:
                                    last.then_inc(blocks_used, 1)
                for n in range(2):
                    pe.wait_ge(e_h, e * 2 + (n + 1))
                    for j in range(4):
                        o, src, i_ = bank(3, SLOTS, (4 * n + j) * SLOTS), h_s[0:SLOTS, j * P:(j + 1) * P], \
                            ident[0:SLOTS, 0:SLOTS]
                        last = mm(o, src, i_, start=True, stop=True) if j == 0 else trp(o, src, i_)
                    last.then_inc(e_htr, 1)
                pe.wait_ge(e_hT, e + 1)
                for i in range(2):
                    pe.wait_ge(landed[2 * i], e * 48 + 16 * (B_EX + 3))
                    pe.wait_ge(landed[2 * i + 1], e * 48 + 16 * (B_EX + 3))
                    for k in range(HK):
                        for u in range(2):
                            last = mm(bank(2 + i, p0=64 * u, p1=64 * u + SLOTS), hTe[:, k, :],
                                      ring[:, 2 * i + u, k, :], start=k == 0, stop=k == HK - 1)
                            if k == HK - 1:
                                last.then_inc(blocks_used, 1)
                pe.wait_ge(sc_st, e + 1)
                for i in range(2):
                    pe.wait_ge(e_yc, e * 2 + (i + 1))
                    for m in range(MT):
                        for u in range(2):
                            n = (i * MT + m) * 2 + u
                            if n >= 4:
                                pe.wait_ge(e_acc, e * 12 + (n - 3))
                            mm(bank(4 + n % 4), s_cur[64 * u:64 * u + SLOTS, m * P:(m + 1) * P],
                               ye[64 * u:64 * u + SLOTS, i, :], start=True, stop=True).then_inc(e_sc, 1)
                pe.wait_ge(e_acc, e * 12 + 12)

            broadcast_gates(diag2_ready, g2_bc, g2_used)

        @blk.scalar
        def _(act):
            A = nc.scalar.activation
            act.dma_start(col, cols).then_inc(small_in, 16)
            act.dma_start(KC[:, N_COLS:N_COLS + N_TABS], tabs).then_inc(small_in, 16)
            act.dma_start(xn[:, 0, :], x_prompt).then_inc(x_in, 16)
            act.dma_start(xn[:, 1:3, :], x_sample.rearrange("(m p) d -> p m d", p=P)).then_inc(x_in, 16)
            act.dma_start(zf[0:HE, :], zfeat).then_inc(filt_in, 16)
            act.dma_start(f1[0:HE, :], f1_w).then_inc(filt_in, 16)
            act.dma_start(f2[0:HF, :], f2_w).then_inc(filt_in, 16)
            act.dma_start(fv[0:HF, :], f_vec).then_inc(filt_in, 16)
            act.dma_start(f3[0:HF, :], f3_w).then_inc(filt_in, 16)
            act.dma_start(dec[:, 0, :], decay[0]).then_inc(filt_in, 16)
            act.dma_start(dec[:, 1:3, :], decay[1:3].rearrange("m p d -> p m d")).then_inc(filt_in, 16)

            act.wait_ge(small_in, 32)
            act.wait_ge(cond_ready, 1)
            A(condS[:, :, 0:2], col[:, C_COND:C_COND + 32].rearrange("p (c k) -> p k c", c=2),
              ACT.Silu).then_inc(cond_ready, 1)
            act.wait_ge(x_in, 32)
            for m in range(MT):
                A(sq_scr, xn[:, m, :], ACT.Square, accum_out=ss[:, m:m + 1]).then_inc(sumsq1, 1)
                act.drain()
            act.wait_ge(f_arg, 1)
            A(arg[0:HF, :], arg[0:HF, :], ACT.Sin).then_inc(f_sin, 1)
            act.wait_ge(f_arg, 2)
            A(arg[0:HF, :], arg[0:HF, :], ACT.Sin).then_inc(f_sin, 1)
            act.wait_ge(tr1, KT)
            act.dma_start(dft_t, dft).then_inc(dft_in, 16)

            def rows(used, src_bank, dst):
                act.wait_ge(blocks_used, used)
                A(dst, bank(src_bank), ACT.Copy).then_inc(rows_copied, 1)

            rows(2, 7, rowbuf)
            rows(4, 5, tmp)
            with act.Fori(1, ADA_A // 2) as i:
                act.wait_ge(cols_done, i * 2)
                rows(i * 4 + 2, 7, rowbuf)
                rows(i * 4 + 4, 5, tmp)

            for n in range(0, 12, 2):
                act.wait_ge(f_dft, n + 1)
                A(spec[:, n // 4, (n // 2) % 2, 0:NC_], bank(n % 4), ACT.Copy).then_inc(f_spec_a, 1)
            act.wait_ge(f_spec_v, 6)

            with act.Fori(0, 6) as i:
                act.wait_ge(cols_done, i + 8)
                rows(i * 4 + (4 * B_HY + 2), 7, rowbuf)
                act.wait_ge(blocks_used, i * 4 + (4 * B_HY + 4))
                for j in range(4):
                    A(hyT[:, ds(i * 4 + j, 1), :], bank(j, T), ACT.Identity,
                      bias=col[:, ds(i * 4 + (C_CB + j), 1)],
                      scale=col[:, ds(i * 4 + (C_CW + 24 + j), 1)]).then_inc(conv_mid, 1)

            for n in range(0, 6, 2):
                act.wait_ge(u_tr, n + 1)
                half, m = n // MT, n % MT
                A(uN[:, m, half * NC_:(half + 1) * NC_], bank(n), ACT.Copy).then_inc(u_cp, 1)

            act.wait_ge(z_ready, 6)
            act.dma_start(rope_t[:, :, :, :], rope).then_inc(qk_in, 16)
            act.dma_start(gain_b, qk_g.rearrange("(o a) d -> o (a d)", o=1).to_broadcast([P, 2 * HD])
                          .rearrange("p (a d) -> p a d", a=2)).then_inc(qk_in, 16)
            act.wait_ge(yh_done, 8)
            act.dma_start(kcN, cache_k).then_inc(cache_in, 16)
            act.dma_start(vN[:, 3, :], cache_v).then_inc(cache_in, 16)
            act.wait_ge(yh_done, 8)
            act.nop().then_inc(qkv_raw, 3)
            with act.Fori(0, 5) as i:
                act.wait_ge(cols_done, i + 14)
                rows(i * 4 + (4 * B_QKV + 2), 7, rowbuf)
                act.wait_ge(blocks_used, i * 4 + (4 * B_QKV + 4))
                for m in range(MT):
                    A(qkN[:, m, ds(i * NC_, NC_)], bank(m), ACT.Copy).then_inc(qkv_raw, 1)
            act.wait_ge(cols_done, 19)
            rows(4 * B_QKV + 22, 7, rowbuf)
            act.wait_ge(blocks_used, 4 * B_QKV + 24)
            for m in range(MT):
                A(vN[:, m, :], bank(m), ACT.Copy).then_inc(v_done, 1)
            act.wait_ge(v_done, MT)
            act.dma_start(state_v, vN[:, 0, :]).then_inc(out_done, 16)
            act.wait_ge(qk_done, 5)
            act.dma_start(state_k, qkN[:, 0, D:D + KVW]).then_inc(out_done, 16)

            with act.Fori(0, NKV) as g:
                for j in range(GRP):
                    act.wait_ge(at_trq, g * 5 + (j + 1))
                    A(qT[:, j, :], bank(j, T), ACT.Copy).then_inc(at_qT, 1)
                for j in range(GRP):
                    p = j % 2
                    act.wait_ge(at_max, g * 4 + (j + 1))
                    if j >= 2:
                        act.wait_ge(at_trp, g * 4 + (j - 1))
                    A(prob[:, p, 0:384], bank(2 * p, 384), ACT.Exp, bias=nb[:, p, 0:1], scale=SCALE,
                      accum_out=rs[:, p, 0:1])
                    A(prob[:, p, 384:768], bank(2 * p + 1, 384), ACT.Exp, bias=nb[:, p, 1:2], scale=SCALE,
                      accum_out=rs[:, p, 1:2])
                    A(prob[:, p, 768:896], bank(2 * p, TC, 384), ACT.Exp, bias=nb[:, p, 2:3], scale=SCALE,
                      accum_out=rs[:, p, 2:3])
                    act.drain()
                    act.nop().then_inc(at_exp, 1)
                    act.wait_ge(at_trp, g * 4 + (j + 1))
                    if j >= 1:
                        act.wait_ge(at_o, g * 4 + j)
                    A(probT[:, 0:512], bank(4), ACT.Copy).then_inc(at_pa, 1)
                    act.wait_ge(at_o, g * 4 + (j + 1))
                    A(oT[:, ds(g * 4 + j, 1), :], bank(6 + p, T), ACT.Copy).then_inc(at_oc, 1)

            act.wait_ge(at_oc, NH)
            act.dma_start(res[:, 0, :], x_prompt).then_inc(xres_in, 16)
            act.dma_start(res[:, 1:3, :], x_sample.rearrange("(m p) d -> p m d", p=P)).then_inc(xres_in, 16)

            act.wait_ge(out_done, 32)
            act.nop().then_inc(gate_sig, 1)
            with act.Fori(0, 4) as i:
                act.wait_ge(cols_done, i + 20)
                rows(i * 4 + (4 * B_GA + 2), 7, rowbuf)
                act.wait_ge(blocks_used, i * 4 + (4 * B_GA + 4))
                for j in range(4):
                    A(sg[:, ds(i * 4 + j, 1), :], bank(j, T), ACT.Sigmoid).then_inc(gate_sig, 1)
            with act.Fori(0, 2) as i:
                for a in range(2):
                    act.wait_ge(blocks_used, i * 4 + (4 * B_GB + 2 * a + 2))
                    for j in range(4):
                        A(sg[:, ds(i * 8 + (16 + 4 * a + j), 1), :], bank(4 * a + j, T),
                          ACT.Sigmoid).then_inc(gate_sig, 1)

            act.wait_ge(ho_done, 16)
            act.nop().then_inc(wo_cp, 1)
            with act.Fori(0, 2) as i:
                for a in range(2):
                    act.wait_ge(blocks_used, i * 4 + (4 * B_WO + 2 * a + 2))
                    for m in range(MT):
                        A(mix[:, m, ds(i * 1024 + a * NC_, NC_)], bank(3 * a + m), ACT.Copy).then_inc(wo_cp, 1)
            act.drain()
            for m in range(MT):
                A(sq_scr, mix[:, m, :], ACT.Square, accum_out=ss[:, m:m + 1]).then_inc(sumsq3, 1)
                act.drain()
            for m in range(MT):
                act.wait_ge(res_ready, m + 1)
                A(sq_scr, res[:, m, :], ACT.Square, accum_out=ss[:, m:m + 1]).then_inc(sumsq3, 1)
                act.drain()
            for k in range(1, KT, 2):
                act.wait_ge(tr2, k + 1)
                for c, (lo, hi) in enumerate(SEG):
                    last = A(hT[:, k, lo:hi], bank(k % 4, hi - lo, lo), ACT.Identity,
                             bias=mod[:, SHIFT2 * KT + k, c:c + 1], scale=amp[:, 1, k, c:c + 1])
                last.then_inc(tr2_a, 1)
            act.wait_ge(lg_mm, 1)
            A(lgr, bank(4, T), ACT.Copy).then_inc(lg_cp, 1)
            act.wait_ge(lg_sub, 1)
            A(aff[:, :, :], aff[:, :, :], ACT.Exp).then_inc(lg_exp, 1)
            for k in range(KT):
                act.wait_ge(gat_c, k + 1)
                A(xeT[:, k, :, CAPL:SLOTS], bank(2 + k % 2, NE * CAPC).rearrange("p (e s) -> p e s", e=NE),
                  ACT.Identity, bias=mod[:, SHIFT2 * KT + k, 0:1], scale=amp[:, 1, k, 0:1]).then_inc(gat_ca, 1)
            act.wait_ge(lg_nat, 1)
            for n in range(12):
                act.wait_ge(sg_tr, n + 1)
                m, q = n // 4, n % 4
                A(scat[:, 4 * q:4 * q + 4, m * P:(m + 1) * P],
                  bank(4 + n % 4).rearrange("p (j t) -> p j t", j=4), ACT.Copy).then_inc(sg_cp, 1)

            act.wait_ge(v_tr, 1)
            with act.Fori(0, NE) as e:
                for n in range(2):
                    act.wait_ge(blocks_used, e * 12 + (4 * (B_EX + n) + 4))
                    if n:
                        act.wait_ge(e_h, e * 2 + 1)
                    A(act_s[0:SLOTS, :], bank(n, p1=SLOTS), ACT.Silu).then_inc(e_silu, 1)
                for i in range(2):
                    act.wait_ge(blocks_used, e * 12 + (4 * (B_EX + 2) + 2 * i + 2))
                    for u in range(2):
                        last = A(ye[64 * u:64 * u + SLOTS, i, :], bank(2 + i, p0=64 * u, p1=64 * u + SLOTS),
                                 ACT.Copy)
                    last.then_inc(e_yc, 1)
            for m in range(MT):
                act.wait_ge(e_acc, 12 * NE)
                A(sq_scr, facc[:, m, :], ACT.Square, accum_out=ss[:, m:m + 1]).then_inc(sumsq4, 1)
                act.drain()

        @blk.gpsimd
        def _(pool):
            g_ = nc.gpsimd
            g_.memset(condS[:, :, :], 0.0).then_inc(cond_ready, 1)
            g_.memset(neghalf, -0.5)
            pool.drain()

            def inv_root(src_sem, n, cols_, done):
                pool.wait_ge(src_sem, n)
                g_.tensor_tensor(rstd[:, 0:cols_], ss[:, 0:cols_], neghalf[:, 0:cols_],
                                 ALU.pow).then_inc(done, 1)

            inv_root(ms1, 1, MT, rstd1)
            with pool.Fori(0, 5) as i:
                pool.wait_ge(q_ms, i + 1)
                g_.tensor_tensor(rstd, ss, neghalf, ALU.pow).then_inc(q_rstd, 1)
            pool.wait_ge(qk_done, 5)
            pool.wait_ge(v_done, MT)
            pool.wait_ge(cache_in, 32)
            with pool.Fori(0, NKV) as g:
                g_.tensor_copy(q_st[:, :, :, :].rearrange("p m j d -> p m (j d)"), qkN[:, :, ds(g * 512, 512)])
                g_.tensor_copy(k_st[:, 0:3, :], qkN[:, :, ds(g * HD + D, HD)])
                g_.tensor_copy(k_st[:, 3, :], kcN[:, ds(g * HD, HD)])
                g_.tensor_copy(v_st[:, :, :], vN[:, :, ds(g * HD, HD)])
                pool.drain()
                g_.memset(SM[:, 120:121], 0.0).then_inc(staged, 1)
                pool.wait_ge(at_o, g * 4 + 4)
            inv_root(ms2, 1, MT, rstd2)
            pool.wait_ge(mod3_read, 1)
            g_.memset(wr[:, :, :], 0.0)
            g_.memset(ones, 1.0).then_inc(wr_zero, 1)
            pool.wait_ge(wr_zero, 1)
            pool.dma_start(wr[:, :, 0:NE], w_router.rearrange("(k p) e -> p k e", p=P)).then_inc(wr_in, 16)
            inv_root(ms3, 1, MT, rstd3s)
            pool.wait_ge(gat_lv, KT)
            pool.wait_ge(gat_ca, KT)
            g_.memset(facc[:, :, :], 0.0).then_inc(facc_zero, 1)
            pool.wait_ge(sg_cp, 12)
            with pool.Fori(0, NE) as e:
                g_.tensor_copy(x_cur[:, :, :], xeT[:, :, ds(e, 1), :].rearrange("p k o s -> p k (o s)"))\
                    .then_inc(xe_st, 1)
                g_.tensor_copy(s_cur, scat[:, ds(e, 1), :].rearrange("p o t -> p (o t)")).then_inc(sc_st, 1)
                pool.wait_ge(e_sc, e * 12 + 12)
            g_.memset(ones, 1.0).then_inc(wr_zero, 1)
            inv_root(ms4, 1, MT, rstd4)

        @blk.vector
        def _(dve):
            V = nc.vector
            ts_, tt, stt = V.tensor_scalar, V.tensor_tensor, V.scalar_tensor_tensor

            def mean_square(sem_in, n_in, cols_, width, done):
                dve.wait_ge(sem_in, n_in)
                ts_(ss[:, 0:cols_], ss[:, 0:cols_], 1.0 / width, EPS, ALU.mult, ALU.add).then_inc(done, 1)

            def sine_argument(src_bank, bias, n):
                dve.wait_ge(f_mm, n)
                a, r = arg[0:HF, :], rnd[0:HF, :]
                ts_(a, bank(src_bank, T, p1=HF), bias, fv[0:HF, 1:2], ALU.add, ALU.mult)
                dve.drain()
                ts_(r, a, 1.0 / TWO_PI, MAGIC, ALU.mult, ALU.add)
                dve.drain()
                ts_(r, r, MAGIC, None, ALU.subtract)
                for part in (PI_A, PI_B, PI_C):
                    dve.drain()
                    stt(out=a, in0=r, scalar=-part, in1=a, op0=ALU.mult, op1=ALU.add)
                dve.drain()
                ts_(a, a, PI_IN, -PI_IN, ALU.min, ALU.max).then_inc(f_arg, 1)

            dve.wait_ge(filt_in, 112)
            sine_argument(0, fv[0:HF, 0:1], 1)
            mean_square(sumsq1, MT, MT, D, ms1)
            dve.wait_ge(rstd1, 1)
            for m in range(MT):
                ts_(xn[:, m, :], xn[:, m, :], rstd[:, m:m + 1], None, ALU.mult).then_inc(xn1, 1)
            for k in range(KT):
                dve.wait_ge(tr1, k + 1)
                V.tensor_copy(hT[:, k, :], bank(1 + k % 3, T)).then_inc(tr1_copied, 1)
            sine_argument(4, fv[0:HF, 2:3], 2)
            for n in range(12):
                m, c = n // 4, n % 4
                dve.wait_ge(f_tapmm, n + 1)
                tt(hN[:, m, c * NC_:(c + 1) * NC_], bank(n % 4), dec[:, m, (c % 2) * NC_:(c % 2 + 1) * NC_],
                   ALU.mult).then_inc(f_taps, 1)
            dve.drain()
            V.memset(hN[0:1, 0, HYW:D], 0.0)
            V.memset(hN[0:1, 1, HYW:D], 0.0)
            dve.drain()
            tt(dec[:, :, :], hN[:, :, 0:HYW], hN[:, :, HYW:D], ALU.add)
            dve.drain()
            tt(hN[:, :, 0:HYW], hN[:, :, 0:HYW], hN[:, :, HYW:D], ALU.subtract).then_inc(f_sumdiff, 1)
            for n in range(1, 12, 2):
                dve.wait_ge(f_dft, n + 1)
                V.tensor_copy(spec[:, n // 4, (n // 2) % 2, NC_:2 * NC_], bank(n % 4)).then_inc(f_spec_v, 1)

            def read_mods(lo, hi, n):
                dve.wait_ge(cols_done, n)
                tt(mod[:, lo:hi, :], PS[:, 6, 2 * lo:2 * hi].rearrange("p (a c) -> p a c", c=2),
                   col[:, C_BADA + lo:C_BADA + hi].unsqueeze(2).to_broadcast([P, hi - lo, 2]), ALU.add)
                dve.drain()

            def gains(dst, part, gain, add):
                stt(out=dst, in0=mod[:, part * KT:(part + 1) * KT, :], scalar=add,
                    in1=col[:, gain:gain + KT].unsqueeze(2).to_broadcast([P, KT, 2]), op0=ALU.add, op1=ALU.mult)

            read_mods(0, 32, ADA_A)
            gains(amp[:, 0], SCALE1, C_GPRE1, 1.0)
            dve.drain()
            with dve.Fori(0, KT) as k:
                for c, (lo, hi) in enumerate(SEG):
                    ts_(hT[:, ds(k, 1), lo:hi], hT[:, ds(k, 1), lo:hi], MODS[:, ds(k * 2 + (192 + c), 1)],
                        MODS[:, ds(k * 2 + (SHIFT1 * KT * 2 + c), 1)], ALU.mult, ALU.add)
            dve.drain()
            dve.wait_ge(f_spec_a, 6)
            V.memset(SM[:, 121:122], 0.0).then_inc(conv_free, 4)

            with dve.Fori(0, 6) as i:
                for j in range(4):
                    dve.wait_ge(conv_mid, i * 4 + (j + 1))
                    for tap in range(2):
                        w = col[:, ds(i * 4 + (C_CW + 48 * tap + j), 1)]
                        for lo, hi in SEG:
                            a, b = (lo + 1, hi) if tap == 0 else (lo, hi - 1)
                            o = -1 if tap == 0 else 1
                            last = stt(out=hyT[:, ds(i * 4 + j, 1), a:b].rearrange("p o t -> p (o t)"),
                                       in0=bank(j, b - a, a + o), scalar=w,
                                       in1=hyT[:, ds(i * 4 + j, 1), a:b].rearrange("p o t -> p (o t)"),
                                       op0=ALU.mult, op1=ALU.add)
                        if tap == 0:
                            dve.drain()
                    last.then_inc(conv_free, 1)
            dve.drain()
            tt(hyT[:, 2 * HYT:3 * HYT, :], hyT[:, 2 * HYT:3 * HYT, :], hyT[:, HYT:2 * HYT, :],
               ALU.mult).then_inc(u_ready, 1)
            for n in range(1, 6, 2):
                dve.wait_ge(u_tr, n + 1)
                half, m = n // MT, n % MT
                V.tensor_copy(uN[:, m, half * NC_:(half + 1) * NC_], bank(n)).then_inc(u_cp, 1)
            for half in range(2):
                hs = slice(half * NC_, (half + 1) * NC_)
                for j in range(3):
                    dve.wait_ge(u_dft, 3 * half + j + 1)
                    if half and j == 0:
                        dve.wait_ge(z_inv, 4)
                    hc, hsn = spec[:, j, 0, hs], spec[:, j, 1, hs]
                    uc, us = bank(2 * j), bank(2 * j + 1)
                    dve.drain()
                    tt(Z[:, j, 0, :], uc, hc, ALU.mult)
                    tt(tmp, us, hsn, ALU.mult)
                    tt(Z[:, j, 1, :], uc, hsn, ALU.mult)
                    dve.drain()
                    tt(Z[:, j, 0, :], Z[:, j, 0, :], tmp, ALU.subtract)
                    dve.drain()
                    tt(tmp, us, hc, ALU.mult)
                    dve.drain()
                    tt(Z[:, j, 1, :], Z[:, j, 1, :], tmp, ALU.add).then_inc(z_ready, 1)
                for c in range(4):
                    n = 4 * half + c
                    dve.wait_ge(z_inv, n + 1)
                    dve.drain()
                    stt(out=tmp[:, 0:T], in0=hyT[:, 2 * HYT + n, :], scalar=col[:, C_SKIP + n:C_SKIP + n + 1],
                        in1=bank(7 if n % 2 == 0 else 5, T), op0=ALU.mult, op1=ALU.add)
                    dve.drain()
                    tt(yhT[:, n, :], tmp[:, 0:T], hyT[:, n, :], ALU.mult).then_inc(yh_done, 1)

            dve.wait_ge(qk_in, 32)
            for a in range(2):
                for m in range(2):
                    tt(rot[:, a, m, :, :], rope_t[:, m, :, :],
                       gain_b[:, a, :].unsqueeze(1).to_broadcast([P, 2, HD]), ALU.mult)
            dve.drain()

            def qk_norm(i, x, a):
                for m in range(MT):
                    dve.drain()
                    dve.wait_ge(qkv_raw, i * 3 + (m + 4))
                    tt(t_a, x(m), x(m), ALU.mult)
                    dve.drain()
                    V.tensor_reduce(ss[:, 4 * m:4 * m + 4], t_a.rearrange("p (h d) -> p h d", h=4), AX_X, ALU.add)
                dve.drain()
                ts_(ss, ss, 1.0 / HD, EPS, ALU.mult, ALU.add).then_inc(q_ms, 1)
                dve.wait_ge(q_rstd, i + 1)
                for m in range(MT):
                    xh = x(m).rearrange("p (h d) -> p h d", h=4)
                    tah, tbh = (t.rearrange("p (h d) -> p h d", h=4) for t in (t_a, t_b))
                    if m:
                        dve.drain()
                    tt(xh, xh, rstd[:, 4 * m:4 * m + 4].unsqueeze(2).to_broadcast([P, 4, HD]), ALU.mult)
                    dve.drain()
                    if m == 0:
                        tt(xh, xh, gain_b[:, a, :].unsqueeze(1).to_broadcast([P, 4, HD]), ALU.mult)
                        continue
                    own = rot[:, a, m - 1, 0, :].unsqueeze(1).to_broadcast([P, 4, HD])
                    other = rot[:, a, m - 1, 1, :].unsqueeze(1).to_broadcast([P, 4, HD])
                    tt(tah, xh, own, ALU.mult)
                    tt(tbh, xh, other, ALU.mult)
                    dve.drain()
                    x4 = x(m).rearrange("p (g s d) -> p g s d", s=2, d=32)
                    a4, b4 = (t.rearrange("p (g s d) -> p g s d", s=2, d=32) for t in (t_a, t_b))
                    for s in range(2):
                        tt(x4[:, :, s, :], a4[:, :, s, :], b4[:, :, 1 - s, :], ALU.add)
                dve.drain()
                V.memset(SM[:, 121:122], 0.0).then_inc(qk_done, 1)
                dve.drain()

            with dve.Fori(0, 4) as i:
                qk_norm(i, lambda m: qkN[:, m, ds(i * NC_, NC_)], 0)
            qk_norm(4, lambda m: qkN[:, m, D:D + KVW], 1)
            read_mods(32, 80, 20)
            gains(amp[:, 1], SCALE2, C_GPRE2, 1.0)
            gains(gout[:, 0], GATE1, C_GPOST1, 0.0)
            dve.drain()
            V.memset(SM[:, 121:122], 0.0).then_inc(mod2_read, 1)

            with dve.Fori(0, NKV) as g:
                dve.wait_ge(at_trq, g * 5 + 5)
                V.tensor_copy(kT, bank(4)).then_inc(at_kT, 1)

                def maxima(j):
                    p = j % 2
                    dve.wait_ge(at_s, g * 4 + (j + 1))
                    V.reduce_max(mx[:, p, 0:1], bank(2 * p, 384), AX_X)
                    V.reduce_max(mx[:, p, 1:2], bank(2 * p + 1, 384), AX_X)
                    V.reduce_max(mx[:, p, 2:3], bank(2 * p, TC, 384), AX_X)
                    dve.drain()
                    ts_(nb[:, p, :], mx[:, p, :], -SCALE, None, ALU.mult).then_inc(at_max, 1)
                    dve.drain()

                maxima(0)
                for j in range(GRP):
                    p = j % 2
                    if j + 1 < GRP:
                        maxima(j + 1)
                    dve.wait_ge(at_exp, g * 4 + (j + 1))
                    V.reciprocal(ri[:, p, :], rs[:, p, :])
                    dve.drain()
                    for t, (lo, hi) in enumerate(((0, 384), (384, 768), (768, 896))):
                        last = ts_(prob[:, p, lo:hi], prob[:, p, lo:hi], ri[:, p, t:t + 1], None, ALU.mult)
                    last.then_inc(at_norm, 1)
                    dve.wait_ge(at_trp, g * 4 + (j + 1))
                    if j >= 1:
                        dve.wait_ge(at_o, g * 4 + j)
                    V.tensor_copy(probT[:, 512:896], bank(5, 384)).then_inc(at_pb, 1)
                dve.drain()

            read_mods(80, 96, 24)
            gains(gout[:, 1], GATE2, C_GPOST2, 0.0)
            dve.drain()
            V.memset(SM[:, 121:122], 0.0).then_inc(mod3_read, 1)
            dve.wait_ge(gate_sig, 33)
            V.memset(SM[:, 122:123], 0.0).then_inc(ao_done, 1)
            with dve.Fori(0, 2) as i:
                for a in range(2):
                    dve.wait_ge(blocks_used, i * 4 + (4 * B_AO + 2 * a + 2))
                    for j in range(4):
                        d = sg[:, ds(i * 8 + (4 * a + j), 1), :].rearrange("p o t -> p (o t)")
                        tt(d, bank(4 * a + j, T), d, ALU.mult).then_inc(ao_done, 1)
            for c in range(4):
                dve.wait_ge(blocks_used, 4 * B_HO + c + 1)
                for j in range(4):
                    n, b = 4 * c + j, 4 * (c % 2) + j
                    dve.drain()
                    tt(sg[:, KT + n, :], bank(b, T), sg[:, KT + n, :], ALU.mult)
                    dve.drain()
                    tt(sg[:, n, :], sg[:, n, :], sg[:, KT + n, :], ALU.add).then_inc(ho_done, 1)

            def residual(which, src, ready, bc, used, done):
                for n in range(2):
                    diagonals(which, n, ready)
                order = [(c, q) for c in range(2) for q in range(4)]
                for n, (c, q) in enumerate(order):
                    dve.wait_ge(bc, n + 1)
                    qs = slice(q * NC_, (q + 1) * NC_)
                    for m in ((0,), (1, 2))[c]:
                        stt(out=src[:, m, qs], in0=src[:, m, qs], scalar=rstd[:, m:m + 1], in1=bank(6 + n % 2),
                            op0=ALU.mult, op1=ALU.mult)
                    dve.drain()
                    V.memset(SM[:, 121:122], 0.0).then_inc(used, 1)
                    for m in ((0,), (1, 2))[c]:
                        last = tt(res[:, m, qs], res[:, m, qs], src[:, m, qs], ALU.add)
                        if q == 3:
                            last.then_inc(done, 1)
                    dve.drain()
                    if n + 2 < 8:
                        diagonals(which, n + 2, ready)

            def diagonals(which, n, ready):
                c, q = n // 4, n % 4
                for j in range(4):
                    last = ts_(diag[:, n % 2, j * P:(j + 1) * P], ident,
                               gout[:, which, 4 * q + j, c:c + 1], None, ALU.mult)
                last.then_inc(ready, 1)

            mean_square(sumsq3, MT, MT, D, ms2)
            dve.wait_ge(rstd2, 1)
            dve.wait_ge(xres_in, 32)
            dve.wait_ge(wr_zero, 1)
            residual(0, mix, diag_ready, g_bc, g_used, res_ready)

            mean_square(sumsq3, 2 * MT, MT, D, ms3)
            dve.wait_ge(rstd3s, 1)
            for m in range(MT):
                ts_(xn[:, m, :], res[:, m, :], rstd[:, m:m + 1], None, ALU.mult).then_inc(xn2, 1)
            for k in range(0, KT, 2):
                dve.wait_ge(tr2, k + 1)
                for c, (lo, hi) in enumerate(SEG):
                    last = ts_(hT[:, k, lo:hi], bank(k % 4, hi - lo, lo), amp[:, 1, k, c:c + 1],
                               mod[:, SHIFT2 * KT + k, c:c + 1], ALU.mult, ALU.add)
                last.then_inc(tr2_v, 1)
            dve.wait_ge(lg_nat, 1)
            lg = PS[:, 5, 0:MT * NE].rearrange("p (m e) -> p m e", e=NE)

            def over_experts(v):
                return v.unsqueeze(2).to_broadcast([P, MT, NE])

            V.tensor_reduce(smx, lg, AX_X, ALU.max)
            dve.drain()
            tt(aff[:, :, :], lg, over_experts(smx), ALU.subtract).then_inc(lg_sub, 1)
            dve.wait_ge(lg_exp, 1)
            dve.drain()
            V.tensor_reduce(smx, aff[:, :, :], AX_X, ALU.add)
            dve.drain()
            V.reciprocal(smx, smx)
            dve.drain()
            tt(aff[:, :, :], aff[:, :, :], over_experts(smx), ALU.mult).then_inc(aff_ready, 1)
            dve.wait_ge(aff_tr, 1)
            V.tensor_copy(wk[0:NE, :], bank(4, T, p1=NE))
            for (lo, hi), cap in zip(SEG, (CAPC, CAPL)):
                for _ in range(cap // 8):
                    dve.drain()
                    V.max(m8[0:NE, :], wk[0:NE, lo:hi])
                    dve.drain()
                    V.match_replace(wk[0:NE, lo:hi], m8[0:NE, :], wk[0:NE, lo:hi], -1.0)
            dve.drain()
            ts_(wk[0:NE, :], wk[0:NE, :], 0.0, None, ALU.is_lt)
            dve.drain()
            for lo, hi in SEG:
                V.tensor_tensor_scan(cum[0:NE, lo:hi], wk[0:NE, lo:hi], wk[0:NE, lo:hi], 0.0, ALU.add, ALU.max)
            dve.drain()
            tt(cum[0:NE, :], cum[0:NE, :], wk[0:NE, :], ALU.mult).then_inc(v_ready, 1)
            dve.wait_ge(v_tr, 1)
            V.tensor_copy(vsel[:, :, :], PS[:, 5, 0:MT * NE].rearrange("p (m e) -> p m e", e=NE))
            dve.drain()
            tt(selC[:, :, :], vsel[:, 0, :].unsqueeze(2).to_broadcast([P, NE, CAPC]),
               slot_no[:, 0:CAPC].unsqueeze(1).to_broadcast([P, NE, CAPC]), ALU.is_equal)
            for t in range(2):
                last = tt(selL[:, t, :, :], vsel[:, 1 + t, :].unsqueeze(2).to_broadcast([P, NE, CAPL]),
                          slot_no.unsqueeze(1).to_broadcast([P, NE, CAPL]), ALU.is_equal)
            V.memset(selG[:, :, :], 0.0)
            dve.drain()
            V.memset(SM[:, 121:122], 0.0).then_inc(sel_ready, 1)

            def gated(m):
                s, o, n = (selC[:, :, :], CAPL, CAPC) if m == 0 else (selL[:, m - 1, :, :], 0, CAPL)
                for u in range(2):
                    last = tt(selG[:, :, 64 * u + o:64 * u + o + n], s,
                              aff[:, m, :].unsqueeze(2).to_broadcast([P, NE, n]), ALU.mult)
                last.then_inc(sg_ready, 1)

            gated(0)
            for k in range(KT):
                dve.wait_ge(gat_l, k + 1)
                ts_(xeT[:, k, :, 0:CAPL], bank(k % 2).rearrange("p (e s) -> p e s", e=NE), amp[:, 1, k, 1:2],
                    mod[:, SHIFT2 * KT + k, 1:2], ALU.mult, ALU.add).then_inc(gat_lv, 1)
            for m in (1, 2):
                dve.wait_ge(sg_tr, 4 * m)
                if m == 1:
                    for u in range(2):
                        V.memset(selG[:, :, 64 * u + CAPL:64 * u + SLOTS], 0.0)
                    dve.drain()
                gated(m)

            dve.wait_ge(facc_zero, 1)
            dve.wait_ge(sg_cp, 12)
            with dve.Fori(0, NE) as e:
                for n in range(2):
                    dve.wait_ge(e_silu, e * 2 + (n + 1))
                    if n:
                        dve.wait_ge(e_htr, e * 2 + 1)
                    tt(h_s[0:SLOTS, :], act_s[0:SLOTS, :], bank(n, p0=64, p1=64 + SLOTS),
                       ALU.mult).then_inc(e_h, 1)
                dve.wait_ge(e_htr, e * 2 + 2)
                V.tensor_copy(hTe[:, :, :], bank(3, HK * SLOTS).rearrange("p (k s) -> p k s", k=HK))\
                    .then_inc(e_hT, 1)
                for i in range(2):
                    for m in range(MT):
                        for u in range(2):
                            n = (i * MT + m) * 2 + u
                            q = slice((2 * i + u) * NC_, (2 * i + u + 1) * NC_)
                            dve.wait_ge(e_sc, e * 12 + (n + 1))
                            tt(facc[:, m, q], facc[:, m, q], bank(4 + n % 4), ALU.add).then_inc(e_acc, 1)
                dve.drain()

            mean_square(sumsq4, MT, MT, D, ms4)
            dve.wait_ge(rstd4, 1)
            dve.wait_ge(wr_zero, 2)
            residual(1, facc, diag2_ready, g2_bc, g2_used, y_ready)


def tables():
    f32 = np.float32
    p = np.arange(P)
    tabs = np.zeros((P, N_TABS), f32)
    tabs[:, T_ID:T_ID + P] = np.eye(P)
    tabs[:, T_SEL2:T_SEL2 + 2] = (p[:, None] % 32) == np.arange(2)
    tabs[:, T_SEL16:T_SEL16 + 16] = (p[:, None] % 32) == np.arange(16)
    tabs[:, T_SLOT:T_SLOT + 32] = np.arange(1, 33)

    def dft(L):
        ang = np.pi * (2 * np.arange(L)[None, :] + 1) * np.arange(L)[:, None] / (2 * L)
        return np.cos(ang), np.sin(ang)

    parts = []
    for inverse in (False, True):
        for L in (TL, TC):
            for t in range(L // P):
                for m in dft(L):
                    m = m.T / L if inverse else m
                    parts.append(m[t * P:(t + 1) * P])
    dft_all = np.concatenate(parts, axis=1).astype(f32)

    def positions(L):
        t = np.linspace(0.0, 1.0, L, dtype=f32)
        bands = (HE - 1) // 2
        w = (f32(TWO_PI) * np.arange(L, dtype=f32) / f32(L)).astype(f32)
        f = np.linspace(1e-4, bands - 1, bands, dtype=f32)
        ang = (w[:, None] * f[None, :]).astype(f32)
        z = np.concatenate([t[:, None], np.cos(ang), -np.sin(ang)], axis=-1).astype(f32)
        lo, hi = math.log(1e-2) / 1.5, math.log(1e-2) / 0.3
        deltas = np.abs(np.linspace(lo, hi, HYW, dtype=f32))
        return z, np.exp(-t[:, None] * deltas[None, :]).astype(f32)

    zc, dc = positions(TC)
    zl, dl = positions(TL)
    zfeat = np.ascontiguousarray(np.concatenate([zc, zl]).T)
    decay = np.concatenate([dc, dl]).reshape(MT, P, HYW)

    half = HD // 2
    inv_freq = f32(10000.0) ** (-np.arange(0, half, 2, dtype=f32) / f32(half))
    n = np.arange(TL, dtype=f32)
    ang = np.concatenate([(np.floor(n / 64))[:, None] * inv_freq[None], (n % 64)[:, None] * inv_freq[None]], 1)
    ang = ang.astype(f32).reshape(TL, 2, 1, half // 2)
    cos = np.broadcast_to(np.cos(ang), (TL, 2, 2, half // 2))
    sin = np.concatenate([np.sin(ang), -np.sin(ang)], axis=2)
    rope = np.stack([cos.reshape(TL, HD), sin.reshape(TL, HD)], 1).reshape(2, P, 2, HD)
    rope = np.ascontiguousarray(rope.transpose(1, 0, 2, 3)).astype(f32)
    return tabs, dft_all, zfeat, decay, rope


def kernel(**inputs):
    import concourse.bacc as bacc
    from concourse.bass_utils import run_bass_kernel_spmd

    a = {k: np.asarray(v) for k, v in inputs.items()}

    def columns(v):
        return np.asarray(v).reshape(-1, P).T

    cols = np.ascontiguousarray(np.concatenate([
        columns(a["c_ctx"]), columns(a["c"]), columns(a["b_ada"]), columns(a["g_pre_mix"]),
        columns(a["g_post_mix"]), columns(a["g_pre_ffn"]), columns(a["g_post_ffn"]),
        columns(a["hy_conv_w"]), columns(a["hy_conv_b"]), columns(a["hy_skip"])], axis=1))
    f_vec = np.ascontiguousarray(np.concatenate([a["hy_f1_b"], a["hy_sin_freq"], a["hy_f2_b"]]).T)
    tabs, dft, zfeat, decay, rope = tables()
    ins = [
        ("x_prompt", a["x_prompt"][0]), ("x_sample", a["x_sample"][0]),
        ("cache_k", a["cache_k_ctx"].reshape(PAST, KVW)), ("cache_v", a["cache_v_ctx"].reshape(PAST, KVW)),
        ("cols", cols), ("w_ada", a["w_ada"][0]), ("w_in", a["w_in"][0]),
        ("qk_g", np.concatenate([a["q_norm_g"], a["k_norm_g"]])), ("w_attn_o", a["w_attn_o"][0]),
        ("f1_w", a["hy_f1_w"][0]), ("f_vec", f_vec), ("f2_w", a["hy_f2_w"][0]), ("f3_w", a["hy_f3_w"][0]),
        ("w_hy_o", a["w_hy_o"][0]), ("w_out", a["w_out"][0]), ("w_router", a["w_router"][0]),
        ("w_gate", a["w_exp_gate"].reshape(NE * D, FF)), ("w_up", a["w_exp_up"].reshape(NE * D, FF)),
        ("w_down", a["w_exp_down"].reshape(NE * FF, D)),
        ("tabs", tabs), ("dft", dft), ("zfeat", zfeat), ("decay", decay), ("rope", rope),
    ]
    outs = [("y_prompt", (TC, D)), ("y_sample", (TL, D)), ("state_k", (TC, KVW)), ("state_v", (TC, KVW))]
    nc = bacc.Bacc("TRN2", target_bir_lowering=False, num_devices=1)
    arrays, args = {}, []
    for name, v in ins:
        arrays[f"in_{name}"] = np.ascontiguousarray(v)
        args.append(nc.dram_tensor(f"in_{name}", v.shape, F32, kind="ExternalInput").ap())
    for name, shape in outs:
        args.append(nc.dram_tensor(f"out_{name}", shape, F32, kind="ExternalOutput").ap())
    build(nc, *args)
    r = run_bass_kernel_spmd(nc, [arrays], core_ids=[0]).results[0]
    return (r["out_y_prompt"].reshape(1, TC, D), r["out_y_sample"].reshape(1, TL, D),
            r["out_state_k"].reshape(1, 1, TC, NKV, HD), r["out_state_v"].reshape(1, 1, TC, NKV, HD))
```

```python
from contextlib import ExitStack
import math

import numpy as np

import concourse.bass as bass
from concourse import mybir

F32 = mybir.dt.float32
ALU = mybir.AluOpType
ACT = mybir.ActivationFunctionType
AX_X = mybir.AxisListType.X
ds = bass.ds

P = 128
D = 2048
KT = D // P
NC_ = 512
HK = 8
TC, TL = 128, 256
T = TC + TL
MT = T // P
SEG = ((0, TC), (TC, T))
NH, NKV, HD = 16, 4, 128
GRP = NH // NKV
KVW = NKV * HD
HYW = D // 2
HYT = HYW // P
PAST = 128
NE = 16
FF = D // 2
CAPC, CAPL = 2 * TC // NE, 2 * TL // NE
SLOTS = CAPC + CAPL
EPS = 1e-6
SCALE = HD ** -0.5
HF = 64
HE = 33
MAGIC = 1.5 * 2.0 ** 23
TWO_PI = 2.0 * math.pi
PI_A = 6.28125
PI_B = float(np.float32(np.round((TWO_PI - PI_A) * 2 ** 20) / 2 ** 20))
PI_C = float(np.float32(TWO_PI - PI_A - PI_B))
PI_IN = 3.1415925

ADA_A = 8
SHIFT1, SCALE1, GATE1, SHIFT2, SCALE2, GATE2 = range(6)

C_COND, C_BADA, C_GPRE1, C_GPOST1, C_GPRE2, C_GPOST2, C_CW, C_CB, C_SKIP = 0, 32, 128, 144, 160, 176, 192, 264, 288
N_COLS = 296
T_ID, T_SEL2, T_SEL16, T_SLOT = 0, 128, 130, 146
N_TABS = 178


def build(nc, x_prompt, x_sample, cache_k, cache_v, cols, w_ada, w_in, qk_g, w_attn_o, f1_w, f_vec, f2_w,
          f3_w, w_hy_o, w_out, w_router, w_gate, w_up, w_down, tabs, dft, zfeat, decay, rope,
          y_prompt, y_sample, state_k, state_v):
    ctx = ExitStack()
    with ctx:
        def sb(name, n):
            return ctx.enter_context(nc.sbuf_tensor(name, [P, n], F32))

        def sem(name):
            return ctx.enter_context(nc.semaphore(name))

        def view(t, off, *dims):
            n = int(np.prod(dims))
            v = t[:, off:off + n]
            if len(dims) == 1:
                return v
            names = "abcd"[:len(dims)]
            return v.rearrange(f"p ({' '.join(names)}) -> p {' '.join(names)}",
                               **{k: d for k, d in zip(names[1:], dims[1:])})

        ring_t = sb("ring", 4 * HK * NC_)
        RA, RB, RC = sb("RA", MT * D), sb("RB", MT * D), sb("RC", MT * D)
        RE, RF, RG = sb("RE", 2 * MT * D), sb("RF", 3072), sb("RG", 2048)
        KC = sb("KC", N_COLS + N_TABS)
        MODS = sb("MODS", 192 + 64 + 64)
        SM = sb("SM", 136)

        ring = view(ring_t, 0, 4, HK, NC_)
        col = KC[:, 0:N_COLS]
        ident = KC[:, N_COLS + T_ID:N_COLS + T_ID + P]
        sel2 = KC[:, N_COLS + T_SEL2:N_COLS + T_SEL2 + 2]
        sel16 = KC[:, N_COLS + T_SEL16:N_COLS + T_SEL16 + 16]
        slot_no = KC[:, N_COLS + T_SLOT:N_COLS + T_SLOT + 32]
        mod = view(MODS, 0, 96, 2)
        amp = view(MODS, 192, 2, KT, 2)
        gout = view(MODS, 256, 2, KT, 2)

        spec = view(RA, 0, 3, 2, HYW)
        rope_t = view(RA, 0, 2, 2, HD)
        rot = view(RA, 512, 2, 2, 2, HD)
        gain_b = view(RA, 1536, 2, HD)
        t_a, t_b = view(RA, 1792, NC_), view(RA, 2304, NC_)
        kT = view(RA, 0, NKV, T + PAST)
        q_st = view(RA, 2048, 2, MT, HD)
        qT = view(RA, 2816, 2, T)
        v_st = view(RA, 3584, 4, HD)
        res = view(RA, 0, MT, D)
        hT = view(RB, 0, KT, T)
        g_rows = view(RB, 0, 2, D)
        scat = view(RB, 0, NE, T)
        xn = view(RC, 0, MT, D)
        Z = view(RC, 0, 3, 2, NC_)
        dft_t = view(RC, 3072, 2560)
        fwd_l, fwd_c = view(RC, 3072, 2, 2, TL), view(RC, 4096, 2, TC)
        inv_l, inv_c = view(RC, 4352, 2, 2, TL), view(RC, 5376, 2, TC)
        oT = view(RC, 0, NH, T)
        mix = view(RC, 0, MT, D)
        facc = view(RC, 0, MT, D)
        hN = view(RE, 0, MT, D)
        dec = view(RE, 6144, MT, HYW)
        f3 = view(RE, 9216, D)
        zf = view(RE, 11264, T)
        f1 = view(RE, 11648, HF)
        f2 = view(RE, 11712, HF)
        fv = view(RE, 11776, 3)
        hyT = view(RE, 0, 3 * HYT, T)
        uN = view(RE, 9216, MT, HYW)
        qkN = view(RE, 0, MT, D + KVW)
        vN = view(RE, 7680, 4, KVW)
        kcN = view(RE, 9728, KVW)
        prob = view(RE, 10240, 2, 2 * 384 + TC)
        sg = view(RE, 0, 2 * KT, T)
        xeT = view(RE, 0, KT, NE, SLOTS)
        g2_rows = view(RE, 0, 2, D)
        ones2 = view(RE, 2 * D, P)
        f_g = view(RE, 2 * D + P, MT, D)
        sq_scr = view(RF, 0, D)
        yhT = view(RF, 0, HYT, T)
        selG = view(RF, 0, NE, P)
        selL = view(RF, 2048, 2, NE, CAPL)
        x_cur = view(RF, 0, KT, SLOTS)
        s_cur = view(RF, 768, T)
        hTe = view(RF, 1152, HK, SLOTS)
        rowbuf = view(RG, 0, NC_)
        condS = view(RG, 512, KT, 32)
        arg, rnd = view(RE, 11792, T), view(RF, 2048, T)
        tmp = view(RG, 1024, NC_)
        probT = view(RG, 1024, 896)
        wr = view(RG, 0, KT, 32)
        ones = view(RG, 512, P)
        diag = view(RF, 2048, 2, NC_)
        lgr = view(RG, 512, T)
        selC = view(RG, 512, NE, CAPC)
        aT, wk, cum = view(RG, 896, T), view(RG, 1280, T), view(RG, 1664, T)
        act_s, h_s = view(RF, 1536, NC_), view(RG, 0, 2, NC_)
        ye = view(RG, 1024, 2, NC_)

        ss = view(SM, 0, 12)
        neghalf = view(SM, 124, 12)
        rstd = view(SM, 24, 12)
        rstd3 = view(SM, 24, MT, 4)
        mx = view(SM, 36, 2, 3)
        nb = view(SM, 42, 2, 3)
        rs = view(SM, 48, 2, 3)
        ri = view(SM, 54, 2, 3)
        aff = view(SM, 60, MT, NE)
        vsel = view(SM, 0, MT, NE)
        smx = view(SM, 108, MT)
        m8 = view(SM, 112, 8)

        PS = ctx.enter_context(nc.psum_tensor("PS", [P, 8, 512], F32))

        def bank(b, n=512, off=0, p0=0, p1=P):
            return PS[p0:p1, b, off:off + n]

        landed = [sem(f"landed{j}") for j in range(4)]
        blocks_used = sem("blocks_used")
        small_in, x_in, filt_in, taps_in, dft_in, qk_in, cache_in, xres_in, wr_in = (
            sem(n) for n in ("small_in", "x_in", "filt_in", "taps_in", "dft_in", "qk_in", "cache_in", "xres_in", "wr_in"))
        out_done = sem("out_done")
        cond_ready, rows_copied, cols_done = sem("cond_ready"), sem("rows_copied"), sem("cols_done")
        sumsq1, ms1, rstd1, xn1 = sem("sumsq1"), sem("ms1"), sem("rstd1"), sem("xn1")
        tr1, tr1_copied = sem("tr1"), sem("tr1_copied")
        f_mm, f_arg, f_sin, f_taps, f_tapmm = (sem(n) for n in ("f_mm", "f_arg", "f_sin", "f_taps", "f_tapmm"))
        f_sumdiff, f_dft, f_spec_a, f_spec_v = (sem(n) for n in ("f_sumdiff", "f_dft", "f_spec_a", "f_spec_v"))
        mod1_read, conv_free, conv_mid = sem("mod1_read"), sem("conv_free"), sem("conv_mid")
        u_ready, u_tr, u_cp, u_dft, z_ready, z_inv, yh_done = (
            sem(n) for n in ("u_ready", "u_tr", "u_cp", "u_dft", "z_ready", "z_inv", "yh_done"))
        qkv_raw, q_ms, q_rstd, qk_done, v_done, rope_done = (
            sem(n) for n in ("qkv_raw", "q_ms", "q_rstd", "qk_done", "v_done", "rope_done"))
        q_staged, v_staged, at_trk, at_kT, at_trq, at_qT, at_s, at_max, at_exp, at_norm, at_trp, at_pa, at_pb, at_o, at_oc = (
            sem(n) for n in ("q_staged", "v_staged", "at_trk", "at_kT", "at_trq", "at_qT", "at_s", "at_max", "at_exp", "at_norm",
                             "at_trp", "at_pa", "at_pb", "at_o", "at_oc"))
        mod2_read, gate_sig, ao_done, ho_done, mod3_read = (
            sem(n) for n in ("mod2_read", "gate_sig", "ao_done", "ho_done", "mod3_read"))
        wo_cp, ms2, rstd2, diag_ready, g_bc, g_used = (
            sem(n) for n in ("wo_cp", "ms2", "rstd2", "diag_ready", "g_bc", "g_used"))
        res_ready, sumsq3, ms3, rstd3s, xn2, tr2, tr2_v, tr2_a = (
            sem(n) for n in ("res_ready", "sumsq3", "ms3", "rstd3s", "xn2", "tr2", "tr2_v", "tr2_a"))
        wr_zero, lg_mm, lg_cp, lg_nat, lg_sub, lg_exp, aff_ready, aff_tr, v_ready, v_tr, sel_ready = (
            sem(n) for n in ("wr_zero", "lg_mm", "lg_cp", "lg_nat", "lg_sub", "lg_exp", "aff_ready", "aff_tr",
                             "v_ready", "v_tr", "sel_ready"))
        gat_l, gat_c, gat_lv, gat_ca = (sem(n) for n in ("gat_l", "gat_c", "gat_lv", "gat_ca"))
        sg_ready, sg_tr, sg_cp = sem("sg_ready"), sem("sg_tr"), sem("sg_cp")
        facc_zero, xe_st, sc_st, e_silu, e_h, e_htr, e_hT, e_yc, e_sc, e_acc = (
            sem(n) for n in ("facc_zero", "xe_st", "sc_st", "e_silu", "e_h", "e_htr", "e_hT", "e_yc", "e_sc",
                             "e_acc"))
        sumsq4, ms4, rstd4, diag2_ready, g2_bc, g2_used, y_ready = (
            sem(n) for n in ("sumsq4", "ms4", "rstd4", "diag2_ready", "g2_bc", "g2_used", "y_ready"))

        B_HY = ADA_A // 2
        B_QKV = B_HY + 6
        B_GA = B_QKV + 6
        B_GB = B_GA + 4
        B_AO = B_GB + 2
        B_HO = B_AO + 2
        B_WO = B_HO + 1
        B_EX = B_WO + 2

        def block(w, h, c):
            return w[h * HK * P:(h + 1) * HK * P, ds(c * NC_, NC_)].rearrange("(k p) n -> p k n", p=P)

        blk = ctx.enter_context(nc.Block())

        @blk.sync
        def _(sp):
            def turn(b, parts):
                for j, (w, h, c) in enumerate(parts):
                    if b is not None:
                        sp.wait_ge(blocks_used, b * 4 + (j - 3))
                    sp.dma_start(ring[:, j], block(w, h, c)).then_inc(landed[j], 16)

            sp.dma_start(zf[0:HE, :], zfeat).then_inc(filt_in, 16)
            sp.dma_start(f1[0:HE, :], f1_w).then_inc(filt_in, 16)
            sp.dma_start(f2[0:HF, :], f2_w).then_inc(filt_in, 16)
            sp.dma_start(fv[0:HF, :], f_vec).then_inc(filt_in, 16)
            sp.dma_start(xn[:, 0, :], x_prompt).then_inc(x_in, 16)
            sp.dma_start(xn[:, 1:3, :], x_sample.rearrange("(m p) d -> p m d", p=P)).then_inc(x_in, 16)
            turn(None, [(w_ada, 0, 0), (w_ada, 1, 0), (w_ada, 0, 4), (w_ada, 1, 4)])
            with sp.Fori(1, ADA_A // 2) as i:
                turn(i, [(w_ada, 0, i), (w_ada, 1, i), (w_ada, 0, i + 4), (w_ada, 1, i + 4)])
            for base, ada0, in0, n in ((B_HY, 8, 6, 6), (B_QKV, 14, 0, 6), (B_GA, 20, 12, 4)):
                with sp.Fori(0, n) as i:
                    turn(i + base, [(w_ada, 0, i + ada0), (w_ada, 1, i + ada0),
                                    (w_in, 0, i + in0), (w_in, 1, i + in0)])
            for base, w, c0 in ((B_GB, w_in, 16), (B_AO, w_attn_o, 0)):
                with sp.Fori(0, 2) as i:
                    turn(i + base, [(w, 0, 2 * i + c0), (w, 1, 2 * i + c0),
                                    (w, 0, 2 * i + (c0 + 1)), (w, 1, 2 * i + (c0 + 1))])
            turn(B_HO, [(w_hy_o, 0, c) for c in range(4)])
            with sp.Fori(0, 2) as i:
                turn(i + B_WO, [(w_out, 0, 2 * i), (w_out, 1, 2 * i),
                                (w_out, 0, 2 * i + 1), (w_out, 1, 2 * i + 1)])
            with sp.Fori(0, NE) as e:
                def rows(w, n_rows, h, c):
                    return w[ds(e * n_rows + h * HK * P, HK * P), c * NC_:(c + 1) * NC_] \
                        .rearrange("(k p) n -> p k n", p=P)
                for n in range(2):
                    for j, (w, h) in enumerate(((w_gate, 0), (w_up, 0), (w_gate, 1), (w_up, 1))):
                        sp.wait_ge(blocks_used, e * 12 + (4 * (B_EX + n) + j - 3))
                        sp.dma_start(ring[:, j], rows(w, D, h, n)).then_inc(landed[j], 16)
                for j in range(4):
                    sp.wait_ge(blocks_used, e * 12 + (4 * (B_EX + 2) + j - 3))
                    sp.dma_start(ring[:, j], rows(w_down, FF, 0, j)).then_inc(landed[j], 16)
            for m in range(MT):
                sp.wait_ge(y_ready, m + 1)
                dst = y_prompt if m == 0 else y_sample[(m - 1) * P:m * P, :]
                sp.dma_start(dst, res[:, m, :]).then_inc(out_done, 16)
            sp.wait_ge(out_done, 16 * (MT + 2))

        @blk.tensor
        def _(pe):
            mm, trp = nc.tensor.matmul, nc.tensor.transpose

            def ada(b, j0, rows_bank):
                for h in range(2):
                    pe.wait_ge(landed[j0 + h], b * 16 + 16)
                    for k in range(HK):
                        kk, g = h * HK + k, k % 4
                        last = mm(bank(rows_bank, p0=32 * g, p1=32 * g + 32), condS[:, kk, :],
                                  ring[:, j0 + h, k, :], start=kk < 4, stop=kk >= KT - 4)
                    last.then_inc(blocks_used, 1)

            def ada_cols(c, which, n=None):
                pe.wait_ge(rows_copied, (c if n is None else n) + 1)
                src = rowbuf if which == 0 else tmp
                for j in range(4):
                    last = mm(PS[:, 6, ds(c * 8 + 2 * j, 2)], src[:, j * P:(j + 1) * P], sel2,
                              start=True, stop=True)
                last.then_inc(cols_done, 1)

            def channels(b, j0, b0, rhs, free=None):
                for h in range(2):
                    pe.wait_ge(landed[j0 + h], b * 16 + 16)
                    for k in range(HK):
                        for c in range(4):
                            if free and h == 0 and k == 0:
                                pe.wait_ge(conv_free, free(c))
                            last = mm(bank(b0 + c, T), ring[:, j0 + h, k, c * P:(c + 1) * P],
                                      rhs[:, h * HK + k, :], start=(h == 0 and k == 0),
                                      stop=(h == 1 and k == HK - 1))
                    last.then_inc(blocks_used, 1)

            def tokens(b, j0, b0, lhs, then=None):
                for h in range(2):
                    pe.wait_ge(landed[j0 + h], b * 16 + 16)
                    for k in range(HK):
                        for m in range(MT):
                            last = mm(bank(b0 + m), lhs[:, h * HK + k, m * P:(m + 1) * P],
                                      ring[:, j0 + h, k, :], start=(h == 0 and k == 0),
                                      stop=(h == 1 and k == HK - 1))
                    last.then_inc(blocks_used, 1)
                    if then:
                        then(h)

            pe.wait_ge(small_in, 32)

            pe.wait_ge(filt_in, 64)
            mm(bank(0, T, p1=HF), f1[0:HE, :], zf[0:HE, :], start=True, stop=True).then_inc(f_mm, 1)
            pe.wait_ge(xn1, MT)
            for k in range(KT):
                if k >= 3:
                    pe.wait_ge(tr1_copied, k - 2)
                for m in range(MT):
                    last = trp(bank(1 + k % 3, P, m * P), xn[:, m, k * P:(k + 1) * P], ident)
                last.then_inc(tr1, 1)
            pe.wait_ge(f_sin, 1)
            mm(bank(4, T, p1=HF), f2[0:HF, :], arg[0:HF, :], start=True, stop=True).then_inc(f_mm, 1)

            def ada_a(i):
                ada(i, 0, 7)
                ada(i, 2, 5)
                if i:
                    pe.wait_ge(mod1_read, i)
                ada_cols(i, 0, 2 * i)
                ada_cols(i + 4, 1, 2 * i + 1)

            pe.wait_ge(cond_ready, 2)
            ada_a(0)
            pe.wait_ge(f_sin, 2)
            pe.wait_ge(taps_in, 48)
            for m in range(MT):
                for c in range(4):
                    n = 4 * m + c
                    if n >= 4:
                        pe.wait_ge(f_taps, n - 3)
                    elif n > 0:
                        pe.wait_ge(tr1_copied, KT)
                    mm(bank(n % 4), arg[0:HF, m * P:(m + 1) * P], f3[0:HF, c * NC_:(c + 1) * NC_],
                       start=True, stop=True).then_inc(f_tapmm, 1)
            ada_a(1)

            pe.wait_ge(dft_in, 16)
            pe.wait_ge(f_taps, 12)
            pe.wait_ge(f_sumdiff, 1)
            n = 0
            for j in range(3):
                for cs in range(2):
                    taps = dec if cs == 0 else hN
                    for half in range(2):
                        if n >= 4:
                            pe.wait_ge(f_spec_a if n % 2 == 0 else f_spec_v, (n - 4) // 2 + 1)
                        hs = slice(half * NC_, (half + 1) * NC_)
                        if j == 0:
                            last = mm(bank(n % 4), fwd_c[:, cs, :], taps[:, 0, hs], start=True, stop=True)
                        else:
                            for t in range(2):
                                last = mm(bank(n % 4), fwd_l[:, t, cs, (j - 1) * P:j * P], taps[:, 1 + t, hs],
                                          start=t == 0, stop=t == 1)
                        last.then_inc(f_dft, 1)
                        n += 1
            ada_a(2)
            ada_a(3)

            with pe.Fori(0, 6) as i:
                ada(i + B_HY, 0, 7)
                channels(i + B_HY, 2, 0, hT, lambda c: i * 4 + (c + 1))
                ada_cols(i + 8, 0)

            pe.wait_ge(conv_free, 28)
            pe.wait_ge(u_ready, 1)
            for n, (m, half) in enumerate((m, half) for half in range(2) for m in range(MT)):
                for c in range(4):
                    last = trp(bank(n, P, c * P), hyT[:, 2 * HYT + half * 4 + c, m * P:(m + 1) * P], ident)
                last.then_inc(u_tr, 1)
            for half in range(2):
                hs = slice(half * NC_, (half + 1) * NC_)
                pe.wait_ge(u_cp, 6)
                if half:
                    pe.wait_ge(z_ready, 3)
                for j in range(3):
                    for cs in range(2):
                        b = 2 * j + cs
                        if j == 0:
                            last = mm(bank(b), fwd_c[:, cs, :], uN[:, 0, hs], start=True, stop=True)
                        else:
                            for t in range(2):
                                last = mm(bank(b), fwd_l[:, t, cs, (j - 1) * P:j * P], uN[:, 1 + t, hs],
                                          start=t == 0, stop=t == 1)
                    last.then_inc(u_dft, 1)
                pe.wait_ge(z_ready, 3 * half + 3)
                for c in range(4):
                    n = 4 * half + c
                    cc = slice(c * P, (c + 1) * P)
                    b = 7 if n % 2 == 0 else 5
                    if n >= 2:
                        pe.wait_ge(yh_done, n - 1)
                    for cs in range(2):
                        mm(bank(b, TC), Z[:, 0, cs, cc], inv_c[:, cs, :], start=cs == 0, stop=cs == 1)
                    for q in range(4):
                        last = mm(bank(b, TL, TC), Z[:, 1 + q // 2, q % 2, cc], inv_l[:, q // 2, q % 2, :],
                                  start=q == 0, stop=q == 3)
                    last.then_inc(z_inv, 1)
                if half == 0:
                    pe.wait_ge(yh_done, 4)

            pe.wait_ge(yh_done, 8)
            with pe.Fori(0, 6) as i:
                ada(i + B_QKV, 0, 7)
                pe.wait_ge(qkv_raw, i * 3 + 3)
                tokens(i + B_QKV, 2, 0, hT)
                ada_cols(i + 14, 0)

            pe.wait_ge(mod2_read, 1)
            pe.wait_ge(cache_in, 32)
            pe.wait_ge(v_done, MT)
            for g in range(NKV):
                for m in range(4):
                    src = kcN[:, g * HD:(g + 1) * HD] if m == 3 else qkN[:, m, D + g * HD:D + (g + 1) * HD]
                    last = trp(bank(g, P, m * P), src, ident)
                last.then_inc(at_trk, 1)

            def queries(h, j):
                pe.wait_ge(q_staged, h + 1)
                for m in range(MT):
                    last = trp(bank(6, P, m * P), q_st[:, j % 2, m, :], ident)
                last.then_inc(at_trq, 1)

            def scores(h, g, j):
                b0, p = 2 * (j % 2), j % 2
                keys = kT[:, ds(g, 1), :].rearrange("p o t -> p (o t)")
                pe.wait_ge(at_qT, h + 1)
                mm(bank(b0, 384), qT[:, p, TC:TC + P], keys[:, TC:], start=True, stop=True)
                mm(bank(b0, TC, 384), qT[:, p, 0:TC], keys[:, 0:TC], start=True, stop=True)
                mm(bank(b0 + 1, 384), qT[:, p, TC + P:T], keys[:, TC:], start=True, stop=True).then_inc(at_s, 1)

            def step(g, j, more):
                h = g * 4 + j
                pe.wait_ge(at_norm, h + 1)
                for kt in range(3):
                    for qt in range(2):
                        o = kt * 256 + qt * P
                        trp(bank(4 + o // 512, P, o % 512),
                            prob[:, j % 2, qt * 384 + kt * P:qt * 384 + (kt + 1) * P], ident)
                trp(bank(5, P, 256), prob[:, j % 2, 768:896], ident).then_inc(at_trp, 1)
                if more or j + 2 < GRP:
                    scores(h + 2, g + (j + 2) // GRP, j)
                if j == 0:
                    pe.wait_ge(v_staged, g + 1)
                pe.wait_ge(at_pa, h + 1)
                pe.wait_ge(at_pb, h + 1)
                mm(bank(7, TC), v_st[:, 0, :], probT[:, 768:896], start=True, stop=True)
                for kt in range(3):
                    last = mm(bank(7, TL, TC), v_st[:, 1 + kt, :], probT[:, kt * 256:(kt + 1) * 256],
                              start=kt == 0, stop=kt == 2)
                last.then_inc(at_o, 1)
                if more or j + 3 < GRP:
                    queries(h + 3, j + 3)

            queries(0, 0)
            pe.wait_ge(at_kT, NKV)
            scores(0, 0, 0)
            queries(1, 1)
            scores(1, 0, 1)
            queries(2, 2)
            with pe.Fori(0, NKV - 1) as g:
                for j in range(GRP):
                    step(g, j, True)
            for j in range(GRP):
                step(NKV - 1, j, False)
            pe.wait_ge(at_oc, NH)

            with pe.Fori(0, 4) as i:
                ada(i + B_GA, 0, 7)
                pe.wait_ge(gate_sig, i * 4 + 1)
                channels(i + B_GA, 2, 0, hT)
                ada_cols(i + 20, 0)
            pe.wait_ge(mod3_read, 1)
            with pe.Fori(0, 2) as i:
                for a in range(2):
                    pe.wait_ge(gate_sig, i * 8 + (17 if a == 0 else 13))
                    channels(i + B_GB, 2 * a, 4 * a, hT)
            pe.wait_ge(gate_sig, 33)
            with pe.Fori(0, 2) as i:
                for a in range(2):
                    pe.wait_ge(ao_done, i * 8 + (4 * a + 1))
                    channels(i + B_AO, 2 * a, 4 * a, oT)
            for c in range(4):
                pe.wait_ge(ao_done, 17)
                if c >= 2:
                    pe.wait_ge(ho_done, 4 * (c - 1))
                pe.wait_ge(landed[c], 16 * (B_HO + 1))
                for k in range(HYT):
                    for j in range(4):
                        last = mm(bank(4 * (c % 2) + j, T), ring[:, c, k, j * P:(j + 1) * P], yhT[:, k, :],
                                  start=k == 0, stop=k == HYT - 1)
                last.then_inc(blocks_used, 1)
            pe.wait_ge(ho_done, 16)

            def broadcast_gates(n0, b0, one, ready, done, used):
                for n in (n0, n0 + 1):
                    pe.wait_ge(ready, n + 1)
                    if n >= 2:
                        pe.wait_ge(used, n - 1)
                    mm(bank(b0 + n % 2), one, diag[:, n % 2, :], start=True, stop=True).then_inc(done, 1)

            for q in range(4):
                pe.wait_ge(wo_cp, 1 + 3 * max(q - 1, 0))
                tokens(B_WO + q // 2, 2 * (q % 2), 3 * (q % 2), sg,
                       (lambda h: broadcast_gates(4 * q + 2 * h, 6, ones, diag_ready, g_bc, g_used))
                       if q < 2 else None)

            pe.wait_ge(xn2, MT)
            for k in range(KT):
                if k >= 4:
                    pe.wait_ge(tr2_v if k % 2 == 0 else tr2_a, k // 2 - 1)
                for m in range(MT):
                    last = trp(bank(k % 4, P, m * P), xn[:, m, k * P:(k + 1) * P], ident)
                last.then_inc(tr2, 1)
            pe.wait_ge(wr_in, 16)
            pe.wait_ge(tr2_v, KT // 2)
            pe.wait_ge(tr2_a, KT // 2)
            for k in range(KT):
                g = k % 4
                last = mm(bank(4, T, p0=32 * g, p1=32 * g + 32), wr[:, k, :], hT[:, k, :],
                          start=k < 4, stop=k >= KT - 4)
            last.then_inc(lg_mm, 1)
            pe.wait_ge(lg_cp, 1)
            for m in range(MT):
                last = mm(bank(5, NE, m * NE), lgr[:, m * P:(m + 1) * P], sel16, start=True, stop=True)
            last.then_inc(lg_nat, 1)
            pe.wait_ge(aff_ready, 1)
            for m in range(MT):
                last = trp(bank(4, P, m * P, p1=NE), aff[:, m, :], ident)
            last.then_inc(aff_tr, 1)
            pe.wait_ge(v_ready, 1)
            for m in range(MT):
                last = trp(bank(5, NE, m * NE), cum[0:NE, m * P:(m + 1) * P], ident[0:NE, 0:NE])
            last.then_inc(v_tr, 1)
            pe.wait_ge(sel_ready, 1)
            for k in range(KT):
                if k >= 2:
                    pe.wait_ge(gat_lv, k - 1)
                    pe.wait_ge(gat_ca, k - 1)
                kk = slice(k * P, (k + 1) * P)
                mm(bank(2 + k % 2, NE * CAPC), xn[:, 0, kk], selC[:, :, :], start=True,
                   stop=True).then_inc(gat_c, 1)
                for t in range(2):
                    last = mm(bank(k % 2), xn[:, 1 + t, kk], selL[:, t, :, :], start=t == 0, stop=t == 1)
                last.then_inc(gat_l, 1)
            for m in range(MT):
                pe.wait_ge(sg_ready, m + 1)
                for q in range(4):
                    n = 4 * m + q
                    if n >= 4:
                        pe.wait_ge(sg_cp, n - 3)
                    for j in range(4):
                        last = trp(bank(4 + n % 4, P, j * P), selG[:, 4 * q + j, :], ident)
                    last.then_inc(sg_tr, 1)
            pe.wait_ge(sg_cp, 12)

            pe.wait_ge(gat_lv, KT)
            pe.wait_ge(gat_ca, KT)
            pe.wait_ge(facc_zero, 1)

            def scatter(base, i, m, t):
                if m == 0:
                    pe.wait_ge(e_yc, base * 2 + (i + 1))
                for u in range(2):
                    n = 2 * t + u
                    pe.wait_ge(e_acc, base * 12 + (n + 1))
                    mm(bank(4 + n % 4), s_cur[64 * u:64 * u + SLOTS, m * P:(m + 1) * P],
                       ye[64 * u:64 * u + SLOTS, i, :], start=True, stop=True).then_inc(e_sc, 1)

            def expert(e, last_one):
                pe.wait_ge(xe_st, e + 1)
                pe.wait_ge(sc_st, e + 1)
                for n in range(2):
                    for h in range(2):
                        pe.wait_ge(landed[2 * h], e * 48 + 16 * (B_EX + n + 1))
                        pe.wait_ge(landed[2 * h + 1], e * 48 + 16 * (B_EX + n + 1))
                        for k in range(HK):
                            for u in range(2):
                                last = mm(bank(n, p0=64 * u, p1=64 * u + SLOTS), x_cur[:, h * HK + k, :],
                                          ring[:, 2 * h + u, k, :], start=(h == 0 and k == 0),
                                          stop=(h == 1 and k == HK - 1))
                                if k == HK - 1:
                                    last.then_inc(blocks_used, 1)
                        t = 2 * n + h
                        scatter(e, t // MT, t % MT, t)
                for n in range(2):
                    if n == 1:
                        scatter(e, 1, 1, 4)
                        scatter(e, 1, 2, 5)
                    pe.wait_ge(e_h, e * 2 + (n + 1))
                    for j in range(4):
                        o, src, i_ = bank(2 + n, SLOTS, j * SLOTS), h_s[0:SLOTS, n, j * P:(j + 1) * P], \
                            ident[0:SLOTS, 0:SLOTS]
                        last = mm(o, src, i_, start=True, stop=True) if j == 0 else trp(o, src, i_)
                    last.then_inc(e_htr, 1)
                pe.wait_ge(e_hT, e * 2 + 1)
                for i in range(2):
                    pe.wait_ge(landed[2 * i], e * 48 + 16 * (B_EX + 3))
                    pe.wait_ge(landed[2 * i + 1], e * 48 + 16 * (B_EX + 3))
                    for k in range(HK):
                        if i == 0 and k == HK // 2:
                            pe.wait_ge(e_hT, e * 2 + 2)
                        if last_one and k % 4 == 0:
                            broadcast_gates(4 * i + k // 2, 0, ones2, diag2_ready, g2_bc, g2_used)
                        for u in range(2):
                            last = mm(bank(2 + i, p0=64 * u, p1=64 * u + SLOTS), hTe[:, k, :],
                                      ring[:, 2 * i + u, k, :], start=k == 0, stop=k == HK - 1)
                            if k == HK - 1:
                                last.then_inc(blocks_used, 1)

            with pe.Fori(0, NE - 1) as e:
                expert(e, False)
            expert(NE - 1, True)
            pe.wait_ge(sc_st, NE + 1)
            for t in range(2 * MT):
                scatter(NE, t % 2, t // 2, t)

        @blk.scalar
        def _(act):
            A = nc.scalar.activation
            act.dma_start(col, cols).then_inc(small_in, 16)
            act.dma_start(KC[:, N_COLS:N_COLS + N_TABS], tabs).then_inc(small_in, 16)

            act.wait_ge(small_in, 32)
            act.wait_ge(cond_ready, 1)
            A(condS[:, :, 0:2], col[:, C_COND:C_COND + 32].rearrange("p (c k) -> p k c", c=2),
              ACT.Silu).then_inc(cond_ready, 1)
            act.wait_ge(x_in, 32)
            act.dma_start(f3[0:HF, :], f3_w).then_inc(taps_in, 16)
            act.dma_start(dec[:, 0, :], decay[0]).then_inc(taps_in, 16)
            act.dma_start(dec[:, 1:3, :], decay[1:3].rearrange("m p d -> p m d")).then_inc(taps_in, 16)
            for m in range(MT):
                A(sq_scr, xn[:, m, :], ACT.Square, accum_out=ss[:, m:m + 1]).then_inc(sumsq1, 1)
                act.drain()
            act.wait_ge(f_arg, 1)
            A(arg[0:HF, :], arg[0:HF, :], ACT.Sin).then_inc(f_sin, 1)
            act.wait_ge(f_arg, 2)
            A(arg[0:HF, :], arg[0:HF, :], ACT.Sin).then_inc(f_sin, 1)
            act.wait_ge(tr1, KT)
            act.dma_start(dft_t, dft).then_inc(dft_in, 16)

            def rows(used, src_bank, dst):
                act.wait_ge(blocks_used, used)
                A(dst, bank(src_bank), ACT.Copy).then_inc(rows_copied, 1)

            for i in range(ADA_A // 2):
                if i:
                    act.wait_ge(cols_done, i * 2)
                if i == 2:
                    for n in range(0, 12, 2):
                        act.wait_ge(f_dft, n + 1)
                        A(spec[:, n // 4, (n // 2) % 2, 0:NC_], bank(n % 4), ACT.Copy).then_inc(f_spec_a, 1)
                rows(i * 4 + 2, 7, rowbuf)
                rows(i * 4 + 4, 5, tmp)

            with act.Fori(0, 6) as i:
                act.wait_ge(cols_done, i + 8)
                rows(i * 4 + (4 * B_HY + 2), 7, rowbuf)
                act.wait_ge(blocks_used, i * 4 + (4 * B_HY + 4))
                for j in range(4):
                    A(hyT[:, ds(i * 4 + j, 1), :], bank(j, T), ACT.Identity,
                      bias=col[:, ds(i * 4 + (C_CB + j), 1)],
                      scale=col[:, ds(i * 4 + (C_CW + 24 + j), 1)]).then_inc(conv_mid, 1)

            for n in range(0, 6, 2):
                act.wait_ge(u_tr, n + 1)
                half, m = n // MT, n % MT
                A(uN[:, m, half * NC_:(half + 1) * NC_], bank(n), ACT.Copy).then_inc(u_cp, 1)

            act.wait_ge(z_ready, 6)
            act.dma_start(rope_t[:, :, :, :], rope).then_inc(qk_in, 16)
            act.dma_start(gain_b, qk_g.rearrange("(o a) d -> o (a d)", o=1).to_broadcast([P, 2 * HD])
                          .rearrange("p (a d) -> p a d", a=2)).then_inc(qk_in, 16)
            act.wait_ge(yh_done, 8)
            act.dma_start(kcN, cache_k).then_inc(cache_in, 16)
            act.dma_start(vN[:, 3, :], cache_v).then_inc(cache_in, 16)
            act.wait_ge(yh_done, 8)
            act.nop().then_inc(qkv_raw, 3)
            with act.Fori(0, 5) as i:
                act.wait_ge(cols_done, i + 14)
                rows(i * 4 + (4 * B_QKV + 2), 7, rowbuf)
                act.wait_ge(blocks_used, i * 4 + (4 * B_QKV + 4))
                for m in range(MT):
                    A(qkN[:, m, ds(i * NC_, NC_)], bank(m), ACT.Copy).then_inc(qkv_raw, 1)
            act.wait_ge(cols_done, 19)
            rows(4 * B_QKV + 22, 7, rowbuf)
            act.wait_ge(blocks_used, 4 * B_QKV + 24)
            for m in range(MT):
                A(vN[:, m, :], bank(m), ACT.Copy).then_inc(v_done, 1)
            act.wait_ge(v_done, MT)
            act.dma_start(state_v, vN[:, 0, :]).then_inc(out_done, 16)
            act.wait_ge(qk_done, 5)
            act.dma_start(state_k, qkN[:, 0, D:D + KVW]).then_inc(out_done, 16)

            for g in range(0, NKV, 2):
                act.wait_ge(at_trk, g + 1)
                A(kT[:, g, :], bank(g), ACT.Copy).then_inc(at_kT, 1)

            def queries(h, j):
                act.wait_ge(at_trq, h + 1)
                A(qT[:, j % 2, :], bank(6, T), ACT.Copy).then_inc(at_qT, 1)

            def exponentials(h, j):
                p = j % 2
                act.wait_ge(at_max, h + 1)
                for t, (lo, hi) in enumerate(((0, 384), (384, 768), (768, 896))):
                    src = (bank(2 * p, 384), bank(2 * p + 1, 384), bank(2 * p, TC, 384))[t]
                    A(prob[:, p, lo:hi], src, ACT.Exp, bias=nb[:, p, t:t + 1], scale=SCALE,
                      accum_out=rs[:, p, t:t + 1])
                act.drain()
                act.nop().then_inc(at_exp, 1)

            def step(g, j, more):
                h = g * 4 + j
                act.wait_ge(at_trp, h + 1)
                A(probT[:, 0:512], bank(4), ACT.Copy).then_inc(at_pa, 1)
                if more or j + 1 < GRP:
                    exponentials(h + 1, j + 1)
                act.wait_ge(at_o, h + 1)
                A(oT[:, ds(h, 1), :], bank(7, T), ACT.Copy).then_inc(at_oc, 1)
                if more or j + 3 < GRP:
                    queries(h + 3, j + 3)

            queries(0, 0)
            queries(1, 1)
            exponentials(0, 0)
            queries(2, 2)
            with act.Fori(0, NKV - 1) as g:
                for j in range(GRP):
                    step(g, j, True)
            for j in range(GRP):
                step(NKV - 1, j, False)

            act.wait_ge(at_oc, NH)
            act.dma_start(res[:, 0, :], x_prompt).then_inc(xres_in, 16)
            act.dma_start(res[:, 1:3, :], x_sample.rearrange("(m p) d -> p m d", p=P)).then_inc(xres_in, 16)

            act.wait_ge(out_done, 32)
            act.nop().then_inc(gate_sig, 1)
            with act.Fori(0, 4) as i:
                act.wait_ge(cols_done, i + 20)
                rows(i * 4 + (4 * B_GA + 2), 7, rowbuf)
                act.wait_ge(blocks_used, i * 4 + (4 * B_GA + 4))
                for j in range(4):
                    A(sg[:, ds(i * 4 + j, 1), :], bank(j, T), ACT.Sigmoid).then_inc(gate_sig, 1)
            with act.Fori(0, 2) as i:
                for a in range(2):
                    act.wait_ge(blocks_used, i * 4 + (4 * B_GB + 2 * a + 2))
                    for j in range(4):
                        A(sg[:, ds(i * 8 + (16 + 4 * a + j), 1), :], bank(4 * a + j, T),
                          ACT.Sigmoid).then_inc(gate_sig, 1)

            act.wait_ge(ho_done, 16)
            act.nop().then_inc(wo_cp, 1)
            for q in range(4):
                act.wait_ge(blocks_used, 4 * B_WO + 2 * q + 2)
                for m in range(MT):
                    A(sq_scr[:, 0:NC_], bank(3 * (q % 2) + m), ACT.Square,
                      accum_out=ss[:, 4 * m + q:4 * m + q + 1]).then_inc(sumsq3, 1)
                    A(mix[:, m, q * NC_:(q + 1) * NC_], bank(3 * (q % 2) + m), ACT.Copy).then_inc(wo_cp, 1)
                    act.drain()
            act.wait_ge(rstd2, 1)
            for m in range(MT):
                act.wait_ge(res_ready, m + 1)
                A(sq_scr, res[:, m, :], ACT.Square, accum_out=ss[:, m:m + 1]).then_inc(sumsq3, 1)
                act.drain()
            for k in range(1, KT, 2):
                act.wait_ge(tr2, k + 1)
                for c, (lo, hi) in enumerate(SEG):
                    last = A(hT[:, k, lo:hi], bank(k % 4, hi - lo, lo), ACT.Identity,
                             bias=mod[:, SHIFT2 * KT + k, c:c + 1], scale=amp[:, 1, k, c:c + 1])
                last.then_inc(tr2_a, 1)
            act.wait_ge(lg_mm, 1)
            A(lgr, bank(4, T), ACT.Copy).then_inc(lg_cp, 1)
            act.wait_ge(lg_sub, 1)
            A(aff[:, :, :], aff[:, :, :], ACT.Exp).then_inc(lg_exp, 1)
            for k in range(KT):
                act.wait_ge(gat_c, k + 1)
                A(xeT[:, k, :, CAPL:SLOTS], bank(2 + k % 2, NE * CAPC).rearrange("p (e s) -> p e s", e=NE),
                  ACT.Identity, bias=mod[:, SHIFT2 * KT + k, 0:1], scale=amp[:, 1, k, 0:1]).then_inc(gat_ca, 1)
            act.wait_ge(lg_nat, 1)
            for n in range(12):
                act.wait_ge(sg_tr, n + 1)
                m, q = n // 4, n % 4
                A(scat[:, 4 * q:4 * q + 4, m * P:(m + 1) * P],
                  bank(4 + n % 4).rearrange("p (j t) -> p j t", j=4), ACT.Copy).then_inc(sg_cp, 1)

            act.wait_ge(v_tr, 1)
            with act.Fori(0, NE) as e:
                for n in range(2):
                    act.wait_ge(blocks_used, e * 12 + (4 * (B_EX + n) + 4))
                    if n:
                        act.wait_ge(e_h, e * 2 + 1)
                    A(act_s[0:SLOTS, :], bank(n, p1=SLOTS), ACT.Silu).then_inc(e_silu, 1)
                for i in range(2):
                    act.wait_ge(blocks_used, e * 12 + (4 * (B_EX + 2) + 2 * i + 2))
                    for u in range(2):
                        last = A(ye[64 * u:64 * u + SLOTS, i, :], bank(2 + i, p0=64 * u, p1=64 * u + SLOTS),
                                 ACT.Copy)
                    last.then_inc(e_yc, 1)
            for n in range(4 * MT):
                act.wait_ge(e_acc, 12 * NE + 4 + n + 1)
                m, q = n // 4, n % 4
                A(act_s, facc[:, m, q * NC_:(q + 1) * NC_], ACT.Square,
                  accum_out=ss[:, n:n + 1]).then_inc(sumsq4, 1)
                act.drain()

        @blk.gpsimd
        def _(pool):
            g_ = nc.gpsimd
            g_.memset(condS[:, :, :], 0.0).then_inc(cond_ready, 1)
            g_.memset(neghalf, -0.5)
            pool.drain()

            def inv_root(src_sem, n, cols_, done):
                pool.wait_ge(src_sem, n)
                g_.tensor_tensor(rstd[:, 0:cols_], ss[:, 0:cols_], neghalf[:, 0:cols_],
                                 ALU.pow).then_inc(done, 1)

            inv_root(ms1, 1, MT, rstd1)
            with pool.Fori(0, 5) as i:
                pool.wait_ge(q_ms, i + 1)
                g_.tensor_tensor(rstd, ss, neghalf, ALU.pow).then_inc(q_rstd, 1)
            pool.wait_ge(qk_done, 5)
            pool.wait_ge(v_done, MT)
            pool.wait_ge(cache_in, 32)

            def queries(h, j, wait=True):
                if wait:
                    pool.wait_ge(at_trq, h - 1)
                g_.tensor_copy(q_st[:, j % 2, :, :], qkN[:, :, ds(h * HD, HD)]).then_inc(q_staged, 1)

            def values(g, wait=True):
                if wait:
                    pool.wait_ge(at_o, g * 4)
                g_.tensor_copy(v_st[:, :, :], vN[:, :, ds(g * HD, HD)]).then_inc(v_staged, 1)

            for h in range(GRP):
                queries(h, h, h >= 2)
            values(0, False)
            for j in range(GRP):
                queries(4 + j, j)
            with pool.Fori(1, NKV - 1) as g:
                values(g)
                for j in range(GRP):
                    queries(g * 4 + (4 + j), j)
            values(NKV - 1)
            pool.wait_ge(mod3_read, 1)
            g_.memset(wr[:, :, :], 0.0)
            g_.memset(ones, 1.0).then_inc(wr_zero, 1)
            pool.wait_ge(wr_zero, 1)
            pool.dma_start(wr[:, :, 0:NE], w_router.rearrange("(k p) e -> p k e", p=P)).then_inc(wr_in, 16)
            inv_root(ms2, 1, MT, rstd2)
            inv_root(ms3, 1, MT, rstd3s)
            pool.wait_ge(gat_lv, KT)
            pool.wait_ge(gat_ca, KT)
            g_.memset(facc[:, :, :], 0.0)
            pool.wait_ge(sg_cp, 12)
            g_.memset(s_cur, 0.0).then_inc(facc_zero, 1)
            g_.memset(ye[:, :, :], 0.0).then_inc(e_yc, 2)
            pool.wait_ge(facc_zero, 1)
            g_.memset(SM[:, 120:121], 0.0).then_inc(sc_st, 1)
            g_.tensor_copy(x_cur[:, :, :], xeT[:, :, 0:1, :].rearrange("p k o s -> p k (o s)")).then_inc(xe_st, 1)

            def scatter_matrix(e):
                pool.wait_ge(e_sc, e * 12 + 12)
                g_.tensor_copy(s_cur, scat[:, ds(e, 1), :].rearrange("p o t -> p (o t)")).then_inc(sc_st, 1)

            with pool.Fori(0, NE - 1) as e:
                scatter_matrix(e)
                pool.wait_ge(blocks_used, e * 12 + (4 * (B_EX + 2)))
                g_.tensor_copy(x_cur[:, :, :], xeT[:, :, ds(e + 1, 1), :].rearrange("p k o s -> p k (o s)"))\
                    .then_inc(xe_st, 1)
            pool.drain()
            g_.memset(ones2, 1.0).then_inc(wr_zero, 1)
            scatter_matrix(NE - 1)
            for m in range(MT):
                pool.wait_ge(ms4, m + 1)
                g_.tensor_tensor(rstd[:, m:m + 1], smx[:, m:m + 1], neghalf[:, m:m + 1],
                                 ALU.pow).then_inc(rstd4, 1)

        @blk.vector
        def _(dve):
            V = nc.vector
            ts_, tt, stt = V.tensor_scalar, V.tensor_tensor, V.scalar_tensor_tensor

            def mean_square(sem_in, n_in, cols_, width, done):
                dve.wait_ge(sem_in, n_in)
                ts_(ss[:, 0:cols_], ss[:, 0:cols_], 1.0 / width, EPS, ALU.mult, ALU.add).then_inc(done, 1)

            def sine_argument(src_bank, bias, n):
                dve.wait_ge(f_mm, n)
                a, r = arg[0:HF, :], rnd[0:HF, :]
                ts_(a, bank(src_bank, T, p1=HF), bias, fv[0:HF, 1:2], ALU.add, ALU.mult)
                dve.drain()
                ts_(r, a, 1.0 / TWO_PI, MAGIC, ALU.mult, ALU.add)
                dve.drain()
                ts_(r, r, MAGIC, None, ALU.subtract)
                for part in (PI_A, PI_B, PI_C):
                    dve.drain()
                    stt(out=a, in0=r, scalar=-part, in1=a, op0=ALU.mult, op1=ALU.add)
                dve.drain()
                ts_(a, a, PI_IN, -PI_IN, ALU.min, ALU.max).then_inc(f_arg, 1)

            dve.wait_ge(filt_in, 64)
            sine_argument(0, fv[0:HF, 0:1], 1)
            mean_square(sumsq1, MT, MT, D, ms1)
            dve.wait_ge(rstd1, 1)
            for m in range(MT):
                ts_(xn[:, m, :], xn[:, m, :], rstd[:, m:m + 1], None, ALU.mult).then_inc(xn1, 1)
            for k in range(KT):
                dve.wait_ge(tr1, k + 1)
                V.tensor_copy(hT[:, k, :], bank(1 + k % 3, T)).then_inc(tr1_copied, 1)
            sine_argument(4, fv[0:HF, 2:3], 2)
            def read_mods(lo, hi, n):
                dve.wait_ge(cols_done, n)
                tt(mod[:, lo:hi, :], PS[:, 6, 2 * lo:2 * hi].rearrange("p (a c) -> p a c", c=2),
                   col[:, C_BADA + lo:C_BADA + hi].unsqueeze(2).to_broadcast([P, hi - lo, 2]), ALU.add)
                dve.drain()

            def gains(dst, part, gain, add):
                stt(out=dst, in0=mod[:, part * KT:(part + 1) * KT, :], scalar=add,
                    in1=col[:, gain:gain + KT].unsqueeze(2).to_broadcast([P, KT, 2]), op0=ALU.add, op1=ALU.mult)

            def modulate_a(i):
                dve.wait_ge(cols_done, 2 * i + 2)
                for part in (SHIFT1, SCALE1):
                    lo = part * KT + 4 * i
                    last = tt(mod[:, lo:lo + 4, :], PS[:, 6, 2 * lo:2 * lo + 8].rearrange("p (a c) -> p a c", c=2),
                              col[:, C_BADA + lo:C_BADA + lo + 4].unsqueeze(2).to_broadcast([P, 4, 2]), ALU.add)
                last.then_inc(mod1_read, 1)
                dve.drain()
                stt(out=amp[:, 0, 4 * i:4 * i + 4, :], in0=mod[:, SCALE1 * KT + 4 * i:SCALE1 * KT + 4 * i + 4, :],
                    scalar=1.0, in1=col[:, C_GPRE1 + 4 * i:C_GPRE1 + 4 * i + 4].unsqueeze(2).to_broadcast([P, 4, 2]),
                    op0=ALU.add, op1=ALU.mult)
                dve.drain()
                for k in range(4 * i, 4 * i + 4):
                    for c, (lo, hi) in enumerate(SEG):
                        ts_(hT[:, k, lo:hi], hT[:, k, lo:hi], amp[:, 0, k, c:c + 1],
                            mod[:, SHIFT1 * KT + k, c:c + 1], ALU.mult, ALU.add)

            modulate_a(0)
            dve.wait_ge(taps_in, 48)
            for n in range(12):
                m, c = n // 4, n % 4
                dve.wait_ge(f_tapmm, n + 1)
                tt(hN[:, m, c * NC_:(c + 1) * NC_], bank(n % 4), dec[:, m, (c % 2) * NC_:(c % 2 + 1) * NC_],
                   ALU.mult).then_inc(f_taps, 1)
            dve.drain()
            V.memset(hN[0:1, 0, HYW:D], 0.0)
            V.memset(hN[0:1, 1, HYW:D], 0.0)
            dve.drain()
            tt(dec[:, :, :], hN[:, :, 0:HYW], hN[:, :, HYW:D], ALU.add)
            dve.drain()
            tt(hN[:, :, 0:HYW], hN[:, :, 0:HYW], hN[:, :, HYW:D], ALU.subtract).then_inc(f_sumdiff, 1)
            modulate_a(1)
            for n in range(1, 12, 2):
                dve.wait_ge(f_dft, n + 1)
                V.tensor_copy(spec[:, n // 4, (n // 2) % 2, NC_:2 * NC_], bank(n % 4)).then_inc(f_spec_v, 1)

            modulate_a(2)
            modulate_a(3)
            dve.drain()
            dve.wait_ge(f_spec_a, 6)
            V.memset(SM[:, 121:122], 0.0).then_inc(conv_free, 4)

            with dve.Fori(0, 6) as i:
                for j in range(4):
                    dve.wait_ge(conv_mid, i * 4 + (j + 1))
                    for tap in range(2):
                        w = col[:, ds(i * 4 + (C_CW + 48 * tap + j), 1)]
                        for lo, hi in SEG:
                            a, b = (lo + 1, hi) if tap == 0 else (lo, hi - 1)
                            o = -1 if tap == 0 else 1
                            last = stt(out=hyT[:, ds(i * 4 + j, 1), a:b].rearrange("p o t -> p (o t)"),
                                       in0=bank(j, b - a, a + o), scalar=w,
                                       in1=hyT[:, ds(i * 4 + j, 1), a:b].rearrange("p o t -> p (o t)"),
                                       op0=ALU.mult, op1=ALU.add)
                        if tap == 0:
                            dve.drain()
                    last.then_inc(conv_free, 1)
            dve.drain()
            tt(hyT[:, 2 * HYT:3 * HYT, :], hyT[:, 2 * HYT:3 * HYT, :], hyT[:, HYT:2 * HYT, :],
               ALU.mult).then_inc(u_ready, 1)
            for n in range(1, 6, 2):
                dve.wait_ge(u_tr, n + 1)
                half, m = n // MT, n % MT
                V.tensor_copy(uN[:, m, half * NC_:(half + 1) * NC_], bank(n)).then_inc(u_cp, 1)
            for half in range(2):
                hs = slice(half * NC_, (half + 1) * NC_)
                for j in range(3):
                    dve.wait_ge(u_dft, 3 * half + j + 1)
                    if half and j == 0:
                        dve.wait_ge(z_inv, 4)
                    hc, hsn = spec[:, j, 0, hs], spec[:, j, 1, hs]
                    uc, us = bank(2 * j), bank(2 * j + 1)
                    dve.drain()
                    tt(Z[:, j, 0, :], uc, hc, ALU.mult)
                    tt(tmp, us, hsn, ALU.mult)
                    tt(Z[:, j, 1, :], uc, hsn, ALU.mult)
                    dve.drain()
                    tt(Z[:, j, 0, :], Z[:, j, 0, :], tmp, ALU.subtract)
                    dve.drain()
                    tt(tmp, us, hc, ALU.mult)
                    dve.drain()
                    tt(Z[:, j, 1, :], Z[:, j, 1, :], tmp, ALU.add).then_inc(z_ready, 1)
                for c in range(4):
                    n = 4 * half + c
                    dve.wait_ge(z_inv, n + 1)
                    dve.drain()
                    stt(out=tmp[:, 0:T], in0=hyT[:, 2 * HYT + n, :], scalar=col[:, C_SKIP + n:C_SKIP + n + 1],
                        in1=bank(7 if n % 2 == 0 else 5, T), op0=ALU.mult, op1=ALU.add)
                    dve.drain()
                    tt(yhT[:, n, :], tmp[:, 0:T], hyT[:, n, :], ALU.mult).then_inc(yh_done, 1)

            dve.wait_ge(qk_in, 32)
            for a in range(2):
                for m in range(2):
                    tt(rot[:, a, m, :, :], rope_t[:, m, :, :],
                       gain_b[:, a, :].unsqueeze(1).to_broadcast([P, 2, HD]), ALU.mult)
            dve.drain()

            def qk_norm(i, x, a):
                for m in range(MT):
                    dve.drain()
                    dve.wait_ge(qkv_raw, i * 3 + (m + 4))
                    tt(t_a, x(m), x(m), ALU.mult)
                    dve.drain()
                    V.tensor_reduce(ss[:, 4 * m:4 * m + 4], t_a.rearrange("p (h d) -> p h d", h=4), AX_X, ALU.add)
                dve.drain()
                ts_(ss, ss, 1.0 / HD, EPS, ALU.mult, ALU.add).then_inc(q_ms, 1)
                dve.wait_ge(q_rstd, i + 1)
                for m in range(MT):
                    xh = x(m).rearrange("p (h d) -> p h d", h=4)
                    tah, tbh = (t.rearrange("p (h d) -> p h d", h=4) for t in (t_a, t_b))
                    if m:
                        dve.drain()
                    tt(xh, xh, rstd[:, 4 * m:4 * m + 4].unsqueeze(2).to_broadcast([P, 4, HD]), ALU.mult)
                    dve.drain()
                    if m == 0:
                        tt(xh, xh, gain_b[:, a, :].unsqueeze(1).to_broadcast([P, 4, HD]), ALU.mult)
                        continue
                    own = rot[:, a, m - 1, 0, :].unsqueeze(1).to_broadcast([P, 4, HD])
                    other = rot[:, a, m - 1, 1, :].unsqueeze(1).to_broadcast([P, 4, HD])
                    tt(tah, xh, own, ALU.mult)
                    tt(tbh, xh, other, ALU.mult)
                    dve.drain()
                    x4 = x(m).rearrange("p (g s d) -> p g s d", s=2, d=32)
                    a4, b4 = (t.rearrange("p (g s d) -> p g s d", s=2, d=32) for t in (t_a, t_b))
                    for s in range(2):
                        tt(x4[:, :, s, :], a4[:, :, s, :], b4[:, :, 1 - s, :], ALU.add)
                dve.drain()
                V.memset(SM[:, 121:122], 0.0).then_inc(qk_done, 1)
                dve.drain()

            with dve.Fori(0, 4) as i:
                qk_norm(i, lambda m: qkN[:, m, ds(i * NC_, NC_)], 0)
            qk_norm(4, lambda m: qkN[:, m, D:D + KVW], 1)
            read_mods(32, 80, 20)
            gains(amp[:, 1], SCALE2, C_GPRE2, 1.0)
            gains(gout[:, 0], GATE1, C_GPOST1, 0.0)
            dve.drain()
            V.memset(SM[:, 121:122], 0.0).then_inc(mod2_read, 1)

            for g in range(1, NKV, 2):
                dve.wait_ge(at_trk, g + 1)
                V.tensor_copy(kT[:, g, :], bank(g)).then_inc(at_kT, 1)

            def maxima(h, j):
                p = j % 2
                dve.wait_ge(at_s, h + 1)
                V.reduce_max(mx[:, p, 0:1], bank(2 * p, 384), AX_X)
                V.reduce_max(mx[:, p, 1:2], bank(2 * p + 1, 384), AX_X)
                V.reduce_max(mx[:, p, 2:3], bank(2 * p, TC, 384), AX_X)
                dve.drain()
                ts_(nb[:, p, :], mx[:, p, :], -SCALE, None, ALU.mult).then_inc(at_max, 1)

            def normalise(h, j):
                p = j % 2
                dve.wait_ge(at_exp, h + 1)
                V.reciprocal(ri[:, p, :], rs[:, p, :])
                dve.drain()
                for t, (lo, hi) in enumerate(((0, 384), (384, 768), (768, 896))):
                    last = ts_(prob[:, p, lo:hi], prob[:, p, lo:hi], ri[:, p, t:t + 1], None, ALU.mult)
                last.then_inc(at_norm, 1)

            def step(g, j, more):
                h = g * 4 + j
                dve.wait_ge(at_trp, h + 1)
                V.tensor_copy(probT[:, 512:896], bank(5, 384)).then_inc(at_pb, 1)
                if more or j + 2 < GRP:
                    maxima(h + 2, j)
                if more or j + 1 < GRP:
                    normalise(h + 1, j + 1)

            maxima(0, 0)
            maxima(1, 1)
            normalise(0, 0)
            with dve.Fori(0, NKV - 1) as g:
                for j in range(GRP):
                    step(g, j, True)
            for j in range(GRP):
                step(NKV - 1, j, False)

            read_mods(80, 96, 24)
            gains(gout[:, 1], GATE2, C_GPOST2, 0.0)
            dve.drain()
            V.memset(SM[:, 121:122], 0.0).then_inc(mod3_read, 1)
            dve.wait_ge(gate_sig, 33)
            V.memset(SM[:, 122:123], 0.0).then_inc(ao_done, 1)
            with dve.Fori(0, 2) as i:
                for a in range(2):
                    dve.wait_ge(blocks_used, i * 4 + (4 * B_AO + 2 * a + 2))
                    for j in range(4):
                        d = sg[:, ds(i * 8 + (4 * a + j), 1), :].rearrange("p o t -> p (o t)")
                        tt(d, bank(4 * a + j, T), d, ALU.mult).then_inc(ao_done, 1)
            for c in range(4):
                dve.wait_ge(blocks_used, 4 * B_HO + c + 1)
                for j in range(4):
                    n, b = 4 * c + j, 4 * (c % 2) + j
                    dve.drain()
                    tt(sg[:, KT + n, :], bank(b, T), sg[:, KT + n, :], ALU.mult)
                    dve.drain()
                    tt(sg[:, n, :], sg[:, n, :], sg[:, KT + n, :], ALU.add).then_inc(ho_done, 1)

            def diagonals(which, n, ready):
                q, c = n // 2, n % 2
                for j in range(4):
                    last = ts_(diag[:, n % 2, j * P:(j + 1) * P], ident,
                               gout[:, which, 4 * q + j, c:c + 1], None, ALU.mult)
                last.then_inc(ready, 1)

            def gate_rows(which, dst, b0, ready, bc, used):
                diagonals(which, 0, ready)
                diagonals(which, 1, ready)
                for n in range(8):
                    dve.wait_ge(bc, n + 1)
                    V.tensor_copy(dst[:, n % 2, (n // 2) * NC_:(n // 2 + 1) * NC_],
                                  bank(b0 + n % 2)).then_inc(used, 1)
                    if n + 2 < 8:
                        diagonals(which, n + 2, ready)
                dve.drain()

            dve.wait_ge(wr_zero, 1)
            gate_rows(0, g_rows, 6, diag_ready, g_bc, g_used)
            for q in range(4):
                qs = slice(q * NC_, (q + 1) * NC_)
                for m in range(MT):
                    dve.wait_ge(wo_cp, 1 + 3 * q + m + 1)
                    tt(mix[:, m, qs], mix[:, m, qs], g_rows[:, min(m, 1), qs], ALU.mult)
            dve.wait_ge(sumsq3, 4 * MT)
            V.tensor_reduce(smx, ss.rearrange("p (m q) -> p m q", q=4), AX_X, ALU.add)
            dve.drain()
            ts_(ss[:, 0:MT], smx, 1.0 / D, EPS, ALU.mult, ALU.add).then_inc(ms2, 1)
            dve.wait_ge(rstd2, 1)
            dve.wait_ge(xres_in, 32)
            for m in range(MT):
                stt(out=res[:, m, :], in0=mix[:, m, :], scalar=rstd[:, m:m + 1], in1=res[:, m, :],
                    op0=ALU.mult, op1=ALU.add).then_inc(res_ready, 1)
            dve.drain()

            mean_square(sumsq3, 5 * MT, MT, D, ms3)
            dve.wait_ge(rstd3s, 1)
            for m in range(MT):
                ts_(xn[:, m, :], res[:, m, :], rstd[:, m:m + 1], None, ALU.mult).then_inc(xn2, 1)
            for k in range(0, KT, 2):
                dve.wait_ge(tr2, k + 1)
                for c, (lo, hi) in enumerate(SEG):
                    last = ts_(hT[:, k, lo:hi], bank(k % 4, hi - lo, lo), amp[:, 1, k, c:c + 1],
                               mod[:, SHIFT2 * KT + k, c:c + 1], ALU.mult, ALU.add)
                last.then_inc(tr2_v, 1)
            dve.wait_ge(lg_nat, 1)
            lg = PS[:, 5, 0:MT * NE].rearrange("p (m e) -> p m e", e=NE)

            def over_experts(v):
                return v.unsqueeze(2).to_broadcast([P, MT, NE])

            V.tensor_reduce(smx, lg, AX_X, ALU.max)
            dve.drain()
            tt(aff[:, :, :], lg, over_experts(smx), ALU.subtract).then_inc(lg_sub, 1)
            dve.wait_ge(lg_exp, 1)
            dve.drain()
            V.tensor_reduce(smx, aff[:, :, :], AX_X, ALU.add)
            dve.drain()
            V.reciprocal(smx, smx)
            dve.drain()
            tt(aff[:, :, :], aff[:, :, :], over_experts(smx), ALU.mult).then_inc(aff_ready, 1)
            dve.wait_ge(aff_tr, 1)
            V.tensor_copy(wk[0:NE, :], bank(4, T, p1=NE))
            for (lo, hi), cap in zip(SEG, (CAPC, CAPL)):
                for _ in range(cap // 8):
                    dve.drain()
                    V.max(m8[0:NE, :], wk[0:NE, lo:hi])
                    dve.drain()
                    V.match_replace(wk[0:NE, lo:hi], m8[0:NE, :], wk[0:NE, lo:hi], -1.0)
            dve.drain()
            ts_(wk[0:NE, :], wk[0:NE, :], 0.0, None, ALU.is_lt)
            dve.drain()
            for lo, hi in SEG:
                V.tensor_tensor_scan(cum[0:NE, lo:hi], wk[0:NE, lo:hi], wk[0:NE, lo:hi], 0.0, ALU.add, ALU.max)
            dve.drain()
            tt(cum[0:NE, :], cum[0:NE, :], wk[0:NE, :], ALU.mult).then_inc(v_ready, 1)
            dve.wait_ge(v_tr, 1)
            V.tensor_copy(vsel[:, :, :], PS[:, 5, 0:MT * NE].rearrange("p (m e) -> p m e", e=NE))
            dve.drain()
            tt(selC[:, :, :], vsel[:, 0, :].unsqueeze(2).to_broadcast([P, NE, CAPC]),
               slot_no[:, 0:CAPC].unsqueeze(1).to_broadcast([P, NE, CAPC]), ALU.is_equal)
            for t in range(2):
                last = tt(selL[:, t, :, :], vsel[:, 1 + t, :].unsqueeze(2).to_broadcast([P, NE, CAPL]),
                          slot_no.unsqueeze(1).to_broadcast([P, NE, CAPL]), ALU.is_equal)
            V.memset(selG[:, :, :], 0.0)
            dve.drain()
            V.memset(SM[:, 121:122], 0.0).then_inc(sel_ready, 1)

            def gated(m):
                s, o, n = (selC[:, :, :], CAPL, CAPC) if m == 0 else (selL[:, m - 1, :, :], 0, CAPL)
                for u in range(2):
                    last = tt(selG[:, :, 64 * u + o:64 * u + o + n], s,
                              aff[:, m, :].unsqueeze(2).to_broadcast([P, NE, n]), ALU.mult)
                last.then_inc(sg_ready, 1)

            gated(0)
            for k in range(KT):
                dve.wait_ge(gat_l, k + 1)
                ts_(xeT[:, k, :, 0:CAPL], bank(k % 2).rearrange("p (e s) -> p e s", e=NE), amp[:, 1, k, 1:2],
                    mod[:, SHIFT2 * KT + k, 1:2], ALU.mult, ALU.add).then_inc(gat_lv, 1)
            for m in (1, 2):
                dve.wait_ge(sg_tr, 4 * m)
                if m == 1:
                    for u in range(2):
                        V.memset(selG[:, :, 64 * u + CAPL:64 * u + SLOTS], 0.0)
                    dve.drain()
                gated(m)

            dve.wait_ge(facc_zero, 1)
            dve.wait_ge(sg_cp, 12)
            V.memset(SM[:, 121:122], 0.0).then_inc(e_acc, 4)

            def accumulate(turn, i, m, t):
                for u in range(2):
                    n = 2 * t + u
                    q = slice((2 * i + u) * NC_, (2 * i + u + 1) * NC_)
                    dve.wait_ge(e_sc, turn * 12 + (n + 1))
                    tt(facc[:, m, q], facc[:, m, q], bank(4 + n % 4), ALU.add).then_inc(e_acc, 1)

            def products(e, n):
                dve.wait_ge(e_silu, e * 2 + (n + 1))
                tt(h_s[0:SLOTS, n, :], act_s[0:SLOTS, :], bank(n, p0=64, p1=64 + SLOTS), ALU.mult).then_inc(e_h, 1)

            def products_to_columns(e, n):
                dve.wait_ge(e_htr, e * 2 + (n + 1))
                V.tensor_copy(hTe[:, 4 * n:4 * n + 4, :],
                              bank(2 + n, 4 * SLOTS).rearrange("p (k s) -> p k s", k=4)).then_inc(e_hT, 1)

            def expert(e):
                accumulate(e, 0, 0, 0)
                accumulate(e, 0, 1, 1)
                products(e, 0)
                accumulate(e, 0, 2, 2)
                accumulate(e, 1, 0, 3)
                products(e, 1)
                products_to_columns(e, 0)
                accumulate(e, 1, 1, 4)
                accumulate(e, 1, 2, 5)
                products_to_columns(e, 1)

            with dve.Fori(0, NE - 1) as e:
                expert(e)
            expert(NE - 1)
            dve.wait_ge(wr_zero, 2)
            gate_rows(1, g2_rows, 0, diag2_ready, g2_bc, g2_used)

            def finish(m):
                dve.wait_ge(rstd4, m + 1)
                stt(out=res[:, m, :], in0=f_g[:, m, :], scalar=rstd[:, m:m + 1], in1=res[:, m, :],
                    op0=ALU.mult, op1=ALU.add).then_inc(y_ready, 1)

            for m in range(MT):
                for i in range(2):
                    accumulate(NE, i, m, 2 * m + i)
                dve.drain()
                for q in range(4):
                    qs = slice(q * NC_, (q + 1) * NC_)
                    tt(f_g[:, m, qs], facc[:, m, qs], g2_rows[:, min(m, 1), qs], ALU.mult)
                if m:
                    finish(m - 1)
                dve.wait_ge(sumsq4, 4 * m + 4)
                V.tensor_reduce(smx[:, m:m + 1], ss[:, 4 * m:4 * m + 4], AX_X, ALU.add)
                dve.drain()
                ts_(smx[:, m:m + 1], smx[:, m:m + 1], 1.0 / D, EPS, ALU.mult, ALU.add).then_inc(ms4, 1)
            finish(MT - 1)


def tables():
    f32 = np.float32
    p = np.arange(P)
    tabs = np.zeros((P, N_TABS), f32)
    tabs[:, T_ID:T_ID + P] = np.eye(P)
    tabs[:, T_SEL2:T_SEL2 + 2] = (p[:, None] % 32) == np.arange(2)
    tabs[:, T_SEL16:T_SEL16 + 16] = (p[:, None] % 32) == np.arange(16)
    tabs[:, T_SLOT:T_SLOT + 32] = np.arange(1, 33)

    def dft(L):
        ang = np.pi * (2 * np.arange(L)[None, :] + 1) * np.arange(L)[:, None] / (2 * L)
        return np.cos(ang), np.sin(ang)

    parts = []
    for inverse in (False, True):
        for L in (TL, TC):
            for t in range(L // P):
                for m in dft(L):
                    m = m.T / L if inverse else m
                    parts.append(m[t * P:(t + 1) * P])
    dft_all = np.concatenate(parts, axis=1).astype(f32)

    def positions(L):
        t = np.linspace(0.0, 1.0, L, dtype=f32)
        bands = (HE - 1) // 2
        w = (f32(TWO_PI) * np.arange(L, dtype=f32) / f32(L)).astype(f32)
        f = np.linspace(1e-4, bands - 1, bands, dtype=f32)
        ang = (w[:, None] * f[None, :]).astype(f32)
        z = np.concatenate([t[:, None], np.cos(ang), -np.sin(ang)], axis=-1).astype(f32)
        lo, hi = math.log(1e-2) / 1.5, math.log(1e-2) / 0.3
        deltas = np.abs(np.linspace(lo, hi, HYW, dtype=f32))
        return z, np.exp(-t[:, None] * deltas[None, :]).astype(f32)

    zc, dc = positions(TC)
    zl, dl = positions(TL)
    zfeat = np.ascontiguousarray(np.concatenate([zc, zl]).T)
    decay = np.concatenate([dc, dl]).reshape(MT, P, HYW)

    half = HD // 2
    inv_freq = f32(10000.0) ** (-np.arange(0, half, 2, dtype=f32) / f32(half))
    n = np.arange(TL, dtype=f32)
    ang = np.concatenate([(np.floor(n / 64))[:, None] * inv_freq[None], (n % 64)[:, None] * inv_freq[None]], 1)
    ang = ang.astype(f32).reshape(TL, 2, 1, half // 2)
    cos = np.broadcast_to(np.cos(ang), (TL, 2, 2, half // 2))
    sin = np.concatenate([np.sin(ang), -np.sin(ang)], axis=2)
    rope = np.stack([cos.reshape(TL, HD), sin.reshape(TL, HD)], 1).reshape(2, P, 2, HD)
    rope = np.ascontiguousarray(rope.transpose(1, 0, 2, 3)).astype(f32)
    return tabs, dft_all, zfeat, decay, rope


def kernel(**inputs):
    import concourse.bacc as bacc
    from concourse.bass_utils import run_bass_kernel_spmd

    a = {k: np.asarray(v) for k, v in inputs.items()}

    def columns(v):
        return np.asarray(v).reshape(-1, P).T

    cols = np.ascontiguousarray(np.concatenate([
        columns(a["c_ctx"]), columns(a["c"]), columns(a["b_ada"]), columns(a["g_pre_mix"]),
        columns(a["g_post_mix"]), columns(a["g_pre_ffn"]), columns(a["g_post_ffn"]),
        columns(a["hy_conv_w"]), columns(a["hy_conv_b"]), columns(a["hy_skip"])], axis=1))
    f_vec = np.ascontiguousarray(np.concatenate([a["hy_f1_b"], a["hy_sin_freq"], a["hy_f2_b"]]).T)
    tabs, dft, zfeat, decay, rope = tables()
    ins = [
        ("x_prompt", a["x_prompt"][0]), ("x_sample", a["x_sample"][0]),
        ("cache_k", a["cache_k_ctx"].reshape(PAST, KVW)), ("cache_v", a["cache_v_ctx"].reshape(PAST, KVW)),
        ("cols", cols), ("w_ada", a["w_ada"][0]), ("w_in", a["w_in"][0]),
        ("qk_g", np.concatenate([a["q_norm_g"], a["k_norm_g"]])), ("w_attn_o", a["w_attn_o"][0]),
        ("f1_w", a["hy_f1_w"][0]), ("f_vec", f_vec), ("f2_w", a["hy_f2_w"][0]), ("f3_w", a["hy_f3_w"][0]),
        ("w_hy_o", a["w_hy_o"][0]), ("w_out", a["w_out"][0]), ("w_router", a["w_router"][0]),
        ("w_gate", a["w_exp_gate"].reshape(NE * D, FF)), ("w_up", a["w_exp_up"].reshape(NE * D, FF)),
        ("w_down", a["w_exp_down"].reshape(NE * FF, D)),
        ("tabs", tabs), ("dft", dft), ("zfeat", zfeat), ("decay", decay), ("rope", rope),
    ]
    outs = [("y_prompt", (TC, D)), ("y_sample", (TL, D)), ("state_k", (TC, KVW)), ("state_v", (TC, KVW))]
    nc = bacc.Bacc("TRN2", target_bir_lowering=False, num_devices=1)
    arrays, args = {}, []
    for name, v in ins:
        arrays[f"in_{name}"] = np.ascontiguousarray(v)
        args.append(nc.dram_tensor(f"in_{name}", v.shape, F32, kind="ExternalInput").ap())
    for name, shape in outs:
        args.append(nc.dram_tensor(f"out_{name}", shape, F32, kind="ExternalOutput").ap())
    build(nc, *args)
    r = run_bass_kernel_spmd(nc, [arrays], core_ids=[0]).results[0]
    return (r["out_y_prompt"].reshape(1, TC, D), r["out_y_sample"].reshape(1, TL, D),
            r["out_state_k"].reshape(1, 1, TC, NKV, HD), r["out_state_v"].reshape(1, 1, TC, NKV, HD))
```

```python
from contextlib import ExitStack
import math

import numpy as np

import concourse.bass as bass
from concourse import mybir

F32 = mybir.dt.float32
ALU = mybir.AluOpType
ACT = mybir.ActivationFunctionType
AX_X = mybir.AxisListType.X
ds = bass.ds

P = 128
D = 2048
KT = D // P
NC_ = 512
HK = 8
TC, TL = 128, 256
T = TC + TL
MT = T // P
SEG = ((0, TC), (TC, T))
NH, NKV, HD = 16, 4, 128
GRP = NH // NKV
KVW = NKV * HD
HYW = D // 2
HYT = HYW // P
PAST = 128
NE = 16
FF = D // 2
CAPC, CAPL = 2 * TC // NE, 2 * TL // NE
SLOTS = CAPC + CAPL
EPS = 1e-6
SCALE = HD ** -0.5
HF = 64
HE = 33
MAGIC = 1.5 * 2.0 ** 23
TWO_PI = 2.0 * math.pi
PI_A = 6.28125
PI_B = float(np.float32(np.round((TWO_PI - PI_A) * 2 ** 20) / 2 ** 20))
PI_C = float(np.float32(TWO_PI - PI_A - PI_B))
PI_IN = 3.1415925

ADA_A = 8
SHIFT1, SCALE1, GATE1, SHIFT2, SCALE2, GATE2 = range(6)

C_COND, C_BADA, C_GPRE1, C_GPOST1, C_GPRE2, C_GPOST2, C_CW, C_CB, C_SKIP = 0, 32, 128, 144, 160, 176, 192, 264, 288
N_COLS = 296
T_ID, T_SEL2, T_SEL16, T_SLOT = 0, 128, 130, 146
N_TABS = 178


def build(nc, x_prompt, x_sample, cache_k, cache_v, cols, w_ada, w_in, qk_g, w_attn_o, f1_w, f_vec, f2_w,
          f3_w, w_hy_o, w_out, w_router, w_gate, w_up, w_down, tabs, dft, zfeat, decay, rope,
          y_prompt, y_sample, state_k, state_v):
    ctx = ExitStack()
    with ctx:
        def sb(name, n):
            return ctx.enter_context(nc.sbuf_tensor(name, [P, n], F32))

        def sem(name):
            return ctx.enter_context(nc.semaphore(name))

        def view(t, off, *dims):
            n = int(np.prod(dims))
            v = t[:, off:off + n]
            if len(dims) == 1:
                return v
            names = "abcd"[:len(dims)]
            return v.rearrange(f"p ({' '.join(names)}) -> p {' '.join(names)}",
                               **{k: d for k, d in zip(names[1:], dims[1:])})

        ring_t = sb("ring", 4 * HK * NC_)
        RA, RB, RC = sb("RA", MT * D), sb("RB", MT * D), sb("RC", MT * D)
        RE, RF, RG = sb("RE", 2 * MT * D), sb("RF", 3072), sb("RG", 2048)
        KC = sb("KC", N_COLS + N_TABS)
        MODS = sb("MODS", 192 + 64 + 64)
        SM = sb("SM", 136)

        ring = view(ring_t, 0, 4, HK, NC_)
        col = KC[:, 0:N_COLS]
        ident = KC[:, N_COLS + T_ID:N_COLS + T_ID + P]
        sel2 = KC[:, N_COLS + T_SEL2:N_COLS + T_SEL2 + 2]
        sel16 = KC[:, N_COLS + T_SEL16:N_COLS + T_SEL16 + 16]
        slot_no = KC[:, N_COLS + T_SLOT:N_COLS + T_SLOT + 32]
        mod = view(MODS, 0, 96, 2)
        amp = view(MODS, 192, 2, KT, 2)
        gout = view(MODS, 256, 2, KT, 2)

        spec = view(RA, 0, 3, 2, HYW)
        rope_t = view(RA, 0, 2, 2, HD)
        rot = view(RA, 512, 2, 2, 2, HD)
        gain_b = view(RA, 1536, 2, HD)
        t_a, t_b = view(RA, 1792, NC_), view(RA, 2304, NC_)
        kT = view(RA, 0, NKV, T + PAST)
        q_st = view(RA, 2048, 2, MT, HD)
        qT = view(RA, 2816, 2, T)
        v_st = view(RA, 3584, 4, HD)
        res = view(RA, 0, MT, D)
        hT = view(RB, 0, KT, T)
        g_rows = view(RB, 0, 2, D)
        scat = view(RB, 0, NE, T)
        xn = view(RC, 0, MT, D)
        Z = view(RC, 0, 3, 2, NC_)
        dft_t = view(RC, 3072, 2560)
        fwd_l, fwd_c = view(RC, 3072, 2, 2, TL), view(RC, 4096, 2, TC)
        inv_l, inv_c = view(RC, 4352, 2, 2, TL), view(RC, 5376, 2, TC)
        oT = view(RC, 0, NH, T)
        mix = view(RC, 0, MT, D)
        selG = view(RC, 0, MT, NE, P)
        facc = view(RC, 0, MT, D)
        hN = view(RE, 0, MT, D)
        dec = view(RE, 6144, MT, HYW)
        f3 = view(RE, 9216, D)
        zf = view(RE, 11264, T)
        f1 = view(RE, 11648, HF)
        f2 = view(RE, 11712, HF)
        fv = view(RE, 11776, 3)
        hyT = view(RE, 0, 3 * HYT, T)
        uN = view(RE, 9216, MT, HYW)
        qkN = view(RE, 0, MT, D + KVW)
        vN = view(RE, 7680, 4, KVW)
        kcN = view(RE, 9728, KVW)
        prob = view(RE, 10240, 2, 2 * 384 + TC)
        sg = view(RE, 0, 2 * KT, T)
        xeT = view(RE, 0, KT, NE, SLOTS)
        g2_rows = view(RE, 0, 2, D)
        ones2 = view(RE, 2 * D, P)
        f_g = view(RE, 2 * D + P, MT, D)
        sq_scr = view(RF, 0, D)
        yhT = view(RF, 0, HYT, T)
        selL = view(RF, 2048, 2, NE, CAPL)
        x_cur = view(RF, 0, KT, SLOTS)
        s_cur = view(RF, 768, T)
        hTe = view(RF, 1152, HK, SLOTS)
        rowbuf = view(RG, 0, NC_)
        condS = view(RG, 512, KT, 32)
        arg, rnd = view(RE, 11792, T), view(RF, 2048, T)
        tmp = view(RG, 1024, NC_)
        probT = view(RG, 1024, 896)
        wr = view(RG, 0, KT, 32)
        ones = view(RG, 512, P)
        diag = view(RF, 2048, 2, NC_)
        lgr = view(RG, 512, T)
        selC = view(RG, 512, NE, CAPC)
        aT, wk, cum = view(RG, 896, T), view(RG, 1280, T), view(RG, 1664, T)
        act_s, h_s = view(RF, 1536, NC_), view(RG, 0, 2, NC_)
        ye = view(RG, 1024, 2, NC_)

        ss = view(SM, 0, 12)
        neghalf = view(SM, 124, 12)
        rstd = view(SM, 24, 12)
        rstd3 = view(SM, 24, MT, 4)
        mx = view(SM, 36, 2, 3)
        nb = view(SM, 42, 2, 3)
        rs = view(SM, 48, 2, 3)
        ri = view(SM, 54, 2, 3)
        aff = view(SM, 60, MT, NE)
        vsel = view(SM, 0, MT, NE)
        smx = view(SM, 108, MT)
        m8 = view(SM, 112, 8)

        PS = ctx.enter_context(nc.psum_tensor("PS", [P, 8, 512], F32))

        U_BANK = ((4, 5, 0), (1, 2, 3))
        Z_BANK = ((4, 0, 2), (0, 2, 4))

        def bank(b, n=512, off=0, p0=0, p1=P):
            return PS[p0:p1, b, off:off + n]

        landed = [sem(f"landed{j}") for j in range(4)]
        blocks_used = sem("blocks_used")
        landed_2 = [sem(f"landed_2_{j}") for j in range(4)]
        half_used = sem("half_used")
        small_in, x_in, filt_in, taps_in, dft_in, qk_in, cache_in, xres_in, wr_in = (
            sem(n) for n in ("small_in", "x_in", "filt_in", "taps_in", "dft_in", "qk_in", "cache_in", "xres_in", "wr_in"))
        out_done = sem("out_done")
        cond_ready, rows_copied, cols_done = sem("cond_ready"), sem("rows_copied"), sem("cols_done")
        sumsq1, ms1, rstd1, xn1 = sem("sumsq1"), sem("ms1"), sem("rstd1"), sem("xn1")
        tr1, tr1_copied = sem("tr1"), sem("tr1_copied")
        f_mm, f_arg, f_sin, f_taps, f_tapmm = (sem(n) for n in ("f_mm", "f_arg", "f_sin", "f_taps", "f_tapmm"))
        f_sumdiff, f_dft, f_spec_a, f_spec_v = (sem(n) for n in ("f_sumdiff", "f_dft", "f_spec_a", "f_spec_v"))
        mod1_read, conv_free, conv_mid = sem("mod1_read"), sem("conv_free"), sem("conv_mid")
        u_ready, u_tr, u_cp, u_dft, z_ready, z_inv, yh_done = (
            sem(n) for n in ("u_ready", "u_tr", "u_cp", "u_dft", "z_ready", "z_inv", "yh_done"))
        qkv_raw, q_ms, q_rstd, qk_done, v_done, rope_done = (
            sem(n) for n in ("qkv_raw", "q_ms", "q_rstd", "qk_done", "v_done", "rope_done"))
        q_staged, v_staged, at_trk, at_kT, at_trq, at_qT, at_s, at_max, at_exp, at_norm, at_trp, at_pa, at_pb, at_o, at_oc = (
            sem(n) for n in ("q_staged", "v_staged", "at_trk", "at_kT", "at_trq", "at_qT", "at_s", "at_max", "at_exp", "at_norm",
                             "at_trp", "at_pa", "at_pb", "at_o", "at_oc"))
        mod2_read, gate_sig, ao_done, ho_done, mod3_read = (
            sem(n) for n in ("mod2_read", "gate_sig", "ao_done", "ho_done", "mod3_read"))
        wo_cp, ms2, rstd2, diag_ready, g_bc, g_used = (
            sem(n) for n in ("wo_cp", "ms2", "rstd2", "diag_ready", "g_bc", "g_used"))
        res_ready, sumsq3, ms3, rstd3s, xn2, tr2, tr2_v, tr2_a = (
            sem(n) for n in ("res_ready", "sumsq3", "ms3", "rstd3s", "xn2", "tr2", "tr2_v", "tr2_a"))
        wr_zero, lg_mm, lg_cp, lg_nat, lg_sub, lg_exp, aff_ready, aff_tr, v_ready, v_tr, sel_ready = (
            sem(n) for n in ("wr_zero", "lg_mm", "lg_cp", "lg_nat", "lg_sub", "lg_exp", "aff_ready", "aff_tr",
                             "v_ready", "v_tr", "sel_ready"))
        gat_l, gat_c, gat_lv, gat_ca = (sem(n) for n in ("gat_l", "gat_c", "gat_lv", "gat_ca"))
        sg_ready, sg_tr, sg_cp = sem("sg_ready"), sem("sg_tr"), sem("sg_cp")
        facc_zero, xe_st, sc_st, e_silu, e_h, e_htr, e_hT, e_yc, e_sc, e_acc = (
            sem(n) for n in ("facc_zero", "xe_st", "sc_st", "e_silu", "e_h", "e_htr", "e_hT", "e_yc", "e_sc",
                             "e_acc"))
        sumsq4, ms4, rstd4, diag2_ready, g2_bc, g2_used, y_ready = (
            sem(n) for n in ("sumsq4", "ms4", "rstd4", "diag2_ready", "g2_bc", "g2_used", "y_ready"))

        B_HY = ADA_A // 2
        B_QKV = B_HY + 6
        B_GA = B_QKV + 6
        B_GB = B_GA + 4
        B_AO = B_GB + 2
        B_HO = B_AO + 2
        B_WO = B_HO + 1
        B_EX = B_WO + 2

        def block(w, h, c):
            return w[h * HK * P:(h + 1) * HK * P, ds(c * NC_, NC_)].rearrange("(k p) n -> p k n", p=P)

        blk = ctx.enter_context(nc.Block())

        @blk.sync
        def _(sp):
            def turn(b, parts):
                for j, (w, h, c) in enumerate(parts):
                    if b is not None:
                        sp.wait_ge(blocks_used, b * 4 + (j - 3))
                    sp.dma_start(ring[:, j], block(w, h, c)).then_inc(landed[j], 16)

            sp.dma_start(zf[0:HE, :], zfeat).then_inc(filt_in, 16)
            sp.dma_start(f1[0:HE, :], f1_w).then_inc(filt_in, 16)
            sp.dma_start(f2[0:HF, :], f2_w).then_inc(filt_in, 16)
            sp.dma_start(fv[0:HF, :], f_vec).then_inc(filt_in, 16)
            sp.dma_start(xn[:, 0, :], x_prompt).then_inc(x_in, 16)
            sp.dma_start(xn[:, 1:3, :], x_sample.rearrange("(m p) d -> p m d", p=P)).then_inc(x_in, 16)
            turn(None, [(w_ada, 0, 0), (w_ada, 1, 0), (w_ada, 0, 4), (w_ada, 1, 4)])
            with sp.Fori(1, ADA_A // 2) as i:
                turn(i, [(w_ada, 0, i), (w_ada, 1, i), (w_ada, 0, i + 4), (w_ada, 1, i + 4)])
            for base, ada0, in0, n in ((B_HY, 8, 6, 6), (B_QKV, 14, 0, 6), (B_GA, 20, 12, 4)):
                with sp.Fori(0, n) as i:
                    turn(i + base, [(w_ada, 0, i + ada0), (w_ada, 1, i + ada0),
                                    (w_in, 0, i + in0), (w_in, 1, i + in0)])
            for base, w, c0 in ((B_GB, w_in, 16), (B_AO, w_attn_o, 0)):
                with sp.Fori(0, 2) as i:
                    turn(i + base, [(w, 0, 2 * i + c0), (w, 1, 2 * i + c0),
                                    (w, 0, 2 * i + (c0 + 1)), (w, 1, 2 * i + (c0 + 1))])
            turn(B_HO, [(w_hy_o, 0, c) for c in range(4)])
            with sp.Fori(0, 2) as i:
                turn(i + B_WO, [(w_out, 0, 2 * i), (w_out, 1, 2 * i),
                                (w_out, 0, 2 * i + 1), (w_out, 1, 2 * i + 1)])
            with sp.Fori(0, NE) as e:
                def rows(w, n_rows, h, c):
                    return w[ds(e * n_rows + h * HK * P, HK * P), c * NC_:(c + 1) * NC_] \
                        .rearrange("(k p) n -> p k n", p=P)
                def pair(turn, j0, blocks):
                    for u in range(2):
                        sp.wait_ge(half_used, e * 12 + (4 * turn + j0 + u + 1))
                        sp.dma_start(ring[:, j0 + u, 0:HK // 2], blocks[u][:, 0:HK // 2])\
                            .then_inc(landed[j0 + u], 16)
                    for u in range(2):
                        sp.wait_ge(blocks_used, e * 12 + (4 * (B_EX + turn) + j0 + u - 3))
                        sp.dma_start(ring[:, j0 + u, HK // 2:HK], blocks[u][:, HK // 2:HK])\
                            .then_inc(landed_2[j0 + u], 16)

                for n in range(2):
                    for h in range(2):
                        pair(n, 2 * h, [rows(w_gate, D, h, n), rows(w_up, D, h, n)])
                for i in range(2):
                    pair(2, 2 * i, [rows(w_down, FF, 0, 2 * i), rows(w_down, FF, 0, 2 * i + 1)])
            for m in range(MT):
                sp.wait_ge(y_ready, m + 1)
                dst = y_prompt if m == 0 else y_sample[(m - 1) * P:m * P, :]
                sp.dma_start(dst, res[:, m, :]).then_inc(out_done, 16)
            sp.wait_ge(out_done, 16 * (MT + 2))

        @blk.tensor
        def _(pe):
            mm, trp = nc.tensor.matmul, nc.tensor.transpose

            def ada(b, j0, rows_bank):
                for h in range(2):
                    pe.wait_ge(landed[j0 + h], b * 16 + 16)
                    for k in range(HK):
                        kk, g = h * HK + k, k % 4
                        last = mm(bank(rows_bank, p0=32 * g, p1=32 * g + 32), condS[:, kk, :],
                                  ring[:, j0 + h, k, :], start=kk < 4, stop=kk >= KT - 4)
                    last.then_inc(blocks_used, 1)

            def ada_cols(c, which, n=None):
                pe.wait_ge(rows_copied, (c if n is None else n) + 1)
                src = rowbuf if which == 0 else tmp
                for j in range(4):
                    last = mm(PS[:, 6, ds(c * 8 + 2 * j, 2)], src[:, j * P:(j + 1) * P], sel2,
                              start=True, stop=True)
                last.then_inc(cols_done, 1)

            def channels(b, j0, b0, rhs, free=None):
                for h in range(2):
                    pe.wait_ge(landed[j0 + h], b * 16 + 16)
                    for k in range(HK):
                        for c in range(4):
                            if free and h == 0 and k == 0:
                                pe.wait_ge(conv_free, free(c))
                            last = mm(bank(b0 + c, T), ring[:, j0 + h, k, c * P:(c + 1) * P],
                                      rhs[:, h * HK + k, :], start=(h == 0 and k == 0),
                                      stop=(h == 1 and k == HK - 1))
                    last.then_inc(blocks_used, 1)

            def tokens(b, j0, b0, lhs, then=None):
                for h in range(2):
                    pe.wait_ge(landed[j0 + h], b * 16 + 16)
                    for k in range(HK):
                        for m in range(MT):
                            last = mm(bank(b0 + m), lhs[:, h * HK + k, m * P:(m + 1) * P],
                                      ring[:, j0 + h, k, :], start=(h == 0 and k == 0),
                                      stop=(h == 1 and k == HK - 1))
                    last.then_inc(blocks_used, 1)
                    if then:
                        then(h)

            pe.wait_ge(small_in, 32)

            pe.wait_ge(filt_in, 64)
            mm(bank(0, T, p1=HF), f1[0:HE, :], zf[0:HE, :], start=True, stop=True).then_inc(f_mm, 1)
            pe.wait_ge(xn1, MT)
            for k in range(KT):
                if k >= 3:
                    pe.wait_ge(tr1_copied, k - 2)
                for m in range(MT):
                    last = trp(bank(1 + k % 3, P, m * P), xn[:, m, k * P:(k + 1) * P], ident)
                last.then_inc(tr1, 1)
            pe.wait_ge(f_sin, 1)
            mm(bank(4, T, p1=HF), f2[0:HF, :], arg[0:HF, :], start=True, stop=True).then_inc(f_mm, 1)

            def ada_a(i):
                ada(i, 0, 7)
                ada(i, 2, 5)
                if i:
                    pe.wait_ge(mod1_read, i)
                ada_cols(i, 0, 2 * i)
                ada_cols(i + 4, 1, 2 * i + 1)

            pe.wait_ge(cond_ready, 2)
            ada_a(0)
            pe.wait_ge(f_sin, 2)
            pe.wait_ge(taps_in, 48)
            for m in range(MT):
                for c in range(4):
                    n = 4 * m + c
                    if n >= 4:
                        pe.wait_ge(f_taps, n - 3)
                    elif n > 0:
                        pe.wait_ge(tr1_copied, KT)
                    mm(bank(n % 4), arg[0:HF, m * P:(m + 1) * P], f3[0:HF, c * NC_:(c + 1) * NC_],
                       start=True, stop=True).then_inc(f_tapmm, 1)
            ada_a(1)

            def filter_spectrum(j):
                for cs in range(2):
                    taps = dec if cs == 0 else hN
                    for half in range(2):
                        n = 4 * j + 2 * cs + half
                        if n >= 4:
                            pe.wait_ge(f_spec_a if n % 2 == 0 else f_spec_v, (n - 4) // 2 + 1)
                        hs = slice(half * NC_, (half + 1) * NC_)
                        if j == 0:
                            last = mm(bank(n % 4), fwd_c[:, cs, :], taps[:, 0, hs], start=True, stop=True)
                        else:
                            for t in range(2):
                                last = mm(bank(n % 4), fwd_l[:, t, cs, (j - 1) * P:j * P], taps[:, 1 + t, hs],
                                          start=t == 0, stop=t == 1)
                        last.then_inc(f_dft, 1)

            pe.wait_ge(dft_in, 16)
            pe.wait_ge(f_taps, 12)
            pe.wait_ge(f_sumdiff, 1)
            filter_spectrum(0)
            filter_spectrum(1)
            ada_a(2)
            filter_spectrum(2)
            ada_a(3)

            with pe.Fori(0, 6) as i:
                ada(i + B_HY, 0, 7)
                channels(i + B_HY, 2, 0, hT, lambda c: i * 4 + (c + 1))
                ada_cols(i + 8, 0)

            def u_tokens(half, m):
                for c in range(4):
                    last = trp(bank(U_BANK[half][m], P, c * P),
                               hyT[:, 2 * HYT + half * 4 + c, m * P:(m + 1) * P], ident)
                last.then_inc(u_tr, 1)

            def u_spectrum(half, j):
                hs = slice(half * NC_, (half + 1) * NC_)
                for cs in range(2):
                    b = Z_BANK[half][j] + cs
                    if j == 0:
                        last = mm(bank(b), fwd_c[:, cs, :], uN[:, 0, hs], start=True, stop=True)
                    else:
                        for t in range(2):
                            last = mm(bank(b), fwd_l[:, t, cs, (j - 1) * P:j * P], uN[:, 1 + t, hs],
                                      start=t == 0, stop=t == 1)
                last.then_inc(u_dft, 1)

            def inverse(half):
                pe.wait_ge(z_ready, 3 * half + 3)
                for c in range(4):
                    n = 4 * half + c
                    cc = slice(c * P, (c + 1) * P)
                    b = 7 if n % 2 == 0 else 5
                    if n >= 2:
                        pe.wait_ge(yh_done, n - 1)
                    for cs in range(2):
                        mm(bank(b, TC), Z[:, 0, cs, cc], inv_c[:, cs, :], start=cs == 0, stop=cs == 1)
                    for q in range(4):
                        last = mm(bank(b, TL, TC), Z[:, 1 + q // 2, q % 2, cc], inv_l[:, q // 2, q % 2, :],
                                  start=q == 0, stop=q == 3)
                    last.then_inc(z_inv, 1)

            pe.wait_ge(u_ready, 1)
            u_tokens(0, 0)
            u_tokens(0, 1)
            pe.wait_ge(conv_free, 25)
            u_tokens(0, 2)
            pe.wait_ge(u_cp, 2)
            u_spectrum(0, 0)
            pe.wait_ge(conv_free, 28)
            pe.wait_ge(u_ready, 2)
            for m in range(MT):
                u_tokens(1, m)
            pe.wait_ge(u_cp, 4)
            u_spectrum(0, 1)
            pe.wait_ge(u_cp, 6)
            u_spectrum(0, 2)
            pe.wait_ge(z_ready, 2)
            u_spectrum(1, 0)
            inverse(0)
            u_spectrum(1, 1)
            pe.wait_ge(yh_done, 4)
            u_spectrum(1, 2)
            inverse(1)

            pe.wait_ge(yh_done, 8)
            with pe.Fori(0, 6) as i:
                ada(i + B_QKV, 0, 7)
                pe.wait_ge(qkv_raw, i * 3 + 3)
                tokens(i + B_QKV, 2, 0, hT)
                ada_cols(i + 14, 0)

            pe.wait_ge(mod2_read, 1)
            pe.wait_ge(cache_in, 32)
            pe.wait_ge(v_done, MT)
            for g in range(NKV):
                for m in range(4):
                    src = kcN[:, g * HD:(g + 1) * HD] if m == 3 else qkN[:, m, D + g * HD:D + (g + 1) * HD]
                    last = trp(bank(g, P, m * P), src, ident)
                last.then_inc(at_trk, 1)

            def queries(h, j):
                pe.wait_ge(q_staged, h + 1)
                for m in range(MT):
                    last = trp(bank(6, P, m * P), q_st[:, j % 2, m, :], ident)
                last.then_inc(at_trq, 1)

            def scores(h, g, j):
                b0, p = 2 * (j % 2), j % 2
                keys = kT[:, ds(g, 1), :].rearrange("p o t -> p (o t)")
                pe.wait_ge(at_qT, h + 1)
                mm(bank(b0, 384), qT[:, p, TC:TC + P], keys[:, TC:], start=True, stop=True)
                mm(bank(b0, TC, 384), qT[:, p, 0:TC], keys[:, 0:TC], start=True, stop=True)
                mm(bank(b0 + 1, 384), qT[:, p, TC + P:T], keys[:, TC:], start=True, stop=True).then_inc(at_s, 1)

            def step(g, j, more):
                h = g * 4 + j
                pe.wait_ge(at_norm, h + 1)
                for kt in range(3):
                    for qt in range(2):
                        o = kt * 256 + qt * P
                        trp(bank(4 + o // 512, P, o % 512),
                            prob[:, j % 2, qt * 384 + kt * P:qt * 384 + (kt + 1) * P], ident)
                trp(bank(5, P, 256), prob[:, j % 2, 768:896], ident).then_inc(at_trp, 1)
                if more or j + 2 < GRP:
                    scores(h + 2, g + (j + 2) // GRP, j)
                if j == 0:
                    pe.wait_ge(v_staged, g + 1)
                pe.wait_ge(at_pa, h + 1)
                pe.wait_ge(at_pb, h + 1)
                mm(bank(7, TC), v_st[:, 0, :], probT[:, 768:896], start=True, stop=True)
                for kt in range(3):
                    last = mm(bank(7, TL, TC), v_st[:, 1 + kt, :], probT[:, kt * 256:(kt + 1) * 256],
                              start=kt == 0, stop=kt == 2)
                last.then_inc(at_o, 1)
                if more or j + 3 < GRP:
                    queries(h + 3, j + 3)

            queries(0, 0)
            pe.wait_ge(at_kT, NKV)
            scores(0, 0, 0)
            queries(1, 1)
            scores(1, 0, 1)
            queries(2, 2)
            with pe.Fori(0, NKV - 1) as g:
                for j in range(GRP):
                    step(g, j, True)
            for j in range(GRP):
                step(NKV - 1, j, False)
            pe.wait_ge(at_oc, NH)

            with pe.Fori(0, 4) as i:
                ada(i + B_GA, 0, 7)
                pe.wait_ge(gate_sig, i * 4 + 1)
                channels(i + B_GA, 2, 0, hT)
                ada_cols(i + 20, 0)
            pe.wait_ge(mod3_read, 1)
            with pe.Fori(0, 2) as i:
                for a in range(2):
                    pe.wait_ge(gate_sig, i * 8 + (17 if a == 0 else 13))
                    channels(i + B_GB, 2 * a, 4 * a, hT)
            pe.wait_ge(gate_sig, 33)
            with pe.Fori(0, 2) as i:
                for a in range(2):
                    pe.wait_ge(ao_done, i * 8 + (4 * a + 1))
                    channels(i + B_AO, 2 * a, 4 * a, oT)
            for c in range(4):
                pe.wait_ge(ao_done, 17)
                if c >= 2:
                    pe.wait_ge(ho_done, 4 * (c - 1))
                pe.wait_ge(landed[c], 16 * (B_HO + 1))
                for k in range(HYT):
                    for j in range(4):
                        last = mm(bank(4 * (c % 2) + j, T), ring[:, c, k, j * P:(j + 1) * P], yhT[:, k, :],
                                  start=k == 0, stop=k == HYT - 1)
                last.then_inc(blocks_used, 1)
            pe.wait_ge(ho_done, 16)

            def broadcast_gates(n0, b0, one, ready, done, used):
                for n in (n0, n0 + 1):
                    pe.wait_ge(ready, n + 1)
                    if n >= 2:
                        pe.wait_ge(used, n - 1)
                    mm(bank(b0 + n % 2), one, diag[:, n % 2, :], start=True, stop=True).then_inc(done, 1)

            for q in range(4):
                pe.wait_ge(wo_cp, 1 + 3 * max(q - 1, 0))
                tokens(B_WO + q // 2, 2 * (q % 2), 3 * (q % 2), sg,
                       (lambda h: broadcast_gates(4 * q + 2 * h, 6, ones, diag_ready, g_bc, g_used))
                       if q < 2 else None)

            pe.wait_ge(xn2, MT)
            for k in range(KT):
                if k >= 4:
                    pe.wait_ge(tr2_v if k % 2 == 0 else tr2_a, k // 2 - 1)
                for m in range(MT):
                    last = trp(bank(k % 4, P, m * P), xn[:, m, k * P:(k + 1) * P], ident)
                    if k == 0 and m == 0:
                        last.then_inc(half_used, 4)
                last.then_inc(tr2, 1)
            pe.wait_ge(wr_in, 16)
            pe.wait_ge(tr2_v, KT // 2)
            pe.wait_ge(tr2_a, KT // 2)
            for k in range(KT):
                g = k % 4
                last = mm(bank(4, T, p0=32 * g, p1=32 * g + 32), wr[:, k, :], hT[:, k, :],
                          start=k < 4, stop=k >= KT - 4)
            last.then_inc(lg_mm, 1)
            pe.wait_ge(lg_cp, 1)
            for m in range(MT):
                last = mm(bank(5, NE, m * NE), lgr[:, m * P:(m + 1) * P], sel16, start=True, stop=True)
            last.then_inc(lg_nat, 1)
            pe.wait_ge(aff_ready, 1)
            for m in range(MT):
                last = trp(bank(4, P, m * P, p1=NE), aff[:, m, :], ident)
            last.then_inc(aff_tr, 1)
            pe.wait_ge(v_ready, 1)
            for m in range(MT):
                last = trp(bank(5, NE, m * NE), cum[0:NE, m * P:(m + 1) * P], ident[0:NE, 0:NE])
            last.then_inc(v_tr, 1)
            pe.wait_ge(sel_ready, 1)
            for k in range(KT):
                if k >= 2:
                    pe.wait_ge(gat_lv, k - 1)
                    pe.wait_ge(gat_ca, k - 1)
                kk = slice(k * P, (k + 1) * P)
                mm(bank(2 + k % 2, NE * CAPC), xn[:, 0, kk], selC[:, :, :], start=True,
                   stop=True).then_inc(gat_c, 1)
                for t in range(2):
                    last = mm(bank(k % 2), xn[:, 1 + t, kk], selL[:, t, :, :], start=t == 0, stop=t == 1)
                last.then_inc(gat_l, 1)
            pe.wait_ge(gat_lv, KT)
            pe.wait_ge(gat_ca, KT)

            def scatter_matrices(t):
                for n in (2 * t, 2 * t + 1):
                    m, q = n // 4, n % 4
                    pe.wait_ge(sg_ready, m + 1)
                    if n >= 4:
                        pe.wait_ge(sg_cp, n - 3)
                    for j in range(4):
                        last = trp(bank(4 + n % 4, P, j * P), selG[:, m, 4 * q + j, :], ident)
                    last.then_inc(sg_tr, 1)

            def scatter(turn, i, m, t):
                if m == 0:
                    pe.wait_ge(e_yc, turn * 2 + (i - 1))
                for u in range(2):
                    n = 2 * t + u
                    pe.wait_ge(e_acc, turn * 12 + (n - 11))
                    mm(bank(4 + n % 4), s_cur[64 * u:64 * u + SLOTS, m * P:(m + 1) * P],
                       ye[64 * u:64 * u + SLOTS, i, :], start=True, stop=True).then_inc(e_sc, 1)

            def expert(e, first=False, final=False):
                def beside(t):
                    if first:
                        scatter_matrices(t)
                    else:
                        scatter(e, t // MT, t % MT, t)
                    if final and t < 4:
                        broadcast_gates(2 * t, 2, ones2, diag2_ready, g2_bc, g2_used)

                def landing(turn, j0, k):
                    for j in (j0, j0 + 1):
                        if k == 0:
                            pe.wait_ge(landed[j], e * 48 + 16 * (B_EX + turn + 1))
                        elif k == HK // 2:
                            pe.wait_ge(landed_2[j], e * 48 + 16 * (turn + 1))

                def release(last, k):
                    if k == HK // 2 - 1:
                        last.then_inc(half_used, 1)
                    elif k == HK - 1:
                        last.then_inc(blocks_used, 1)

                if not first:
                    pe.wait_ge(xe_st, e)
                    pe.wait_ge(sc_st, e)
                if final:
                    pe.wait_ge(e_yc, 2 * e)
                for n in range(2):
                    for h in range(2):
                        for k in range(HK):
                            landing(n, 2 * h, k)
                            kk = h * HK + k
                            for u in range(2):
                                last = mm(bank(n, p0=64 * u, p1=64 * u + SLOTS),
                                          xeT[:, kk, 0, :] if first else x_cur[:, kk, :],
                                          ring[:, 2 * h + u, k, :], start=(h == 0 and k == 0),
                                          stop=(h == 1 and k == HK - 1))
                                release(last, k)
                        beside(2 * n + h)
                if final:
                    pe.wait_ge(g2_used, 8)
                for n in range(2):
                    pe.wait_ge(e_h, e * 2 + (n + 1))
                    for j in range(4):
                        o, src, i_ = bank(2 + n, SLOTS, j * SLOTS), h_s[0:SLOTS, n, j * P:(j + 1) * P], \
                            ident[0:SLOTS, 0:SLOTS]
                        last = mm(o, src, i_, start=True, stop=True) if j == 0 else trp(o, src, i_)
                    last.then_inc(e_htr, 1)
                pe.wait_ge(e_hT, e * 2 + 1)
                for i in range(2):
                    for k in range(HK):
                        landing(2, 2 * i, k)
                        if i == 0 and k == HK // 2:
                            beside(4)
                            pe.wait_ge(e_hT, e * 2 + 2)
                        if final and i == 1 and k == HK // 2:
                            pe.wait_ge(sc_st, NE)
                            for m in range(MT):
                                scatter(NE, 0, m, m)
                        for u in range(2):
                            last = mm(bank(2 + i, p0=64 * u, p1=64 * u + SLOTS), hTe[:, k, :],
                                      ring[:, 2 * i + u, k, :], start=k == 0, stop=k == HK - 1)
                            release(last, k)
                    if i == 0:
                        beside(5)

            expert(0, first=True)
            with pe.Fori(1, NE - 1) as e:
                expert(e)
            expert(NE - 1, final=True)
            for m in range(MT):
                scatter(NE, 1, m, MT + m)

        @blk.scalar
        def _(act):
            A = nc.scalar.activation
            act.dma_start(col, cols).then_inc(small_in, 16)
            act.dma_start(KC[:, N_COLS:N_COLS + N_TABS], tabs).then_inc(small_in, 16)

            act.wait_ge(small_in, 32)
            act.wait_ge(cond_ready, 1)
            A(condS[:, :, 0:2], col[:, C_COND:C_COND + 32].rearrange("p (c k) -> p k c", c=2),
              ACT.Silu).then_inc(cond_ready, 1)
            act.wait_ge(x_in, 32)
            act.dma_start(f3[0:HF, :], f3_w).then_inc(taps_in, 16)
            act.dma_start(dec[:, 0, :], decay[0]).then_inc(taps_in, 16)
            act.dma_start(dec[:, 1:3, :], decay[1:3].rearrange("m p d -> p m d")).then_inc(taps_in, 16)
            for m in range(MT):
                A(sq_scr, xn[:, m, :], ACT.Square, accum_out=ss[:, m:m + 1]).then_inc(sumsq1, 1)
                act.drain()
            act.wait_ge(f_arg, 1)
            A(arg[0:HF, :], arg[0:HF, :], ACT.Sin).then_inc(f_sin, 1)
            act.wait_ge(f_arg, 2)
            A(arg[0:HF, :], arg[0:HF, :], ACT.Sin).then_inc(f_sin, 1)
            act.wait_ge(tr1, KT)
            act.dma_start(dft_t, dft).then_inc(dft_in, 16)

            def rows(used, src_bank, dst):
                act.wait_ge(blocks_used, used)
                A(dst, bank(src_bank), ACT.Copy).then_inc(rows_copied, 1)

            for i in range(ADA_A // 2):
                if i:
                    act.wait_ge(cols_done, i * 2)
                if i >= 2:
                    for n in range(*((0, 8, 2) if i == 2 else (8, 12, 2))):
                        act.wait_ge(f_dft, n + 1)
                        A(spec[:, n // 4, (n // 2) % 2, 0:NC_], bank(n % 4), ACT.Copy).then_inc(f_spec_a, 1)
                rows(i * 4 + 2, 7, rowbuf)
                rows(i * 4 + 4, 5, tmp)

            with act.Fori(0, 6) as i:
                act.wait_ge(cols_done, i + 8)
                rows(i * 4 + (4 * B_HY + 2), 7, rowbuf)
                act.wait_ge(blocks_used, i * 4 + (4 * B_HY + 4))
                for j in range(4):
                    A(hyT[:, ds(i * 4 + j, 1), :], bank(j, T), ACT.Identity,
                      bias=col[:, ds(i * 4 + (C_CB + j), 1)],
                      scale=col[:, ds(i * 4 + (C_CW + 24 + j), 1)]).then_inc(conv_mid, 1)

            for n in range(6):
                act.wait_ge(u_tr, n + 1)
                half, m = n // MT, n % MT
                A(uN[:, m, half * NC_:(half + 1) * NC_], bank(U_BANK[half][m]), ACT.Copy).then_inc(u_cp, 1)

            act.wait_ge(z_ready, 6)
            act.dma_start(rope_t[:, :, :, :], rope).then_inc(qk_in, 16)
            act.dma_start(gain_b, qk_g.rearrange("(o a) d -> o (a d)", o=1).to_broadcast([P, 2 * HD])
                          .rearrange("p (a d) -> p a d", a=2)).then_inc(qk_in, 16)
            act.wait_ge(yh_done, 8)
            act.dma_start(kcN, cache_k).then_inc(cache_in, 16)
            act.dma_start(vN[:, 3, :], cache_v).then_inc(cache_in, 16)
            act.wait_ge(yh_done, 8)
            act.nop().then_inc(qkv_raw, 3)
            with act.Fori(0, 5) as i:
                act.wait_ge(cols_done, i + 14)
                rows(i * 4 + (4 * B_QKV + 2), 7, rowbuf)
                act.wait_ge(blocks_used, i * 4 + (4 * B_QKV + 4))
                for m in range(MT):
                    A(qkN[:, m, ds(i * NC_, NC_)], bank(m), ACT.Copy).then_inc(qkv_raw, 1)
            act.wait_ge(cols_done, 19)
            rows(4 * B_QKV + 22, 7, rowbuf)
            act.wait_ge(blocks_used, 4 * B_QKV + 24)
            for m in range(MT):
                A(vN[:, m, :], bank(m), ACT.Copy).then_inc(v_done, 1)
            act.wait_ge(v_done, MT)
            act.dma_start(state_v, vN[:, 0, :]).then_inc(out_done, 16)
            act.wait_ge(qk_done, 5)
            act.dma_start(state_k, qkN[:, 0, D:D + KVW]).then_inc(out_done, 16)

            for g in range(0, NKV, 2):
                act.wait_ge(at_trk, g + 1)
                A(kT[:, g, :], bank(g), ACT.Copy).then_inc(at_kT, 1)

            def queries(h, j):
                act.wait_ge(at_trq, h + 1)
                A(qT[:, j % 2, :], bank(6, T), ACT.Copy).then_inc(at_qT, 1)

            def exponentials(h, j):
                p = j % 2
                act.wait_ge(at_max, h + 1)
                for t, (lo, hi) in enumerate(((0, 384), (384, 768), (768, 896))):
                    src = (bank(2 * p, 384), bank(2 * p + 1, 384), bank(2 * p, TC, 384))[t]
                    A(prob[:, p, lo:hi], src, ACT.Exp, bias=nb[:, p, t:t + 1], scale=SCALE,
                      accum_out=rs[:, p, t:t + 1])
                act.drain()
                act.nop().then_inc(at_exp, 1)

            def step(g, j, more):
                h = g * 4 + j
                act.wait_ge(at_trp, h + 1)
                A(probT[:, 0:512], bank(4), ACT.Copy).then_inc(at_pa, 1)
                if more or j + 1 < GRP:
                    exponentials(h + 1, j + 1)
                act.wait_ge(at_o, h + 1)
                A(oT[:, ds(h, 1), :], bank(7, T), ACT.Copy).then_inc(at_oc, 1)
                if more or j + 3 < GRP:
                    queries(h + 3, j + 3)

            queries(0, 0)
            queries(1, 1)
            exponentials(0, 0)
            queries(2, 2)
            with act.Fori(0, NKV - 1) as g:
                for j in range(GRP):
                    step(g, j, True)
            for j in range(GRP):
                step(NKV - 1, j, False)

            act.wait_ge(at_oc, NH)
            act.dma_start(res[:, 0, :], x_prompt).then_inc(xres_in, 16)
            act.dma_start(res[:, 1:3, :], x_sample.rearrange("(m p) d -> p m d", p=P)).then_inc(xres_in, 16)

            act.wait_ge(out_done, 32)
            act.nop().then_inc(gate_sig, 1)
            with act.Fori(0, 4) as i:
                act.wait_ge(cols_done, i + 20)
                rows(i * 4 + (4 * B_GA + 2), 7, rowbuf)
                act.wait_ge(blocks_used, i * 4 + (4 * B_GA + 4))
                for j in range(4):
                    A(sg[:, ds(i * 4 + j, 1), :], bank(j, T), ACT.Sigmoid).then_inc(gate_sig, 1)
            with act.Fori(0, 2) as i:
                for a in range(2):
                    act.wait_ge(blocks_used, i * 4 + (4 * B_GB + 2 * a + 2))
                    for j in range(4):
                        A(sg[:, ds(i * 8 + (16 + 4 * a + j), 1), :], bank(4 * a + j, T),
                          ACT.Sigmoid).then_inc(gate_sig, 1)

            act.wait_ge(ho_done, 16)
            act.nop().then_inc(wo_cp, 1)
            for q in range(4):
                act.wait_ge(blocks_used, 4 * B_WO + 2 * q + 2)
                for m in range(MT):
                    A(sq_scr[:, 0:NC_], bank(3 * (q % 2) + m), ACT.Square,
                      accum_out=ss[:, 4 * m + q:4 * m + q + 1]).then_inc(sumsq3, 1)
                    A(mix[:, m, q * NC_:(q + 1) * NC_], bank(3 * (q % 2) + m), ACT.Copy).then_inc(wo_cp, 1)
                    act.drain()
            act.wait_ge(rstd2, 1)
            for m in range(MT):
                act.wait_ge(res_ready, m + 1)
                A(sq_scr, res[:, m, :], ACT.Square, accum_out=ss[:, m:m + 1]).then_inc(sumsq3, 1)
                act.drain()
            for k in range(1, KT, 2):
                act.wait_ge(tr2, k + 1)
                for c, (lo, hi) in enumerate(SEG):
                    last = A(hT[:, k, lo:hi], bank(k % 4, hi - lo, lo), ACT.Identity,
                             bias=mod[:, SHIFT2 * KT + k, c:c + 1], scale=amp[:, 1, k, c:c + 1])
                last.then_inc(tr2_a, 1)
            act.wait_ge(lg_mm, 1)
            A(lgr, bank(4, T), ACT.Copy).then_inc(lg_cp, 1)
            act.wait_ge(lg_sub, 1)
            A(aff[:, :, :], aff[:, :, :], ACT.Exp).then_inc(lg_exp, 1)
            for k in range(KT):
                act.wait_ge(gat_c, k + 1)
                A(xeT[:, k, :, CAPL:SLOTS], bank(2 + k % 2, NE * CAPC).rearrange("p (e s) -> p e s", e=NE),
                  ACT.Identity, bias=mod[:, SHIFT2 * KT + k, 0:1], scale=amp[:, 1, k, 0:1]).then_inc(gat_ca, 1)
            def scatter_matrices(parts):
                for n in parts:
                    act.wait_ge(sg_tr, n + 1)
                    m, q = n // 4, n % 4
                    A(scat[:, 4 * q:4 * q + 4, m * P:(m + 1) * P],
                      bank(4 + n % 4).rearrange("p (j t) -> p j t", j=4), ACT.Copy).then_inc(sg_cp, 1)

            def expert(e, first=False):
                for n in range(2):
                    if first:
                        scatter_matrices(range(4 * n, 4 * n + 4))
                    act.wait_ge(blocks_used, e * 12 + (4 * (B_EX + n) + 4))
                    if n:
                        act.wait_ge(e_h, e * 2 + 1)
                    A(act_s[0:SLOTS, :], bank(n, p1=SLOTS), ACT.Silu).then_inc(e_silu, 1)
                if first:
                    scatter_matrices(range(8, 12))
                for i in range(2):
                    act.wait_ge(blocks_used, e * 12 + (4 * (B_EX + 2) + 2 * i + 2))
                    for u in range(2):
                        last = A(ye[64 * u:64 * u + SLOTS, i, :], bank(2 + i, p0=64 * u, p1=64 * u + SLOTS),
                                 ACT.Copy)
                    last.then_inc(e_yc, 1)

            expert(0, first=True)
            with act.Fori(1, NE) as e:
                expert(e)
            for n in range(4 * MT):
                act.wait_ge(e_acc, 4 + 12 * (NE - 1) + n + 1)
                m, q = n // 2 % MT, 2 * (n // (2 * MT)) + n % 2
                A(act_s, facc[:, m, q * NC_:(q + 1) * NC_], ACT.Square,
                  accum_out=ss[:, 4 * m + q:4 * m + q + 1]).then_inc(sumsq4, 1)
                act.drain()

        @blk.gpsimd
        def _(pool):
            g_ = nc.gpsimd
            g_.memset(condS[:, :, :], 0.0).then_inc(cond_ready, 1)
            g_.memset(neghalf, -0.5)
            pool.drain()

            def inv_root(src_sem, n, cols_, done):
                pool.wait_ge(src_sem, n)
                g_.tensor_tensor(rstd[:, 0:cols_], ss[:, 0:cols_], neghalf[:, 0:cols_],
                                 ALU.pow).then_inc(done, 1)

            inv_root(ms1, 1, MT, rstd1)
            with pool.Fori(0, 5) as i:
                pool.wait_ge(q_ms, i + 1)
                g_.tensor_tensor(rstd, ss, neghalf, ALU.pow).then_inc(q_rstd, 1)
            pool.wait_ge(qk_done, 5)
            pool.wait_ge(v_done, MT)
            pool.wait_ge(cache_in, 32)

            def queries(h, j, wait=True):
                if wait:
                    pool.wait_ge(at_trq, h - 1)
                g_.tensor_copy(q_st[:, j % 2, :, :], qkN[:, :, ds(h * HD, HD)]).then_inc(q_staged, 1)

            def values(g, wait=True):
                if wait:
                    pool.wait_ge(at_o, g * 4)
                g_.tensor_copy(v_st[:, :, :], vN[:, :, ds(g * HD, HD)]).then_inc(v_staged, 1)

            for h in range(GRP):
                queries(h, h, h >= 2)
            values(0, False)
            for j in range(GRP):
                queries(4 + j, j)
            with pool.Fori(1, NKV - 1) as g:
                values(g)
                for j in range(GRP):
                    queries(g * 4 + (4 + j), j)
            values(NKV - 1)
            pool.wait_ge(mod3_read, 1)
            g_.memset(wr[:, :, :], 0.0)
            g_.memset(ones, 1.0).then_inc(wr_zero, 1)
            pool.wait_ge(wr_zero, 1)
            pool.dma_start(wr[:, :, 0:NE], w_router.rearrange("(k p) e -> p k e", p=P)).then_inc(wr_in, 16)
            inv_root(ms2, 1, MT, rstd2)
            inv_root(ms3, 1, MT, rstd3s)
            pool.wait_ge(gat_lv, KT)
            pool.wait_ge(gat_ca, KT)

            def scatter_matrix(e, first=False):
                if not first:
                    pool.wait_ge(e_sc, e * 12)
                g_.tensor_copy(s_cur, scat[:, ds(e, 1), :].rearrange("p o t -> p (o t)")).then_inc(sc_st, 1)

            def next_inputs(e, first=False):
                if not first:
                    pool.wait_ge(blocks_used, e * 12 + (4 * (B_EX + 2)))
                g_.tensor_copy(x_cur[:, :, :], xeT[:, :, ds(e + 1, 1), :].rearrange("p k o s -> p k (o s)"))\
                    .then_inc(xe_st, 1)

            next_inputs(0, first=True)
            pool.wait_ge(sg_cp, 12)
            scatter_matrix(0, first=True)
            g_.memset(facc[:, :, :], 0.0).then_inc(facc_zero, 1)
            with pool.Fori(1, NE - 1) as e:
                scatter_matrix(e)
                next_inputs(e)
            pool.drain()
            g_.memset(ones2, 1.0).then_inc(wr_zero, 1)
            scatter_matrix(NE - 1)
            for m in range(MT):
                pool.wait_ge(ms4, m + 1)
                g_.tensor_tensor(rstd[:, m:m + 1], smx[:, m:m + 1], neghalf[:, m:m + 1],
                                 ALU.pow).then_inc(rstd4, 1)

        @blk.vector
        def _(dve):
            V = nc.vector
            ts_, tt, stt = V.tensor_scalar, V.tensor_tensor, V.scalar_tensor_tensor

            def mean_square(sem_in, n_in, cols_, width, done):
                dve.wait_ge(sem_in, n_in)
                ts_(ss[:, 0:cols_], ss[:, 0:cols_], 1.0 / width, EPS, ALU.mult, ALU.add).then_inc(done, 1)

            def sine_argument(src_bank, bias, n):
                dve.wait_ge(f_mm, n)
                a, r = arg[0:HF, :], rnd[0:HF, :]
                ts_(a, bank(src_bank, T, p1=HF), bias, fv[0:HF, 1:2], ALU.add, ALU.mult)
                dve.drain()
                ts_(r, a, 1.0 / TWO_PI, MAGIC, ALU.mult, ALU.add)
                dve.drain()
                ts_(r, r, MAGIC, None, ALU.subtract)
                for part in (PI_A, PI_B, PI_C):
                    dve.drain()
                    stt(out=a, in0=r, scalar=-part, in1=a, op0=ALU.mult, op1=ALU.add)
                dve.drain()
                ts_(a, a, PI_IN, -PI_IN, ALU.min, ALU.max).then_inc(f_arg, 1)

            dve.wait_ge(filt_in, 64)
            sine_argument(0, fv[0:HF, 0:1], 1)
            mean_square(sumsq1, MT, MT, D, ms1)
            dve.wait_ge(rstd1, 1)
            for m in range(MT):
                ts_(xn[:, m, :], xn[:, m, :], rstd[:, m:m + 1], None, ALU.mult).then_inc(xn1, 1)
            for k in range(KT):
                dve.wait_ge(tr1, k + 1)
                V.tensor_copy(hT[:, k, :], bank(1 + k % 3, T)).then_inc(tr1_copied, 1)
            sine_argument(4, fv[0:HF, 2:3], 2)
            def read_mods(lo, hi, n):
                dve.wait_ge(cols_done, n)
                tt(mod[:, lo:hi, :], PS[:, 6, 2 * lo:2 * hi].rearrange("p (a c) -> p a c", c=2),
                   col[:, C_BADA + lo:C_BADA + hi].unsqueeze(2).to_broadcast([P, hi - lo, 2]), ALU.add)
                dve.drain()

            def gains(dst, part, gain, add):
                stt(out=dst, in0=mod[:, part * KT:(part + 1) * KT, :], scalar=add,
                    in1=col[:, gain:gain + KT].unsqueeze(2).to_broadcast([P, KT, 2]), op0=ALU.add, op1=ALU.mult)

            def modulate_a(i):
                dve.wait_ge(cols_done, 2 * i + 2)
                for part in (SHIFT1, SCALE1):
                    lo = part * KT + 4 * i
                    last = tt(mod[:, lo:lo + 4, :], PS[:, 6, 2 * lo:2 * lo + 8].rearrange("p (a c) -> p a c", c=2),
                              col[:, C_BADA + lo:C_BADA + lo + 4].unsqueeze(2).to_broadcast([P, 4, 2]), ALU.add)
                last.then_inc(mod1_read, 1)
                dve.drain()
                stt(out=amp[:, 0, 4 * i:4 * i + 4, :], in0=mod[:, SCALE1 * KT + 4 * i:SCALE1 * KT + 4 * i + 4, :],
                    scalar=1.0, in1=col[:, C_GPRE1 + 4 * i:C_GPRE1 + 4 * i + 4].unsqueeze(2).to_broadcast([P, 4, 2]),
                    op0=ALU.add, op1=ALU.mult)
                dve.drain()
                for k in range(4 * i, 4 * i + 4):
                    for c, (lo, hi) in enumerate(SEG):
                        ts_(hT[:, k, lo:hi], hT[:, k, lo:hi], amp[:, 0, k, c:c + 1],
                            mod[:, SHIFT1 * KT + k, c:c + 1], ALU.mult, ALU.add)

            modulate_a(0)
            dve.wait_ge(taps_in, 48)
            for n in range(12):
                m, c = n // 4, n % 4
                dve.wait_ge(f_tapmm, n + 1)
                tt(hN[:, m, c * NC_:(c + 1) * NC_], bank(n % 4), dec[:, m, (c % 2) * NC_:(c % 2 + 1) * NC_],
                   ALU.mult).then_inc(f_taps, 1)
            dve.drain()
            V.memset(hN[0:1, 0, HYW:D], 0.0)
            V.memset(hN[0:1, 1, HYW:D], 0.0)
            dve.drain()
            tt(dec[:, :, :], hN[:, :, 0:HYW], hN[:, :, HYW:D], ALU.add)
            dve.drain()
            tt(hN[:, :, 0:HYW], hN[:, :, 0:HYW], hN[:, :, HYW:D], ALU.subtract).then_inc(f_sumdiff, 1)
            modulate_a(1)
            for n in range(1, 8, 2):
                dve.wait_ge(f_dft, n + 1)
                V.tensor_copy(spec[:, n // 4, (n // 2) % 2, NC_:2 * NC_], bank(n % 4)).then_inc(f_spec_v, 1)

            modulate_a(2)
            for n in range(9, 12, 2):
                dve.wait_ge(f_dft, n + 1)
                V.tensor_copy(spec[:, n // 4, (n // 2) % 2, NC_:2 * NC_], bank(n % 4)).then_inc(f_spec_v, 1)

            modulate_a(3)
            dve.drain()
            dve.wait_ge(f_spec_a, 6)
            V.memset(SM[:, 121:122], 0.0).then_inc(conv_free, 4)

            def outer_taps(i):
                for j in range(4):
                    dve.wait_ge(conv_mid, i * 4 + (j + 1))
                    for tap in range(2):
                        w = col[:, ds(i * 4 + (C_CW + 48 * tap + j), 1)]
                        for lo, hi in SEG:
                            a, b = (lo + 1, hi) if tap == 0 else (lo, hi - 1)
                            o = -1 if tap == 0 else 1
                            last = stt(out=hyT[:, ds(i * 4 + j, 1), a:b].rearrange("p o t -> p (o t)"),
                                       in0=bank(j, b - a, a + o), scalar=w,
                                       in1=hyT[:, ds(i * 4 + j, 1), a:b].rearrange("p o t -> p (o t)"),
                                       op0=ALU.mult, op1=ALU.add)
                        if tap == 0:
                            dve.drain()
                    last.then_inc(conv_free, 1)

            def gated_input(half):
                a, b = HYT + 4 * half, 2 * HYT + 4 * half
                dve.drain()
                tt(hyT[:, b:b + 4, :], hyT[:, b:b + 4, :], hyT[:, a:a + 4, :], ALU.mult).then_inc(u_ready, 1)

            with dve.Fori(0, 5) as i:
                outer_taps(i)
            gated_input(0)
            outer_taps(5)
            gated_input(1)
            for half in range(2):
                hs = slice(half * NC_, (half + 1) * NC_)
                for j in range(3):
                    dve.wait_ge(u_dft, 3 * half + j + 1)
                    if half and j == 0:
                        dve.wait_ge(z_inv, 4)
                    hc, hsn = spec[:, j, 0, hs], spec[:, j, 1, hs]
                    uc, us = bank(Z_BANK[half][j]), bank(Z_BANK[half][j] + 1)
                    dve.drain()
                    tt(Z[:, j, 0, :], uc, hc, ALU.mult)
                    tt(tmp, us, hsn, ALU.mult)
                    tt(Z[:, j, 1, :], uc, hsn, ALU.mult)
                    dve.drain()
                    tt(Z[:, j, 0, :], Z[:, j, 0, :], tmp, ALU.subtract)
                    dve.drain()
                    tt(tmp, us, hc, ALU.mult)
                    dve.drain()
                    tt(Z[:, j, 1, :], Z[:, j, 1, :], tmp, ALU.add).then_inc(z_ready, 1)
                for c in range(4):
                    n = 4 * half + c
                    dve.wait_ge(z_inv, n + 1)
                    dve.drain()
                    stt(out=tmp[:, 0:T], in0=hyT[:, 2 * HYT + n, :], scalar=col[:, C_SKIP + n:C_SKIP + n + 1],
                        in1=bank(7 if n % 2 == 0 else 5, T), op0=ALU.mult, op1=ALU.add)
                    dve.drain()
                    tt(yhT[:, n, :], tmp[:, 0:T], hyT[:, n, :], ALU.mult).then_inc(yh_done, 1)

            dve.wait_ge(qk_in, 32)
            for a in range(2):
                for m in range(2):
                    tt(rot[:, a, m, :, :], rope_t[:, m, :, :],
                       gain_b[:, a, :].unsqueeze(1).to_broadcast([P, 2, HD]), ALU.mult)
            dve.drain()

            def qk_norm(i, x, a):
                for m in range(MT):
                    dve.drain()
                    dve.wait_ge(qkv_raw, i * 3 + (m + 4))
                    tt(t_a, x(m), x(m), ALU.mult)
                    dve.drain()
                    V.tensor_reduce(ss[:, 4 * m:4 * m + 4], t_a.rearrange("p (h d) -> p h d", h=4), AX_X, ALU.add)
                dve.drain()
                ts_(ss, ss, 1.0 / HD, EPS, ALU.mult, ALU.add).then_inc(q_ms, 1)
                dve.wait_ge(q_rstd, i + 1)
                for m in range(MT):
                    xh = x(m).rearrange("p (h d) -> p h d", h=4)
                    tah, tbh = (t.rearrange("p (h d) -> p h d", h=4) for t in (t_a, t_b))
                    if m:
                        dve.drain()
                    tt(xh, xh, rstd[:, 4 * m:4 * m + 4].unsqueeze(2).to_broadcast([P, 4, HD]), ALU.mult)
                    dve.drain()
                    if m == 0:
                        tt(xh, xh, gain_b[:, a, :].unsqueeze(1).to_broadcast([P, 4, HD]), ALU.mult)
                        continue
                    own = rot[:, a, m - 1, 0, :].unsqueeze(1).to_broadcast([P, 4, HD])
                    other = rot[:, a, m - 1, 1, :].unsqueeze(1).to_broadcast([P, 4, HD])
                    tt(tah, xh, own, ALU.mult)
                    tt(tbh, xh, other, ALU.mult)
                    dve.drain()
                    x4 = x(m).rearrange("p (g s d) -> p g s d", s=2, d=32)
                    a4, b4 = (t.rearrange("p (g s d) -> p g s d", s=2, d=32) for t in (t_a, t_b))
                    for s in range(2):
                        tt(x4[:, :, s, :], a4[:, :, s, :], b4[:, :, 1 - s, :], ALU.add)
                dve.drain()
                V.memset(SM[:, 121:122], 0.0).then_inc(qk_done, 1)
                dve.drain()

            with dve.Fori(0, 4) as i:
                qk_norm(i, lambda m: qkN[:, m, ds(i * NC_, NC_)], 0)
            qk_norm(4, lambda m: qkN[:, m, D:D + KVW], 1)
            read_mods(32, 80, 20)
            gains(amp[:, 1], SCALE2, C_GPRE2, 1.0)
            gains(gout[:, 0], GATE1, C_GPOST1, 0.0)
            dve.drain()
            V.memset(SM[:, 121:122], 0.0).then_inc(mod2_read, 1)

            for g in range(1, NKV, 2):
                dve.wait_ge(at_trk, g + 1)
                V.tensor_copy(kT[:, g, :], bank(g)).then_inc(at_kT, 1)

            def maxima(h, j):
                p = j % 2
                dve.wait_ge(at_s, h + 1)
                V.reduce_max(mx[:, p, 0:1], bank(2 * p, 384), AX_X)
                V.reduce_max(mx[:, p, 1:2], bank(2 * p + 1, 384), AX_X)
                V.reduce_max(mx[:, p, 2:3], bank(2 * p, TC, 384), AX_X)
                dve.drain()
                ts_(nb[:, p, :], mx[:, p, :], -SCALE, None, ALU.mult).then_inc(at_max, 1)

            def normalise(h, j):
                p = j % 2
                dve.wait_ge(at_exp, h + 1)
                V.reciprocal(ri[:, p, :], rs[:, p, :])
                dve.drain()
                for t, (lo, hi) in enumerate(((0, 384), (384, 768), (768, 896))):
                    last = ts_(prob[:, p, lo:hi], prob[:, p, lo:hi], ri[:, p, t:t + 1], None, ALU.mult)
                last.then_inc(at_norm, 1)

            def step(g, j, more):
                h = g * 4 + j
                dve.wait_ge(at_trp, h + 1)
                V.tensor_copy(probT[:, 512:896], bank(5, 384)).then_inc(at_pb, 1)
                if more or j + 2 < GRP:
                    maxima(h + 2, j)
                if more or j + 1 < GRP:
                    normalise(h + 1, j + 1)

            maxima(0, 0)
            maxima(1, 1)
            normalise(0, 0)
            with dve.Fori(0, NKV - 1) as g:
                for j in range(GRP):
                    step(g, j, True)
            for j in range(GRP):
                step(NKV - 1, j, False)

            read_mods(80, 96, 24)
            gains(gout[:, 1], GATE2, C_GPOST2, 0.0)
            dve.drain()
            V.memset(SM[:, 121:122], 0.0).then_inc(mod3_read, 1)
            dve.wait_ge(gate_sig, 33)
            V.memset(SM[:, 122:123], 0.0).then_inc(ao_done, 1)
            with dve.Fori(0, 2) as i:
                for a in range(2):
                    dve.wait_ge(blocks_used, i * 4 + (4 * B_AO + 2 * a + 2))
                    for j in range(4):
                        d = sg[:, ds(i * 8 + (4 * a + j), 1), :].rearrange("p o t -> p (o t)")
                        tt(d, bank(4 * a + j, T), d, ALU.mult).then_inc(ao_done, 1)
            for c in range(4):
                dve.wait_ge(blocks_used, 4 * B_HO + c + 1)
                for j in range(4):
                    n, b = 4 * c + j, 4 * (c % 2) + j
                    dve.drain()
                    tt(sg[:, KT + n, :], bank(b, T), sg[:, KT + n, :], ALU.mult)
                    dve.drain()
                    tt(sg[:, n, :], sg[:, n, :], sg[:, KT + n, :], ALU.add).then_inc(ho_done, 1)

            def diagonals(which, n, ready):
                q, c = n // 2, n % 2
                for j in range(4):
                    last = ts_(diag[:, n % 2, j * P:(j + 1) * P], ident,
                               gout[:, which, 4 * q + j, c:c + 1], None, ALU.mult)
                last.then_inc(ready, 1)

            def gate_rows(which, dst, b0, ready, bc, used, n0=0, n1=8):
                if n0 == 0:
                    diagonals(which, 0, ready)
                    diagonals(which, 1, ready)
                for n in range(n0, n1):
                    dve.wait_ge(bc, n + 1)
                    V.tensor_copy(dst[:, n % 2, (n // 2) * NC_:(n // 2 + 1) * NC_],
                                  bank(b0 + n % 2)).then_inc(used, 1)
                    if n + 2 < 8:
                        diagonals(which, n + 2, ready)
                dve.drain()

            dve.wait_ge(wr_zero, 1)
            gate_rows(0, g_rows, 6, diag_ready, g_bc, g_used)
            for q in range(4):
                qs = slice(q * NC_, (q + 1) * NC_)
                for m in range(MT):
                    dve.wait_ge(wo_cp, 1 + 3 * q + m + 1)
                    tt(mix[:, m, qs], mix[:, m, qs], g_rows[:, min(m, 1), qs], ALU.mult)
            dve.wait_ge(sumsq3, 4 * MT)
            V.tensor_reduce(smx, ss.rearrange("p (m q) -> p m q", q=4), AX_X, ALU.add)
            dve.drain()
            ts_(ss[:, 0:MT], smx, 1.0 / D, EPS, ALU.mult, ALU.add).then_inc(ms2, 1)
            dve.wait_ge(rstd2, 1)
            dve.wait_ge(xres_in, 32)
            for m in range(MT):
                stt(out=res[:, m, :], in0=mix[:, m, :], scalar=rstd[:, m:m + 1], in1=res[:, m, :],
                    op0=ALU.mult, op1=ALU.add).then_inc(res_ready, 1)
            dve.drain()

            mean_square(sumsq3, 5 * MT, MT, D, ms3)
            dve.wait_ge(rstd3s, 1)
            for m in range(MT):
                ts_(xn[:, m, :], res[:, m, :], rstd[:, m:m + 1], None, ALU.mult).then_inc(xn2, 1)
            for k in range(0, KT, 2):
                dve.wait_ge(tr2, k + 1)
                for c, (lo, hi) in enumerate(SEG):
                    last = ts_(hT[:, k, lo:hi], bank(k % 4, hi - lo, lo), amp[:, 1, k, c:c + 1],
                               mod[:, SHIFT2 * KT + k, c:c + 1], ALU.mult, ALU.add)
                last.then_inc(tr2_v, 1)
            dve.wait_ge(lg_nat, 1)
            lg = PS[:, 5, 0:MT * NE].rearrange("p (m e) -> p m e", e=NE)

            def over_experts(v):
                return v.unsqueeze(2).to_broadcast([P, MT, NE])

            V.tensor_reduce(smx, lg, AX_X, ALU.max)
            dve.drain()
            tt(aff[:, :, :], lg, over_experts(smx), ALU.subtract).then_inc(lg_sub, 1)
            dve.wait_ge(lg_exp, 1)
            dve.drain()
            V.tensor_reduce(smx, aff[:, :, :], AX_X, ALU.add)
            dve.drain()
            V.reciprocal(smx, smx)
            dve.drain()
            tt(aff[:, :, :], aff[:, :, :], over_experts(smx), ALU.mult).then_inc(aff_ready, 1)
            dve.wait_ge(aff_tr, 1)
            V.tensor_copy(wk[0:NE, :], bank(4, T, p1=NE))
            for (lo, hi), cap in zip(SEG, (CAPC, CAPL)):
                for _ in range(cap // 8):
                    dve.drain()
                    V.max(m8[0:NE, :], wk[0:NE, lo:hi])
                    dve.drain()
                    V.match_replace(wk[0:NE, lo:hi], m8[0:NE, :], wk[0:NE, lo:hi], -1.0)
            dve.drain()
            ts_(wk[0:NE, :], wk[0:NE, :], 0.0, None, ALU.is_lt)
            dve.drain()
            for lo, hi in SEG:
                V.tensor_tensor_scan(cum[0:NE, lo:hi], wk[0:NE, lo:hi], wk[0:NE, lo:hi], 0.0, ALU.add, ALU.max)
            dve.drain()
            tt(cum[0:NE, :], cum[0:NE, :], wk[0:NE, :], ALU.mult).then_inc(v_ready, 1)
            dve.wait_ge(v_tr, 1)
            V.tensor_copy(vsel[:, :, :], PS[:, 5, 0:MT * NE].rearrange("p (m e) -> p m e", e=NE))
            dve.drain()
            tt(selC[:, :, :], vsel[:, 0, :].unsqueeze(2).to_broadcast([P, NE, CAPC]),
               slot_no[:, 0:CAPC].unsqueeze(1).to_broadcast([P, NE, CAPC]), ALU.is_equal)
            for t in range(2):
                last = tt(selL[:, t, :, :], vsel[:, 1 + t, :].unsqueeze(2).to_broadcast([P, NE, CAPL]),
                          slot_no.unsqueeze(1).to_broadcast([P, NE, CAPL]), ALU.is_equal)
            dve.drain()
            V.memset(SM[:, 121:122], 0.0).then_inc(sel_ready, 1)

            def gated(m):
                s, o, n = (selC[:, :, :], CAPL, CAPC) if m == 0 else (selL[:, m - 1, :, :], 0, CAPL)
                for u in range(2):
                    last = tt(selG[:, m, :, 64 * u + o:64 * u + o + n], s,
                              aff[:, m, :].unsqueeze(2).to_broadcast([P, NE, n]), ALU.mult)
                last.then_inc(sg_ready, 1)

            for k in range(KT):
                dve.wait_ge(gat_l, k + 1)
                ts_(xeT[:, k, :, 0:CAPL], bank(k % 2).rearrange("p (e s) -> p e s", e=NE), amp[:, 1, k, 1:2],
                    mod[:, SHIFT2 * KT + k, 1:2], ALU.mult, ALU.add).then_inc(gat_lv, 1)
            V.memset(selG[:, :, :, :], 0.0)
            dve.drain()
            for m in range(MT):
                gated(m)

            def accumulate(turn, i, m, t):
                for u in range(2):
                    n = 2 * t + u
                    q = slice((2 * i + u) * NC_, (2 * i + u + 1) * NC_)
                    dve.wait_ge(e_sc, turn * 12 + (n - 11))
                    tt(facc[:, m, q], facc[:, m, q], bank(4 + n % 4), ALU.add).then_inc(e_acc, 1)

            def products(e, n):
                dve.wait_ge(e_silu, e * 2 + (n + 1))
                tt(h_s[0:SLOTS, n, :], act_s[0:SLOTS, :], bank(n, p0=64, p1=64 + SLOTS), ALU.mult).then_inc(e_h, 1)

            def products_to_columns(e, n):
                dve.wait_ge(e_htr, e * 2 + (n + 1))
                V.tensor_copy(hTe[:, 4 * n:4 * n + 4, :],
                              bank(2 + n, 4 * SLOTS).rearrange("p (k s) -> p k s", k=4)).then_inc(e_hT, 1)

            def gates(n):
                gate_rows(1, g2_rows, 2, diag2_ready, g2_bc, g2_used, n, n + 2)

            def expert(e, final=False):
                accumulate(e, 0, 0, 0)
                if final:
                    dve.wait_ge(wr_zero, 2)
                    gates(0)
                accumulate(e, 0, 1, 1)
                if final:
                    gates(2)
                products(e, 0)
                accumulate(e, 0, 2, 2)
                if final:
                    gates(4)
                accumulate(e, 1, 0, 3)
                if final:
                    gates(6)
                products(e, 1)
                products_to_columns(e, 0)
                products_to_columns(e, 1)
                accumulate(e, 1, 1, 4)
                accumulate(e, 1, 2, 5)

            products(0, 0)
            products(0, 1)
            products_to_columns(0, 0)
            products_to_columns(0, 1)
            dve.wait_ge(sg_cp, 12)
            V.memset(SM[:, 121:122], 0.0).then_inc(e_acc, 4)
            dve.wait_ge(facc_zero, 1)
            with dve.Fori(1, NE - 1) as e:
                expert(e)
            expert(NE - 1, final=True)

            def finish(m):
                dve.wait_ge(rstd4, m + 1)
                stt(out=res[:, m, :], in0=f_g[:, m, :], scalar=rstd[:, m:m + 1], in1=res[:, m, :],
                    op0=ALU.mult, op1=ALU.add).then_inc(y_ready, 1)

            def last_sum(i, m):
                accumulate(NE, i, m, MT * i + m)
                dve.drain()
                for q in (2 * i, 2 * i + 1):
                    qs = slice(q * NC_, (q + 1) * NC_)
                    tt(f_g[:, m, qs], facc[:, m, qs], g2_rows[:, min(m, 1), qs], ALU.mult)

            for m in range(MT):
                last_sum(0, m)
            for m in range(MT):
                last_sum(1, m)
                if m:
                    finish(m - 1)
                dve.wait_ge(sumsq4, 2 * MT + 2 * m + 2)
                V.tensor_reduce(smx[:, m:m + 1], ss[:, 4 * m:4 * m + 4], AX_X, ALU.add)
                dve.drain()
                ts_(smx[:, m:m + 1], smx[:, m:m + 1], 1.0 / D, EPS, ALU.mult, ALU.add).then_inc(ms4, 1)
            finish(MT - 1)


def tables():
    f32 = np.float32
    p = np.arange(P)
    tabs = np.zeros((P, N_TABS), f32)
    tabs[:, T_ID:T_ID + P] = np.eye(P)
    tabs[:, T_SEL2:T_SEL2 + 2] = (p[:, None] % 32) == np.arange(2)
    tabs[:, T_SEL16:T_SEL16 + 16] = (p[:, None] % 32) == np.arange(16)
    tabs[:, T_SLOT:T_SLOT + 32] = np.arange(1, 33)

    def dft(L):
        ang = np.pi * (2 * np.arange(L)[None, :] + 1) * np.arange(L)[:, None] / (2 * L)
        return np.cos(ang), np.sin(ang)

    parts = []
    for inverse in (False, True):
        for L in (TL, TC):
            for t in range(L // P):
                for m in dft(L):
                    m = m.T / L if inverse else m
                    parts.append(m[t * P:(t + 1) * P])
    dft_all = np.concatenate(parts, axis=1).astype(f32)

    def positions(L):
        t = np.linspace(0.0, 1.0, L, dtype=f32)
        bands = (HE - 1) // 2
        w = (f32(TWO_PI) * np.arange(L, dtype=f32) / f32(L)).astype(f32)
        f = np.linspace(1e-4, bands - 1, bands, dtype=f32)
        ang = (w[:, None] * f[None, :]).astype(f32)
        z = np.concatenate([t[:, None], np.cos(ang), -np.sin(ang)], axis=-1).astype(f32)
        lo, hi = math.log(1e-2) / 1.5, math.log(1e-2) / 0.3
        deltas = np.abs(np.linspace(lo, hi, HYW, dtype=f32))
        return z, np.exp(-t[:, None] * deltas[None, :]).astype(f32)

    zc, dc = positions(TC)
    zl, dl = positions(TL)
    zfeat = np.ascontiguousarray(np.concatenate([zc, zl]).T)
    decay = np.concatenate([dc, dl]).reshape(MT, P, HYW)

    half = HD // 2
    inv_freq = f32(10000.0) ** (-np.arange(0, half, 2, dtype=f32) / f32(half))
    n = np.arange(TL, dtype=f32)
    ang = np.concatenate([(np.floor(n / 64))[:, None] * inv_freq[None], (n % 64)[:, None] * inv_freq[None]], 1)
    ang = ang.astype(f32).reshape(TL, 2, 1, half // 2)
    cos = np.broadcast_to(np.cos(ang), (TL, 2, 2, half // 2))
    sin = np.concatenate([np.sin(ang), -np.sin(ang)], axis=2)
    rope = np.stack([cos.reshape(TL, HD), sin.reshape(TL, HD)], 1).reshape(2, P, 2, HD)
    rope = np.ascontiguousarray(rope.transpose(1, 0, 2, 3)).astype(f32)
    return tabs, dft_all, zfeat, decay, rope


def kernel(**inputs):
    import concourse.bacc as bacc
    from concourse.bass_utils import run_bass_kernel_spmd

    a = {k: np.asarray(v) for k, v in inputs.items()}

    def columns(v):
        return np.asarray(v).reshape(-1, P).T

    cols = np.ascontiguousarray(np.concatenate([
        columns(a["c_ctx"]), columns(a["c"]), columns(a["b_ada"]), columns(a["g_pre_mix"]),
        columns(a["g_post_mix"]), columns(a["g_pre_ffn"]), columns(a["g_post_ffn"]),
        columns(a["hy_conv_w"]), columns(a["hy_conv_b"]), columns(a["hy_skip"])], axis=1))
    f_vec = np.ascontiguousarray(np.concatenate([a["hy_f1_b"], a["hy_sin_freq"], a["hy_f2_b"]]).T)
    tabs, dft, zfeat, decay, rope = tables()
    ins = [
        ("x_prompt", a["x_prompt"][0]), ("x_sample", a["x_sample"][0]),
        ("cache_k", a["cache_k_ctx"].reshape(PAST, KVW)), ("cache_v", a["cache_v_ctx"].reshape(PAST, KVW)),
        ("cols", cols), ("w_ada", a["w_ada"][0]), ("w_in", a["w_in"][0]),
        ("qk_g", np.concatenate([a["q_norm_g"], a["k_norm_g"]])), ("w_attn_o", a["w_attn_o"][0]),
        ("f1_w", a["hy_f1_w"][0]), ("f_vec", f_vec), ("f2_w", a["hy_f2_w"][0]), ("f3_w", a["hy_f3_w"][0]),
        ("w_hy_o", a["w_hy_o"][0]), ("w_out", a["w_out"][0]), ("w_router", a["w_router"][0]),
        ("w_gate", a["w_exp_gate"].reshape(NE * D, FF)), ("w_up", a["w_exp_up"].reshape(NE * D, FF)),
        ("w_down", a["w_exp_down"].reshape(NE * FF, D)),
        ("tabs", tabs), ("dft", dft), ("zfeat", zfeat), ("decay", decay), ("rope", rope),
    ]
    outs = [("y_prompt", (TC, D)), ("y_sample", (TL, D)), ("state_k", (TC, KVW)), ("state_v", (TC, KVW))]
    nc = bacc.Bacc("TRN2", target_bir_lowering=False, num_devices=1)
    arrays, args = {}, []
    for name, v in ins:
        arrays[f"in_{name}"] = np.ascontiguousarray(v)
        args.append(nc.dram_tensor(f"in_{name}", v.shape, F32, kind="ExternalInput").ap())
    for name, shape in outs:
        args.append(nc.dram_tensor(f"out_{name}", shape, F32, kind="ExternalOutput").ap())
    build(nc, *args)
    r = run_bass_kernel_spmd(nc, [arrays], core_ids=[0]).results[0]
    return (r["out_y_prompt"].reshape(1, TC, D), r["out_y_sample"].reshape(1, TL, D),
            r["out_state_k"].reshape(1, 1, TC, NKV, HD), r["out_state_v"].reshape(1, 1, TC, NKV, HD))
```
